# Optimizing a Trainium2 kernel written in Bass

```python
import math
import jax, jax.numpy as jnp
from jax import lax
import numpy as np

D_MODEL = 1024
BATCH = 1
SEQ = 256
DEPTH = 2

GRID_W = 64
CTX_LEN = 256

F_GROUPS = 4
F_GROUP_DIM = D_MODEL // 8
F_WIDTH = F_GROUPS * F_GROUP_DIM
HEAD_DIM = 64
N_HEADS = (D_MODEL // 2) // HEAD_DIM
N_KV_HEADS = N_HEADS // 4
GQ = N_HEADS // N_KV_HEADS
Q_WIDTH = N_HEADS * HEAD_DIM
KV_WIDTH = N_KV_HEADS * HEAD_DIM
KV_START = F_WIDTH + Q_WIDTH
MIX_IN = F_WIDTH + Q_WIDTH + 2 * KV_WIDTH
MIX_OUT = F_WIDTH + Q_WIDTH
Q_BLOCK = 128
ROPE_THETA = 10000.0
AXIS_ROT_DIM = HEAD_DIM // 2
ATTN_SCALE = HEAD_DIM ** -0.5

D_INNER = 2 * D_MODEL
SSM_HEAD_DIM = 64
N_SSM_HEADS = D_INNER // SSM_HEAD_DIM
N_GROUPS = 4
HEADS_PER_GROUP = N_SSM_HEADS // N_GROUPS
D_STATE = 128
D_CONV = 5
CONV_PAD = D_CONV // 2
CONV_DIM = D_INNER + 2 * N_GROUPS * D_STATE
SSM_IN = D_INNER + CONV_DIM + 2 * N_SSM_HEADS
CHUNK = 128
DT_MIN = 0.001
DT_MAX = 0.1
A_MIN = 1.0
A_MAX = 16.0

D_FF = 2816
N_EXPERTS = 8
TOP_K = 2
D_FF_EXPERT = 3584

N_EVEN = (DEPTH + 1) // 2
N_ODD = DEPTH // 2
EPS = 1e-6

kernel_name = "hybrid_fourier_gqa_ssd_moe_dit"

def _rms_norm(x, w):
    xf = x.astype(jnp.float32)
    y = xf * lax.rsqrt(jnp.mean(xf * xf, axis=-1, keepdims=True) + EPS)
    return (y * w.astype(jnp.float32)).astype(x.dtype)

def _modulate(h, shift, scale):
    return h * (1.0 + scale) + shift

def _axial_rope_tables(rows):
    row = jnp.repeat(jnp.arange(rows, dtype=jnp.float32), GRID_W)
    col = jnp.tile(jnp.arange(GRID_W, dtype=jnp.float32), rows)
    freqs = ROPE_THETA ** (-jnp.arange(0, AXIS_ROT_DIM, 2, dtype=jnp.float32) / AXIS_ROT_DIM)
    ang = jnp.concatenate([row[:, None] * freqs, col[:, None] * freqs], axis=-1)
    return jnp.cos(ang), jnp.sin(ang)

def _rope(x, cos, sin):
    xf = x.astype(jnp.float32).reshape(*x.shape[:-1], HEAD_DIM // 2, 2)
    x1, x2 = xf[..., 0], xf[..., 1]
    c = cos[None, :, None, :]
    s = sin[None, :, None, :]
    out = jnp.stack([x1 * c - x2 * s, x1 * s + x2 * c], axis=-1).reshape(x.shape)
    return out.astype(x.dtype)

def _attend(q, k, v):
    s = jnp.einsum('bqkgd,bskd->bkgqs', q, k).astype(jnp.float32) * ATTN_SCALE
    p = jax.nn.softmax(s, axis=-1).astype(v.dtype)
    return jnp.einsum('bkgqs,bskd->bqkgd', p, v)

def _blocked_attention(q, k, v):
    b, s = q.shape[:2]
    qb = q.reshape(b, s // Q_BLOCK, Q_BLOCK, N_KV_HEADS, GQ, HEAD_DIM).swapaxes(0, 1)
    o = lax.map(lambda blk: _attend(blk, k, v), qb)
    return o.swapaxes(0, 1).reshape(b, s, Q_WIDTH)

def _fourier_mix(u):
    b, l, _ = u.shape
    ug = u.astype(jnp.float32).reshape(b, l, F_GROUPS, F_GROUP_DIM)
    f = jnp.fft.fft2(ug, axes=(1, 3), norm='ortho').real
    return f.reshape(b, l, F_WIDTH).astype(u.dtype)

def _fourier_attention_mixer(hx, hc, w_in, q_norm_w, k_norm_w, w_out, cos, sin, need_ctx):
    b, s, _ = hx.shape
    lc = hc.shape[1]
    px = hx @ w_in
    u_x = px[..., :F_WIDTH]
    q_x = px[..., F_WIDTH:KV_START].reshape(b, s, N_HEADS, HEAD_DIM)
    k_x = px[..., KV_START:KV_START + KV_WIDTH].reshape(b, s, N_KV_HEADS, HEAD_DIM)
    v_x = px[..., KV_START + KV_WIDTH:].reshape(b, s, N_KV_HEADS, HEAD_DIM)
    q_x = _rope(_rms_norm(q_x, q_norm_w), cos, sin)
    k_x = _rope(_rms_norm(k_x, k_norm_w), cos, sin)
    pc = hc @ w_in[:, KV_START:]
    k_c = _rms_norm(pc[..., :KV_WIDTH].reshape(b, lc, N_KV_HEADS, HEAD_DIM), k_norm_w)
    v_c = pc[..., KV_WIDTH:].reshape(b, lc, N_KV_HEADS, HEAD_DIM)
    k_all = jnp.concatenate([k_c, k_x], axis=1)
    v_all = jnp.concatenate([v_c, v_x], axis=1)
    a_x = _blocked_attention(q_x.reshape(b, s, N_KV_HEADS, GQ, HEAD_DIM), k_all, v_all)
    y_x = jnp.concatenate([_fourier_mix(u_x), a_x], axis=-1) @ w_out
    if not need_ctx:
        return y_x, None
    pcq = hc @ w_in[:, :KV_START]
    u_c = pcq[..., :F_WIDTH]
    q_c = _rms_norm(pcq[..., F_WIDTH:].reshape(b, lc, N_HEADS, HEAD_DIM), q_norm_w)
    a_c = _attend(q_c.reshape(b, lc, N_KV_HEADS, GQ, HEAD_DIM), k_c, v_c).reshape(b, lc, Q_WIDTH)
    y_c = jnp.concatenate([_fourier_mix(u_c), a_c], axis=-1) @ w_out
    return y_x, y_c

def _dwconv(u, w, bias):
    ch = u.shape[-1]
    out = lax.conv_general_dilated(u, w[:, None, :], window_strides=(1,),
                                   padding=[(CONV_PAD, CONV_PAD)],
                                   dimension_numbers=('NWC', 'WIO', 'NWC'),
                                   feature_group_count=ch)
    return out + bias

def _ssd_scan(x, dt, A, B, C, h0, return_y):
    b, l, g, hg, p = x.shape
    n = B.shape[-1]
    nc = l // CHUNK
    f32 = jnp.float32
    x = x.astype(f32).reshape(b, nc, CHUNK, g, hg, p)
    dt = dt.reshape(b, nc, CHUNK, g, hg)
    B = B.astype(f32).reshape(b, nc, CHUNK, g, n)
    C = C.astype(f32).reshape(b, nc, CHUNK, g, n)
    a_cum = jnp.cumsum(dt * A, axis=2)
    xdt = x * dt[..., None]
    decay_end = jnp.exp(a_cum[:, :, -1:] - a_cum)
    states = jnp.einsum('bcqgn,bcqgh,bcqghp->bcghpn', B, decay_end, xdt)
    chunk_decay = jnp.exp(a_cum[:, :, -1])

    def step(h, inp):
        dec, st = inp
        return dec[..., None, None] * h + st, h

    final, prev = lax.scan(step, h0, (jnp.moveaxis(chunk_decay, 1, 0), jnp.moveaxis(states, 1, 0)))
    if not return_y:
        return None, final
    prev = jnp.moveaxis(prev, 0, 1)
    idx = jnp.arange(CHUNK)
    mask = (idx[:, None] >= idx[None, :])[:, :, None, None]
    seg = a_cum[:, :, :, None] - a_cum[:, :, None]
    decay = jnp.exp(jnp.where(mask, seg, -jnp.inf))
    cb = jnp.einsum('bcign,bcjgn->bcijg', C, B)
    y_diag = jnp.einsum('bcijg,bcijgh,bcjghp->bcighp', cb, decay, xdt)
    y_off = jnp.einsum('bcign,bcghpn,bcigh->bcighp', C, prev, jnp.exp(a_cum))
    return (y_diag + y_off).reshape(b, l, g, hg, p), final

def _ssd_branch(h, w_in, conv_w, conv_b, dt_bias, A, d_skip, norm_w, w_out, h0_f, h0_b, with_out):
    b, l, _ = h.shape
    if with_out:
        proj = h @ w_in
        z = proj[..., :D_INNER]
        rest = proj[..., D_INNER:]
    else:
        rest = h @ w_in[:, D_INNER:]
    xbc = jax.nn.silu(_dwconv(rest[..., :CONV_DIM], conv_w, conv_b))
    xs = xbc[..., :D_INNER].reshape(b, l, N_GROUPS, HEADS_PER_GROUP, SSM_HEAD_DIM)
    bm = xbc[..., D_INNER:D_INNER + N_GROUPS * D_STATE].reshape(b, l, N_GROUPS, D_STATE)
    cm = xbc[..., D_INNER + N_GROUPS * D_STATE:].reshape(b, l, N_GROUPS, D_STATE)
    dt = jax.nn.softplus(rest[..., CONV_DIM:].astype(jnp.float32).reshape(b, l, 2, N_GROUPS, HEADS_PER_GROUP)
                         + dt_bias.astype(jnp.float32).reshape(2, N_GROUPS, HEADS_PER_GROUP))
    flip = lambda a: jnp.flip(a, axis=1)
    y_f, s_f = _ssd_scan(xs, dt[:, :, 0], A[0], bm, cm, h0_f, with_out)
    y_b, s_b = _ssd_scan(flip(xs), flip(dt[:, :, 1]), A[1], flip(bm), flip(cm), h0_b, with_out)
    if not with_out:
        return None, s_f, s_b
    y = y_f + flip(y_b) + d_skip.astype(jnp.float32).reshape(N_GROUPS, HEADS_PER_GROUP, 1) * xs.astype(jnp.float32)
    gy = (y.reshape(b, l, D_INNER) * jax.nn.silu(z.astype(jnp.float32))).reshape(b, l, N_GROUPS, D_INNER // N_GROUPS)
    gy = _rms_norm(gy, norm_w.reshape(N_GROUPS, D_INNER // N_GROUPS)).reshape(b, l, D_INNER).astype(h.dtype)
    return gy @ w_out, s_f, s_b

def _ssd_mixer(hx, hc, w_in, conv_w, conv_b, dt_bias, a_log, d_skip, norm_w, w_out, need_ctx):
    A = -jnp.exp(a_log.astype(jnp.float32)).reshape(2, N_GROUPS, HEADS_PER_GROUP)
    zeros = jnp.zeros((hc.shape[0], N_GROUPS, HEADS_PER_GROUP, SSM_HEAD_DIM, D_STATE), jnp.float32)
    y_c, s_f, s_b = _ssd_branch(hc, w_in, conv_w, conv_b, dt_bias, A, d_skip, norm_w, w_out,
                                zeros, zeros, need_ctx)
    y_x, _, _ = _ssd_branch(hx, w_in, conv_w, conv_b, dt_bias, A, d_skip, norm_w, w_out,
                            s_f, s_b, True)
    return y_x, y_c

def _swiglu(h, w_gu, w_down):
    gu = h @ w_gu
    f = w_gu.shape[-1] // 2
    return (jax.nn.silu(gu[..., :f]) * gu[..., f:]) @ w_down

def _moe(h, router_w, w_gu, w_down):
    shape = h.shape
    t = h.reshape(-1, shape[-1])
    logits = (t @ router_w).astype(jnp.float32)
    top_v, top_i = lax.top_k(logits, TOP_K)
    gates = jax.nn.softmax(top_v, axis=-1)
    combine = jnp.einsum('nk,nke->ne', gates,
                         jax.nn.one_hot(top_i, N_EXPERTS, dtype=jnp.float32)).astype(t.dtype)
    out = jnp.zeros_like(t)
    for e in range(N_EXPERTS):
        out = out + combine[:, e:e + 1] * _swiglu(t, w_gu[e], w_down[e])
    return out.reshape(shape)

def setup_inputs(seed: int = 0) -> dict:
    key = jax.random.key(seed)
    ks = jax.random.split(key, 24)
    f32 = jnp.float32

    def nrm(k, shape, scale):
        return jax.random.normal(k, shape, f32) * scale

    def gain(k, shape):
        return 1.0 + 0.05 * jax.random.normal(k, shape, f32)

    dt0 = jnp.exp(jax.random.uniform(ks[16], (N_ODD, 2, N_SSM_HEADS), f32, math.log(DT_MIN), math.log(DT_MAX)))
    return {
        "x": nrm(ks[0], (BATCH, SEQ, D_MODEL), 1.0),
        "c": nrm(ks[1], (BATCH, D_MODEL), 1.0),
        "ctx": nrm(ks[2], (BATCH, CTX_LEN, D_MODEL), 1.0),
        "c_ctx": nrm(ks[3], (D_MODEL,), 1.0),
        "ada_w": nrm(ks[4], (DEPTH, D_MODEL, 6 * D_MODEL), 0.5 * D_MODEL ** -0.5),
        "ada_b": nrm(ks[5], (DEPTH, 6 * D_MODEL), 0.01),
        "norm_w": gain(ks[6], (DEPTH, 4, D_MODEL)),
        "mix_in_w": nrm(ks[7], (N_EVEN, D_MODEL, MIX_IN), D_MODEL ** -0.5),
        "q_norm_w": gain(ks[8], (N_EVEN, HEAD_DIM)),
        "k_norm_w": gain(ks[9], (N_EVEN, HEAD_DIM)),
        "mix_out_w": nrm(ks[10], (N_EVEN, MIX_OUT, D_MODEL), MIX_OUT ** -0.5),
        "ffn_gu_w": nrm(ks[11], (N_EVEN, D_MODEL, 2 * D_FF), D_MODEL ** -0.5),
        "ffn_down_w": nrm(ks[12], (N_EVEN, D_FF, D_MODEL), D_FF ** -0.5),
        "ssm_in_w": nrm(ks[13], (N_ODD, D_MODEL, SSM_IN), D_MODEL ** -0.5),
        "ssm_conv_w": nrm(ks[14], (N_ODD, D_CONV, CONV_DIM), D_CONV ** -0.5),
        "ssm_conv_b": nrm(ks[15], (N_ODD, CONV_DIM), 0.01),
        "ssm_dt_bias": dt0 + jnp.log(-jnp.expm1(-dt0)),
        "ssm_a_log": jnp.log(jax.random.uniform(ks[17], (N_ODD, 2, N_SSM_HEADS), f32, A_MIN, A_MAX)),
        "ssm_d": gain(ks[18], (N_ODD, N_SSM_HEADS)),
        "ssm_norm_w": gain(ks[19], (N_ODD, D_INNER)),
        "ssm_out_w": nrm(ks[20], (N_ODD, D_INNER, D_MODEL), D_INNER ** -0.5),
        "router_w": nrm(ks[21], (N_ODD, D_MODEL, N_EXPERTS), D_MODEL ** -0.5),
        "moe_gu_w": nrm(ks[22], (N_ODD, N_EXPERTS, D_MODEL, 2 * D_FF_EXPERT), D_MODEL ** -0.5),
        "moe_down_w": nrm(ks[23], (N_ODD, N_EXPERTS, D_FF_EXPERT, D_MODEL), D_FF_EXPERT ** -0.5),
    }

def reference(x, c, ctx, c_ctx, ada_w, ada_b, norm_w, mix_in_w, q_norm_w, k_norm_w, mix_out_w,
              ffn_gu_w, ffn_down_w, ssm_in_w, ssm_conv_w, ssm_conv_b, ssm_dt_bias, ssm_a_log,
              ssm_d, ssm_norm_w, ssm_out_w, router_w, moe_gu_w, moe_down_w):
    rows = x.shape[1] // GRID_W
    cos, sin = _axial_rope_tables(rows)
    silu_c = jax.nn.silu(c)
    silu_cc = jax.nn.silu(c_ctx)
    for i in range(DEPTH):
        last = i == DEPTH - 1
        j = i // 2
        mx = jnp.split((silu_c @ ada_w[i] + ada_b[i])[:, None, :], 6, axis=-1)
        mc = jnp.split((silu_cc @ ada_w[i] + ada_b[i])[None, None, :], 6, axis=-1)
        hx = _modulate(_rms_norm(x, norm_w[i, 0]), mx[0], mx[1])
        hc = _modulate(_rms_norm(ctx, norm_w[i, 0]), mc[0], mc[1])
        if i % 2 == 0:
            yx, yc = _fourier_attention_mixer(hx, hc, mix_in_w[j], q_norm_w[j], k_norm_w[j],
                                              mix_out_w[j], cos, sin, not last)
        else:
            yx, yc = _ssd_mixer(hx, hc, ssm_in_w[j], ssm_conv_w[j], ssm_conv_b[j], ssm_dt_bias[j],
                                ssm_a_log[j], ssm_d[j], ssm_norm_w[j], ssm_out_w[j], not last)
        x = x + mx[2] * _rms_norm(yx, norm_w[i, 1])
        hx = _modulate(_rms_norm(x, norm_w[i, 2]), mx[3], mx[4])
        if i % 2 == 0:
            fx = _swiglu(hx, ffn_gu_w[j], ffn_down_w[j])
        else:
            fx = _moe(hx, router_w[j], moe_gu_w[j], moe_down_w[j])
        x = x + mx[5] * _rms_norm(fx, norm_w[i, 3])
        if not last:
            ctx = ctx + mc[2] * _rms_norm(yc, norm_w[i, 1])
            hc = _modulate(_rms_norm(ctx, norm_w[i, 2]), mc[3], mc[4])
            if i % 2 == 0:
                fc = _swiglu(hc, ffn_gu_w[j], ffn_down_w[j])
            else:
                fc = _moe(hc, router_w[j], moe_gu_w[j], moe_down_w[j])
            ctx = ctx + mc[5] * _rms_norm(fc, norm_w[i, 3])
    return x


_drawn_inputs = setup_inputs


def setup_inputs(seed=0):
    import zlib

    import numpy as np

    out = dict(_drawn_inputs(seed))
    spreads = {}
    factors = {'q_norm_w': 8.0,
     'k_norm_w': 8.0,
     'ssm_conv_b': 13.597,
     'ssm_d': 7.058,
     'ssm_norm_w': 8.712}
    for name, (base, spread) in spreads.items():
        noise = np.random.default_rng([zlib.crc32(name.encode()), seed]).standard_normal(out[name].shape)
        drawn = base * np.exp(spread * noise) if base else spread * noise
        out[name] = __import__('jax').numpy.asarray(drawn.astype(out[name].dtype))
    for name, factor in factors.items():
        out[name] = (out[name] * factor).astype(out[name].dtype)
    return out
```

```python
from contextlib import ExitStack

import numpy as np
import concourse.bass as bass
from concourse import mybir

P = 128
D_MODEL = 1024
SEQ = 256
CTX_LEN = 256
GRID_W = 64
F_GROUPS = 4
F_GROUP_DIM = D_MODEL // 8
F_WIDTH = F_GROUPS * F_GROUP_DIM
HEAD_DIM = 64
N_HEADS = 8
N_KV = 2
Q_WIDTH = N_HEADS * HEAD_DIM
MIX_IN = F_WIDTH + Q_WIDTH + 2 * N_KV * HEAD_DIM
ROPE_THETA = 10000.0
D_INNER = 2 * D_MODEL
N_SSM_HEADS = 32
N_GROUPS = 4
HPG = 8
D_STATE = 128
D_CONV = 5
CONV_DIM = D_INNER + 2 * N_GROUPS * D_STATE
SSM_IN = D_INNER + CONV_DIM + 2 * N_SSM_HEADS
D_FF = 2816
N_EXPERTS = 8
D_FF_EXPERT = 3584
EPS = 1e-6

KC = D_MODEL // P
LAT, CTX = (0, 1), (2, 3)
NBLK = 4

UNIT = 2048
PIECE = 1024
RAW = 6
SPL = 4
UCOL = 256

N_ADA = 2 * 6 * D_MODEL // UCOL
ADA_FIRST = 2 * D_MODEL // UCOL
U_MIXIN = MIX_IN // UCOL
U_MIXOUT = D_MODEL // UCOL
FFN_STEPS = D_FF // UCOL
MOE_STEPS = D_FF_EXPERT // UCOL
MOE_UNITS = 3 * MOE_STEPS
MOE_PIECES = 2 * MOE_UNITS
GROUP_UNITS = 5
S_MIXIN = 0
S_MIXOUT = S_MIXIN + U_MIXIN
S_FFN = S_MIXOUT + U_MIXOUT
S_DT = S_FFN + 2 * 3 * FFN_STEPS
S_GRP = S_DT + 1
S_SSMOUT = S_GRP + N_GROUPS * GROUP_UNITS
S_MOE = S_SSMOUT + 2 * U_MIXOUT
U_MOE = S_MOE + N_ADA

CAP = 128

C_ID, C_ONE, C_TF, C_TB, C_ST, C_IO, C_I8, C_SEL = 0, 128, 256, 384, 512, 640, 768, 776
N_CONST = 778
V_ADAB, V_CONVB, V_NORM, V_SNORM, V_C, V_CC, V_CONVW = 0, 96, 120, 184, 200, 208, 216
N_COLS = 336

F32 = mybir.dt.float32
F32R = mybir.dt.float32r
I32 = mybir.dt.int32
U32 = mybir.dt.uint32
ALU = mybir.AluOpType
ACT = mybir.ActivationFunctionType
AX = mybir.AxisListType


def swiglu_order(n):
    order = []
    for j in range(n + 2):
        if j < n:
            order += [("g", j), ("u", j)]
        if j >= 2:
            order.append(("d", j - 2))
    return order


def shape_constants():
    i = np.arange(P)
    c = np.zeros((P, N_CONST), np.float32)
    c[:, C_ID:C_ID + P] = np.eye(P)
    c[:, C_ONE:C_ONE + P] = 1.0
    c[:, C_TF:C_TF + P] = i[:, None] <= i[None, :]
    c[:, C_TB:C_TB + P] = i[:, None] >= i[None, :]
    c[:, C_ST:C_ST + P] = i[:, None] < i[None, :]
    c[:, C_IO:C_IO + P] = i[None, :]
    c[:, C_I8:C_I8 + 8] = np.arange(8)[None, :]
    for g in range(4):
        c[32 * g, C_SEL] = 1.0
        c[32 * g + 1, C_SEL + 1] = 1.0
    n = np.arange(SEQ)
    ang = 2 * np.pi * ((n[:, None] * n[None, :]) % SEQ) / SEQ
    s = 1.0 / np.sqrt(float(SEQ * F_GROUP_DIM))
    pos = np.concatenate([np.cos(ang) * s, np.sin(ang) * s], axis=1)
    pos = pos.reshape(2, P, 2 * SEQ).transpose(1, 0, 2).reshape(P, 4 * SEQ)
    angc = 2 * np.pi * ((i[:, None] * i[None, :]) % P) / P
    ch = np.concatenate([np.cos(angc), -np.sin(angc)], axis=1)
    t = np.arange(SEQ)
    freqs = np.float32(ROPE_THETA) ** (-np.arange(0, HEAD_DIM // 2, 2, dtype=np.float32) / np.float32(HEAD_DIM // 2))
    rang = np.concatenate([(t // GRID_W).astype(np.float32)[:, None] * freqs,
                           (t % GRID_W).astype(np.float32)[:, None] * freqs], axis=1).astype(np.float32)
    rope = np.stack([np.cos(rang), np.sin(rang)], axis=0).astype(np.float32)
    rope = rope.reshape(2, 2, P, 32).transpose(2, 0, 1, 3).reshape(P, 128)
    first = np.concatenate([pos, ch, rope], axis=1).astype(np.float32)
    return c, first


N_FIRST = 4 * SEQ + 2 * P + 128


def build(nc, A, out):
    es = ExitStack()
    with es:
        def sb(name, shape, dt=F32):
            return es.enter_context(nc.sbuf_tensor(name, shape, dt))

        def sem(name):
            return es.enter_context(nc.semaphore(name))

        bank = [es.enter_context(nc.psum_tensor(f"bank{i}", [P, 512], F32)) for i in range(8)]

        raw = sb("raw", [P, RAW, UNIT])
        hi = sb("hi", [P, SPL, PIECE], F32R)
        lo = sb("lo", [P, SPL, PIECE], F32R)
        xh_t = sb("xh_t", [P, KC * 512], F32R)
        xl_t = sb("xl_t", [P, KC * 512], F32R)
        hth = sb("hth", [P, 2, 512], F32R)
        htl = sb("htl", [P, 2, 512], F32R)
        xres = sb("xres", [P, 2, D_MODEL])
        con = sb("con", [P, N_CONST])
        cols = sb("cols", [P, N_COLS])
        ada = sb("ada", [P, 2, 48, 2])
        moda = sb("moda", [P, 4, KC, 2])
        gatec = sb("gatec", [P, 4, KC, 2])
        sc = sb("sc", [P, KC, 32])
        ss = sb("ss", [P, 32])
        rms = sb("rms", [P, 32])
        rstd = sb("rstd", [P, 32])
        epsc = sb("epsc", [P, 1])
        AR = 18400
        ar = sb("ar", [P, AR])

        xh = xh_t[:, :].rearrange("p (k n) -> p k n", k=KC)
        xl = xl_t[:, :].rearrange("p (k n) -> p k n", k=KC)
        xh16 = xh_t[:, :].rearrange("p (k n) -> p k n", k=16)
        xl16 = xl_t[:, :].rearrange("p (k n) -> p k n", k=16)

        ident = con[:, C_ID:C_ID + P]
        ones = con[:, C_ONE:C_ONE + P]
        tri = [con[:, C_TF:C_TF + P], con[:, C_TB:C_TB + P]]
        strict = con[:, C_ST:C_ST + P]
        iota = con[:, C_IO:C_IO + P]
        iota8 = con[:, C_I8:C_I8 + 8]
        sel = con[:, C_SEL:C_SEL + 2]

        class Arena:
            def __init__(self, base=0):
                self.at = base

            def take(self, n):
                a = ar[:, self.at:self.at + n]
                self.at += n
                assert self.at <= AR, self.at
                return a

        def v3(a, k):
            return a.rearrange("p (k n) -> p k n", k=k)

        m0 = Arena()
        xctx = v3(m0.take(2 * D_MODEL), 2)
        base0 = m0.at
        xn = [m0.take(D_MODEL) for _ in range(2)]
        t32 = m0.take(D_MODEL)
        px = v3(m0.take(NBLK * MIX_IN), NBLK)
        first = m0.take(N_FIRST)
        dpos = v3(first[:, 0:4 * SEQ], 2)
        dch = v3(first[:, 4 * SEQ:4 * SEQ + 2 * P], 2)
        rope = first[:, 4 * SEQ + 2 * P:N_FIRST].rearrange("p (t b n) -> p t b n", t=2, b=2)
        qkw = v3(m0.take(2 * HEAD_DIM), 2)
        part = m0.take(UCOL)
        vec_at = m0.at
        m1 = Arena(base0)
        t1s = [m1.take(512) for _ in range(2)]
        prob = [m1.take(512) for _ in range(2)]
        pts = [m1.take(512) for _ in range(2)]
        assert m1.at <= base0 + 3 * D_MODEL
        m2 = Arena(vec_at)
        qT = m2.take(NBLK * 512).rearrange("p (b c n) -> p b c n", b=NBLK, c=4)
        kT = v3(m2.take(2 * 512), 2)
        qsq = m2.take(640)
        kdup = m2.take(256)
        rtmp = m2.take(4 * 320)
        qss = v3(m2.take(40), 4)
        qrms = v3(m2.take(40), 4)
        qrs = v3(m2.take(40), 4)
        mx = m2.take(32)
        nmx = m2.take(32)
        rsum = m2.take(32)
        rinv = m2.take(32)
        m3 = Arena(vec_at)
        va, vb, vc = m3.take(P), m3.take(P), m3.take(P)
        m4 = Arena(base0 + 3 * D_MODEL)
        y = v3(m4.take(NBLK * D_MODEL), NBLK)
        m5 = Arena(m4.at)
        grow = [m5.take(D_MODEL) for _ in range(4)]
        sg = [m5.take(UCOL) for _ in range(2)]
        hb = [m5.take(UCOL) for _ in range(2)]
        ptmp = m5.take(D_MODEL)
        pjunk = m5.take(D_MODEL)

        s0 = Arena(0)
        gy = v3(s0.take(16 * SEQ), 16)
        dt_ = v3(s0.take(256), 4)
        dta = v3(s0.take(256), 4)
        acum = v3(s0.take(256), 4)
        cdec = v3(s0.take(256), 4)
        eE = v3(s0.take(256), 4)
        st1, st2, st3 = s0.take(256), s0.take(256), s0.take(256)
        dbias, arow = s0.take(64), s0.take(64)
        drow = s0.take(32)
        dcol = s0.take(16)
        cT = s0.take(256)
        bT = s0.take(512)
        xsT = v3(s0.take(4 * 512), 4)
        btok = v3(s0.take(512), 4)
        xtok = v3(s0.take(4 * 512), 4)
        cbm = s0.take(512).rearrange("p (d b n) -> p d b n", d=2, b=2)
        cpad = [s0.take(2 * 260).rearrange("p (s n) -> p s n", s=2) for _ in range(2)]
        cacc = [s0.take(512) for _ in range(2)]
        xE = s0.take(512)
        xdt = s0.take(512)
        mt = [s0.take(512) for _ in range(2)]
        ce = [s0.take(512) for _ in range(2)]
        hst = [s0.take(512) for _ in range(2)]
        o0 = Arena(0)
        yout = v3(o0.take(2 * D_MODEL), 2)
        mgrow = [o0.take(D_MODEL) for _ in range(2)]
        mptmp = o0.take(D_MODEL)
        mpjunk = o0.take(D_MODEL)
        mxn = [o0.take(D_MODEL) for _ in range(2)]
        mt32 = o0.take(D_MODEL)
        yexp = o0.take(D_MODEL)
        msg = [o0.take(UCOL) for _ in range(2)]
        mhb = [o0.take(UCOL) for _ in range(2)]
        slot1 = v3(o0.take(256), 2)
        slotg = v3(o0.take(256), 2)
        gT = v3(o0.take(256), 2)
        rw = v3(o0.take(64), 8)
        lg = v3(o0.take(16), 2)
        top = v3(o0.take(16), 2)
        idxf = v3(o0.take(16), 2)
        sel1 = v3(o0.take(16), 2)
        sel2 = v3(o0.take(16), 2)
        comb = v3(o0.take(16), 2)
        mask = v3(o0.take(16), 2)
        posm = v3(o0.take(16), 2)
        posm2 = v3(o0.take(16), 2)
        gd, ge, gs, g1, g2 = (o0.take(2) for _ in range(5))
        cntf = o0.take(8)
        idx8 = sb("idx8", [P, 2, 8], U32)
        cnt = sb("cnt", [P, 8], I32)

        raw_landed = [sem(f"raw_landed{i}") for i in range(RAW)]
        hi_ready, lo_ready, piece_used = sem("hi_ready"), sem("lo_ready"), sem("piece_used")
        ada_used, ada_part, ada_col, ada_done = (sem(n) for n in ("ada_used", "ada_part", "ada_col", "ada_done"))
        ld_x, ld_ctx, ld_con, ld_first, ld_vec, ld_qkw, ld_ssm, ld_rw = (
            sem(n) for n in ("ld_x", "ld_ctx", "ld_con", "ld_first", "ld_vec", "ld_qkw", "ld_ssm", "ld_rw"))
        zeroed, vec_t, vec_cols, sc_ready, eps_ready = (
            sem(n) for n in ("zeroed", "vec_t", "vec_cols", "sc_ready", "eps_ready"))
        mod_ready = sem("mod_ready")
        n_ss, n_rms, n_rstd, xn_ready, xt_done, xmod_done, xsplit_hi, xsplit_done = (
            sem(n) for n in ("n_ss", "n_rms", "n_rstd", "xn_ready", "xt_done", "xmod_done", "xsplit_hi", "xsplit_done"))
        lin_evac = sem("lin_evac")
        dft_t1, dft_t1s, dft_out, dft_hi, dft_lo = (sem(n) for n in ("dft_t1", "dft_t1s", "dft_out", "dft_hi", "dft_lo"))
        qk_v, qk_ss, qk_rms, qk_ready, qk_t, qk_tc = (
            sem(n) for n in ("qk_v", "qk_ss", "qk_rms", "qk_ready", "qk_t", "qk_tc"))
        at_s, at_m, at_mx, at_exp, at_r, at_nrm, at_t, at_pt, at_pv, at_oh, at_ol = (
            sem(n) for n in ("at_s", "at_m", "at_mx", "at_exp", "at_r", "at_nrm", "at_t", "at_pt", "at_pv", "at_oh", "at_ol"))
        grow_t, grow_ready = sem("grow_t"), sem("grow_ready")
        po_ss, po_rms, po_rstd, po_t, po_done = (sem(n) for n in ("po_ss", "po_rms", "po_rstd", "po_t", "po_done"))
        sil_done, h_done, ht_t, ht_hi, ht_lo, y_evac = (
            sem(n) for n in ("sil_done", "h_done", "ht_t", "ht_hi", "ht_lo", "y_evac"))
        dt_v, dt_e, dt_a, dt_t, dt_x = (sem(n) for n in ("dt_v", "dt_e", "dt_a", "dt_t", "dt_x"))
        pr_copy, cv_v, cv_acc, cv_out, tr_t, tr_copy, cb_t, cb_m = (
            sem(n) for n in ("pr_copy", "cv_v", "cv_acc", "cv_out", "tr_t", "tr_copy", "cb_t", "cb_m"))
        xe_ready, st_t, st_v, st_done = (sem(n) for n in ("xe_ready", "st_t", "st_v", "st_done"))
        xdt_ready, bc_t, ce_exp, sg_ready, mt_exp, mt_ready, ce_ready, yy_t = (
            sem(n) for n in ("xdt_ready", "bc_t", "ce_exp", "sg_ready", "mt_exp", "mt_ready", "ce_ready", "yy_t"))
        gy_v, gy_done, gq_done, gn_t, gn_copy, gn_rms, gn_rstd, gf_v, gf_hi, gf_done = (
            sem(n) for n in ("gy_v", "gy_done", "gq_done", "gn_t", "gn_copy", "gn_rms", "gn_rstd", "gf_v", "gf_hi", "gf_done"))
        lg_t, rt_v, rt_e, rt_t, rt_done = (sem(n) for n in ("lg_t", "rt_v", "rt_e", "rt_t", "rt_done"))
        slot_ready, gat_t, gat_mod, gat_hi, gat_lo, gs_ready, gs_t, gT_ready, cmb_t, cmb_add = (
            sem(n) for n in ("slot_ready", "gat_t", "gat_mod", "gat_hi", "gat_lo", "gs_ready", "gs_t", "gT_ready", "cmb_t", "cmb_add"))
        stored = sem("stored")
        vstep, astep = sem("vstep"), sem("astep")
        ssg = [st1, st2, st3, sc[:, :, :].rearrange("p k n -> p (k n)")]

        def unit_of_split(s):
            return s + ADA_FIRST if s < S_MIXOUT else s + N_ADA

        def wcols(w, c0, n):
            return w.rearrange("(t p) n -> p t n", p=P)[:, :, c0:c0 + n]

        def rawv(u, t):
            return raw[:, u % RAW, :].rearrange("p (t n) -> p t n", t=t)

        order_ffn = swiglu_order(FFN_STEPS)
        order_moe = swiglu_order(MOE_STEPS)

        def pos_of(order):
            return {k: i for i, k in enumerate(order)}

        pos_ffn, pos_moe = pos_of(order_ffn), pos_of(order_moe)

        xblk = [xres[:, 0, :], xres[:, 1, :], xctx[:, 0, :], xctx[:, 1, :]]
        NORMS = ([(0, b // 2, b) for b in range(4)] + [(1, b // 2, b) for b in range(4)] +
                 [(2, b // 2, b) for b in range(4)] + [(3, 0, b) for b in range(2)])
        N_MLP, N_SSM, N_MOE = 4, 8, 12
        POSTS = ([(0, b // 2, b) for b in range(4)] + [(1, b // 2, b) for b in range(4)] +
                 [(2, 0, b) for b in range(2)] + [(3, 0, b) for b in range(2)])
        GROWS = [(0, 0), (0, 1), (1, 0), (1, 1), (2, 0), (3, 0)]

        def grow_tile(r):
            return grow[r] if r < 4 else mgrow[r - 4]

        def grow_of(n):
            return GROWS.index(POSTS[n][:2])

        def post_src(n):
            b = POSTS[n][2]
            return y[:, b, :] if n < 8 else yout[:, b, :]

        def xn_of(n):
            return mxn[n % 2] if n >= N_MOE else xn[n % 2]

        def t32_of(n):
            return mt32 if n >= N_MOE else t32

        def mod_cols(m, s):
            l, w = m // 2, m % 2
            return moda[:, m, :, s], ada[:, l, 24 * w:24 * w + KC, s]

        AT_SCALE = HEAD_DIM ** -0.5
        ITERS = [("dft", i) for i in range(8)] + [("att", i) for i in range(32)]

        def at_info(i):
            s, b, h = i // 16, i // 8, i % 8
            return s, b, h, (0, 4) if s == 0 else (2, 2)

        ssd_idx = [(d, b, q) for d, bs in ((0, (0, 1)), (1, (1, 0))) for b in bs for q in range(2)]
        ssd_states = [(d, k, b) for d, bs in ((0, (2, 3, 0)), (1, (3, 2, 1))) for k, b in enumerate(bs)]
        NQ = len(ssd_idx)
        NST = len(ssd_states)

        LIN_MIXOUT = U_MIXIN * NBLK
        LIN_SSMOUT = LIN_MIXOUT + U_MIXOUT * NBLK
        RT_N = 1

        def is_pair_unit(s):
            return S_GRP <= s < S_SSMOUT and (s - S_GRP) % GROUP_UNITS == 0

        split_unit = {unit_of_split(s): s for s in range(S_MOE)}
        landed, total = {}, [0] * RAW
        for u in range(U_MOE):
            total[u % RAW] += 32 if u in split_unit and is_pair_unit(split_unit[u]) else 16
            landed[u] = total[u % RAW]
        PER_SLOT = 16 * (MOE_UNITS // RAW)

        def landed_moe(i, it):
            return total[(U_MOE + i) % RAW] + 16 * (i // RAW + 1) + it * PER_SLOT

        P_MOE = 2 * S_MOE
        FFN_N = len(order_ffn)
        C_MOE, T_MOE, Y_MOE = 2 * 2 * FFN_STEPS, 2 * FFN_STEPS, 8

        block = es.enter_context(nc.Block())

        @block.sync
        def _(sp):
            sp.dma_start(vb[0:64, :], A["norm_w"].rearrange("i n (k q) -> (i n k) q", q=P)).then_inc(ld_vec, 16)
            sp.dma_start(vb[64:80, :], A["ssm_norm_w"].rearrange("i (k q) -> (i k) q", q=P)).then_inc(ld_vec, 16)
            sp.dma_start(vb[80:88, :], A["c"].rearrange("i (k q) -> (i k) q", q=P)).then_inc(ld_vec, 16)
            sp.dma_start(vb[88:96, :], A["c_ctx"].rearrange("(k q) -> k q", q=P)).then_inc(ld_vec, 16)
            sp.dma_start(con[:, :], A["const"]).then_inc(ld_con, 16)
            sp.dma_start(va[0:96, :], A["ada_b"].rearrange("l (c q) -> (l c) q", q=P)).then_inc(ld_vec, 16)
            sp.dma_start(va[96:120, :], A["ssm_conv_b"].rearrange("l (c q) -> (l c) q", q=P)).then_inc(ld_vec, 16)
            sp.dma_start(vc[0:120, :], A["ssm_conv_w"].rearrange("l t (c q) -> (l t c) q", q=P)).then_inc(ld_vec, 16)

            owner = {}

            def free(u):
                if u >= RAW:
                    kind, n = owner[u - RAW]
                    if kind == "ada":
                        sp.wait_ge(ada_used, n + 1)
                    else:
                        sp.wait_ge(lo_ready, 2 * (n + 1))

            def load(u, kind, n, dst, src):
                free(u)
                sp.dma_start(dst, src).then_inc(raw_landed[u % RAW], 16)
                owner[u] = (kind, n)

            def load_ada(a0, a1):
                for a in range(a0, a1):
                    l, c = divmod(a, N_ADA // 2)
                    u = a if a < ADA_FIRST else a + U_MIXIN
                    load(u, "ada", a, rawv(u, 8), wcols(A["ada_w"][l], c * UCOL, UCOL))

            def load_cols(s, w, c0, n=UCOL):
                u = unit_of_split(s)
                load(u, "split", s, rawv(u, 8)[:, :, 0:n], wcols(w, c0, n))

            load_ada(0, 3)
            sp.dma_start(xres[:, :, :], A["x"].rearrange("o (b p) n -> p (o b) n", p=P)).then_inc(ld_x, 16)
            sp.dma_start(xctx, A["ctx"].rearrange("o (b p) n -> p (o b) n", p=P)).then_inc(ld_ctx, 16)
            load_ada(3, ADA_FIRST)
            for i in range(U_MIXIN):
                load_cols(S_MIXIN + i, A["mix_in_w"][0], i * UCOL)
            sp.dma_start(first, A["first"]).then_inc(ld_first, 16)
            sp.dma_start(qkw[:, 0, :], A["q_norm_w"][0].partition_broadcast(P)).then_inc(ld_qkw, 16)
            sp.dma_start(qkw[:, 1, :], A["k_norm_w"][0].partition_broadcast(P)).then_inc(ld_qkw, 16)
            load_ada(ADA_FIRST, N_ADA)
            for i in range(U_MIXOUT):
                load_cols(S_MIXOUT + i, A["mix_out_w"][0], i * UCOL)
            gu, dn = A["ffn_gu_w"][0], A["ffn_down_w"][0]
            for ps in range(2):
                for i, (k, j) in enumerate(order_ffn):
                    s = S_FFN + ps * FFN_N + i
                    if k == "d":
                        u = unit_of_split(s)
                        load(u, "split", s, rawv(u, 2),
                             dn[j * UCOL:(j + 1) * UCOL, :].rearrange("(t p) n -> p t n", p=P))
                    else:
                        load_cols(s, gu, j * UCOL + (D_FF if k == "u" else 0))
            w_in = A["ssm_in_w"][0]
            x0, b0, c0 = D_INNER, 2 * D_INNER, 2 * D_INNER + N_GROUPS * D_STATE
            load_cols(S_DT, w_in, D_INNER + CONV_DIM, 2 * N_SSM_HEADS)
            for g in range(N_GROUPS):
                s = S_GRP + g * GROUP_UNITS
                u = unit_of_split(s)
                load(u, "split", s, rawv(u, 8)[:, :, 0:P], wcols(w_in, b0 + g * P, P))
                sp.dma_start(rawv(u, 8)[:, :, P:2 * P], wcols(w_in, c0 + g * P, P)).then_inc(raw_landed[u % RAW], 16)
                for i in range(2):
                    load_cols(s + 1 + i, w_in, x0 + g * 512 + i * UCOL)
                for i in range(2):
                    load_cols(s + 3 + i, w_in, g * 512 + i * UCOL)
                if g == 0:
                    sp.wait_ge(xsplit_done, N_SSM + 4)
                    for dst, src in ((dbias, A["ssm_dt_bias"].rearrange("l d h -> (l d h)")),
                                     (arow, A["ssm_a_log"].rearrange("l d h -> (l d h)")),
                                     (drow, A["ssm_d"][0])):
                        sp.dma_start(dst, src.partition_broadcast(P)).then_inc(ld_ssm, 16)
            for i in range(2 * U_MIXOUT):
                q, kh = divmod(i, 2)
                load_cols(S_SSMOUT + i, A["ssm_out_w"][0][kh * D_MODEL:(kh + 1) * D_MODEL, :], q * UCOL)
            sp.wait_ge(gf_done, 4)
            sp.dma_start(rw, A["router_w"][0].rearrange("(t p) n -> p t n", p=P)).then_inc(ld_rw, 16)

            def expert_weights(e, it):
                gu = A["moe_gu_w"][0][bass.ds(e, 1)].rearrange("o k n -> (o k) n")
                dn = A["moe_down_w"][0][bass.ds(e, 1)].rearrange("o k n -> (o k) n")
                for i, (k, j) in enumerate(order_moe):
                    u = U_MOE + i
                    sp.wait_ge(lo_ready, it * MOE_PIECES + 2 * (S_MOE + i - RAW + 1))
                    if k == "d":
                        sp.dma_start(rawv(u, 2), dn[j * UCOL:(j + 1) * UCOL, :].rearrange("(t p) n -> p t n", p=P)
                                     ).then_inc(raw_landed[u % RAW], 16)
                    else:
                        sp.dma_start(rawv(u, 8), wcols(gu, j * UCOL + (D_FF_EXPERT if k == "u" else 0), UCOL)
                                     ).then_inc(raw_landed[u % RAW], 16)

            with sp.Fori(0, N_EXPERTS) as e:
                expert_weights(e, e)
            sp.wait_ge(rt_done, RT_N)
            with sp.Fori(0, N_EXPERTS) as e:
                n = sp.value_load(cnt[0:1, bass.ds(e, 1)], min_val=0, max_val=2 * P)
                with sp.If(n > CAP):
                    expert_weights(e, e + N_EXPERTS)
                with sp.Else():
                    for k in range(RAW):
                        s = raw_landed[(U_MOE + k) % RAW]
                        sp.wait_ge(s, landed_moe(k, e + N_EXPERTS) - 16)
                        sp.sem_inc(s, PER_SLOT)
            for b in range(2):
                sp.wait_ge(po_done, 11 + b)
                sp.dma_start(out.rearrange("o (b p) n -> p (o b) n", p=P)[:, b, :], xres[:, b, :]).then_inc(stored, 16)
            sp.wait_ge(stored, 32)

        @block.gpsimd
        def _(pool):
            pool.memset(sc[:, :, :], 0.0).then_inc(zeroed, 1)
            pool.memset(epsc[:, :], EPS).then_inc(eps_ready, 1)
            pool.wait_ge(xsplit_done, N_SSM + 4)
            for t in cpad:
                pool.memset(t, 0.0).then_inc(zeroed, 1)
            for g in range(N_GROUPS):
                def scaled_x(dst, blk, scale, d, done, used, n):
                    if n > 0:
                        pool.wait_ge(used, n)
                    a = d * N_SSM_HEADS + g * HPG
                    pool.tensor_tensor(dst.rearrange("p (h q) -> p h q", h=HPG),
                                       xtok[:, blk, :].rearrange("p (h q) -> p h q", h=HPG),
                                       scale[:, blk, a:a + HPG].unsqueeze(2).to_broadcast((P, HPG, 64)),
                                       ALU.mult).then_inc(done, 1)

                pool.wait_ge(dt_x, 1)
                pool.wait_ge(tr_copy, 5 * (g + 1))
                pool.wait_ge(cv_out, 6 * (g + 1))

                def xE_(k):
                    d, _, blk = ssd_states[k]
                    scaled_x(xE, blk, eE, d, xe_ready, st_t, g * NST + k)

                def xdt_(m):
                    q = 2 * m
                    d, b, _ = ssd_idx[q]
                    scaled_x(xdt, b, dt_, d, xdt_ready, yy_t, g * NQ + q)

                def ce_(q):
                    d, b, _ = ssd_idx[q]
                    pool.wait_ge(ce_exp, g * NQ + q + 1)
                    pool.tensor_tensor(v3(ce[q % 2], 4), v3(ce[q % 2], 4),
                                       cT[:, b * P:(b + 1) * P].unsqueeze(1).to_broadcast((P, 4, P)),
                                       ALU.mult).then_inc(ce_ready, 1)

                xE_(0)
                xE_(1)
                xdt_(0)
                ce_(0)
                ce_(1)
                xE_(2)
                xdt_(1)
                ce_(2)
                xE_(3)
                xE_(4)
                ce_(3)
                xdt_(2)
                ce_(4)
                ce_(5)
                xE_(5)
                xdt_(3)
                ce_(6)
                ce_(7)

        @block.tensor
        def _(pe):
            mm = pe.matmul

            def tok3(o, a_hi, a_lo, w_hi, w_lo, first, last):
                mm(o, a_hi, w_hi, start=first, stop=False)
                mm(o, a_hi, w_lo, start=False, stop=False)
                return mm(o, a_lo, w_hi, start=False, stop=last)

            def wpart(p, t, n, off=0, width=None):
                a = t * n + off
                return hi[:, p % SPL, a:a + (width or n)], lo[:, p % SPL, a:a + (width or n)]

            pe.wait_ge(ld_vec, 16 * 7)
            pe.wait_ge(ld_con, 16)
            for t, n, c in ((vb, 96, 0), (va, 120, 1), (vc, 120, 2)):
                pe.transpose(bank[5 + c][:, 0:n], t[0:n, :], ident[0:n, 0:n]).then_inc(vec_t, 1)

            def ada_a(a):
                u = a if a < ADA_FIRST else a + U_MIXIN
                pe.wait_ge(raw_landed[u % RAW], landed[u])
                if a == 0:
                    pe.wait_ge(sc_ready, 2)
                if a > 0:
                    pe.wait_ge(ada_part, a)
                w = rawv(u, 8)
                for t in range(2):
                    for g in range(4):
                        m = mm(bank[6][32 * g:32 * g + 32, 0:UCOL], sc[:, 2 * g + t, :], w[:, 2 * g + t, :],
                               start=(t == 0), stop=(t == 1), tile_position=(0, 32 * g))
                m.then_inc(ada_used, 1)

            def ada_b(a):
                pe.wait_ge(ada_part, a + 1)
                if a > 0:
                    pe.wait_ge(ada_done, a)
                for i in range(2):
                    m = mm(bank[7][:, 2 * i:2 * i + 2], part[:, i * P:(i + 1) * P], sel, start=True, stop=True)
                m.then_inc(ada_col, 1)

            pe.wait_ge(vec_cols, 3)
            for a in range(ADA_FIRST + 1):
                if a < ADA_FIRST:
                    ada_a(a)
                if a >= 1:
                    ada_b(a - 1)

            def norm_t(n):
                pe.wait_ge(xn_ready, n + 1)
                if n >= 2:
                    pe.wait_ge(xmod_done, n - 1)
                for k in range(KC):
                    m = pe.transpose(bank[2 * (n % 2) + k // 4][:, (k % 4) * P:(k % 4 + 1) * P],
                                     xn_of(n)[:, k * P:(k + 1) * P], ident)
                m.then_inc(xt_done, 1)

            def linear(s0, lin0):
                for u in range(U_MIXIN if s0 == S_MIXIN else U_MIXOUT):
                    for h in range(2):
                        p = 2 * (s0 + u) + h
                        pe.wait_ge(lo_ready, p + 1)
                        for b in range(NBLK):
                            if h == 0 and u >= 2:
                                pe.wait_ge(lin_evac, lin0 + (u - 2) * NBLK + b + 1)
                            for t in range(4):
                                k = 4 * h + t
                                m = tok3(bank[(u % 2) * 4 + b][:, 0:UCOL], xh[:, k, b * P:(b + 1) * P],
                                         xl[:, k, b * P:(b + 1) * P], *wpart(p, t, UCOL),
                                         first=(k == 0), last=(k == KC - 1))
                        m.then_inc(piece_used, 1)

            for n in range(4):
                norm_t(n)
            pe.wait_ge(xsplit_done, 4)
            pe.wait_ge(ada_done, ADA_FIRST)
            linear(S_MIXIN, 0)

            pe.wait_ge(ld_first, 16)
            pe.wait_ge(lin_evac, LIN_MIXOUT)

            def dft_1(i):
                s, g = divmod(i, 4)
                if i >= 2:
                    pe.wait_ge(dft_t1s, i - 1)
                for b in range(2):
                    m = mm(bank[i % 2][:, :], px[:, 2 * s + b, g * P:(g + 1) * P], dpos[:, b, :],
                           start=(b == 0), stop=(b == 1))
                m.then_inc(dft_t1, 1)

            def dft_2(i):
                pe.wait_ge(dft_t1s, i + 1)
                if i >= 2:
                    pe.wait_ge(dft_lo, i - 1)
                o = bank[2 + i % 2][:, 0:SEQ]
                mm(o, dch[:, 0, :], t1s[i % 2][:, 0:SEQ], start=True, stop=False)
                mm(o, dch[:, 1, :], t1s[i % 2][:, SEQ:2 * SEQ], start=False, stop=True).then_inc(dft_out, 1)

            def qk_t_(b):
                pe.wait_ge(qk_ready, b + 1)
                if b >= 1:
                    pe.wait_ge(qk_tc, 2 * b)
                for c in range(4):
                    a = F_WIDTH + c * P
                    pe.transpose(bank[4][:, c * P:(c + 1) * P], px[:, b, a:a + P], ident)
                for v in range(N_KV):
                    m = pe.transpose(bank[5][:, v * P:(v + 1) * P], kdup[:, v * P:(v + 1) * P], ident)
                m.then_inc(qk_t, 1)

            def att_s(i):
                s, b, h, (k0, nk) = at_info(i)
                if i >= 2:
                    pe.wait_ge(at_exp, i - 1)
                r = (h % 2) * 64
                mm(bank[i % 2][:, 0:nk * P], qT[r:r + 64, b, h // 2, :], kT[r:r + 64, h // 4, k0 % 4 * P:(k0 % 4 + nk) * P],
                   start=True, stop=True).then_inc(at_s, 1)

            def att_t(i):
                nk = at_info(i)[3][1]
                pe.wait_ge(at_nrm, i + 1)
                if i >= 2:
                    pe.wait_ge(at_pt, i - 1)
                for c in range(nk):
                    m = pe.transpose(bank[2 + i % 2][:, c * P:(c + 1) * P], prob[i % 2][:, c * P:(c + 1) * P], ident)
                m.then_inc(at_t, 1)

            def att_pv(i):
                s, b, h, (k0, nk) = at_info(i)
                pe.wait_ge(at_pt, i + 1)
                if h == 0 and b >= 2:
                    pe.wait_ge(at_ol, b - 1)
                r = (h % 2) * 64
                for c in range(nk):
                    a = F_WIDTH + Q_WIDTH + (N_KV + h // 4) * 64
                    m = mm(bank[4 + b % 2][r:r + 64, (h // 2) * P:(h // 2 + 1) * P], px[:, k0 + c, a:a + 64],
                           pts[i % 2][:, c * P:(c + 1) * P], start=(c == 0), stop=(c == nk - 1))
                m.then_inc(at_pv, 1)

            def step(it):
                return ITERS[it] if 0 <= it < len(ITERS) else (None, 0)

            for it in range(len(ITERS) + 2):
                if it == 8:
                    for b in range(NBLK):
                        qk_t_(b)
                    pe.wait_ge(qk_tc, 2 * NBLK)
                k, i = step(it)
                if k == "dft":
                    dft_1(i)
                if k == "att":
                    att_s(i)
                if it < len(ITERS):
                    ada_a(ADA_FIRST + it)
                k, i = step(it - 1)
                if k == "dft":
                    dft_2(i)
                if k == "att":
                    att_t(i)
                k, i = step(it - 2)
                if k == "att":
                    att_pv(i)
                if 1 <= it <= len(ITERS):
                    ada_b(ADA_FIRST + it - 1)
            pe.wait_ge(at_ol, 4)
            pe.wait_ge(dft_lo, 8)
            pe.wait_ge(ada_done, N_ADA)
            linear(S_MIXOUT, LIN_MIXOUT)

            def grow_(r):
                m_, s = GROWS[r]
                if r >= 2:
                    pe.wait_ge(grow_ready, r - 1)
                for k in range(KC):
                    m = mm(bank[4 + 2 * (r % 2) + k // 4][:, (k % 4) * P:(k % 4 + 1) * P],
                           gatec[:, m_, k, s:s + 1].to_broadcast((P, P)), ident, start=True, stop=True)
                m.then_inc(grow_t, 1)

            pe.wait_ge(mod_ready, 8)
            pe.wait_ge(lin_evac, LIN_SSMOUT)
            for r in range(4):
                grow_(r)
            for n in range(4, 8):
                norm_t(n)
            pe.wait_ge(grow_ready, 4)

            def swiglu(s0, it, nblk, n, pos, xoff, c0, t0, y_free, at_step=None):
                pd, cd, td = it * MOE_PIECES, it * MOE_STEPS, it * MOE_STEPS
                for j in range(n + 2):
                    for kind in ("g", "u") if j < n else ():
                        for h in range(2):
                            p = 2 * (s0 + pos[(kind, j)]) + h
                            pe.wait_ge(lo_ready, pd + p + 1)
                            for b in range(nblk):
                                c = c0 + j * nblk + b
                                if kind == "g" and h == 0 and c >= 2:
                                    pe.wait_ge(h_done, cd + c - 1)
                                o = bank[4 + c % 2][:, 0:UCOL] if kind == "g" else bank[4 + c % 2][:, UCOL:2 * UCOL]
                                for t in range(4):
                                    k = 4 * h + t
                                    a = xoff + b * P
                                    m = tok3(o, xh[:, k, a:a + P], xl[:, k, a:a + P], *wpart(p, t, UCOL),
                                             first=(k == 0), last=(k == KC - 1))
                            m.then_inc(piece_used, 1)
                    if 1 <= j <= n:
                        tj = t0 + j - 1
                        pe.wait_ge(h_done, cd + c0 + j * nblk)
                        if tj >= 2:
                            pe.wait_ge(ht_lo, td + tj - 1)
                        for b in range(nblk):
                            for i in range(2):
                                m = pe.transpose(bank[6 + tj % 2][:, (2 * b + i) * P:(2 * b + i + 1) * P],
                                                 hbuf((c0 + (j - 1) * nblk + b) % 2)[:, i * P:(i + 1) * P], ident)
                        m.then_inc(ht_t, 1)
                    if at_step:
                        at_step(j)
                    if j >= 2:
                        tj = t0 + j - 2
                        pe.wait_ge(ht_lo, td + tj + 1)
                        if j == 2 and y_free is not None:
                            pe.wait_ge(y_evac, y_free)
                        for h in range(2):
                            p = 2 * (s0 + pos[("d", j - 2)]) + h
                            pe.wait_ge(lo_ready, pd + p + 1)
                            for b in range(nblk):
                                a = (2 * b + h) * P
                                for half in range(2):
                                    m = tok3(bank[2 * b + half][:, :], hth[:, tj % 2, a:a + P], htl[:, tj % 2, a:a + P],
                                             *wpart(p, 0, 1024, half * 512, 512),
                                             first=(j == 2 and h == 0), last=(j == n + 1 and h == 1))
                            m.then_inc(piece_used, 1)

            def hbuf(i):
                return hcur[0][i]

            hcur = [hb]
            pe.wait_ge(xsplit_done, 8)
            for ps in range(2):
                swiglu(S_FFN + ps * FFN_N, 0, 2, FFN_STEPS, pos_ffn, ps * 2 * P, ps * 2 * FFN_STEPS, ps * FFN_STEPS,
                       4 if ps else None)

            for n in range(8, 12):
                norm_t(n)
            pe.wait_ge(xsplit_done, 12)
            for h in range(2):
                p = 2 * S_DT + h
                pe.wait_ge(lo_ready, p + 1)
                for b in range(NBLK):
                    for t in range(4):
                        k = 4 * h + t
                        m = tok3(bank[b][:, 0:64], xh[:, k, b * P:(b + 1) * P], xl[:, k, b * P:(b + 1) * P],
                                 *wpart(p, t, UCOL, 0, 64), first=(k == 0), last=(k == KC - 1))
                m.then_inc(piece_used, 1)

            def proj(g, ui):
                s = S_GRP + g * GROUP_UNITS + ui
                for h in range(2):
                    p = 2 * s + h
                    pe.wait_ge(lo_ready, p + 1)
                    if h == 0:
                        if ui >= 2:
                            pe.wait_ge(pr_copy, 10 * g + 2 * (ui - 1))
                        elif g > 0:
                            pe.wait_ge(pr_copy, 10 * g)
                        if g == 0 and ui == 0:
                            pe.wait_ge(dt_v, 4)
                        if ui == 1 and g > 0:
                            pe.wait_ge(sg_ready, g * NQ)
                    for c in range(2):
                        n = 512 if ui in (1, 2) or (ui == 0 and c == 0) else SEQ
                        o = bank[2 * (ui % 2) + c][:, 0:n]
                        for t in range(4):
                            k = 4 * h + t
                            w_hi, w_lo = wpart(p, t, UCOL, c * P, P)
                            mm(o, w_hi, xh[:, k, 0:n], start=(k == 0), stop=False)
                            mm(o, w_hi, xl[:, k, 0:n], start=False, stop=False)
                            m = mm(o, w_lo, xh[:, k, 0:n], start=False, stop=(k == KC - 1))
                    m.then_inc(piece_used, 1)

            def to_tok(g, i):
                pe.wait_ge(cv_out, 6 * g + (1 if i == 0 else i + 2))
                if g * 5 + i > 0:
                    pe.wait_ge(tr_copy, g * 5 + i)
                if i == 0 and g > 0:
                    pe.wait_ge(gn_copy, g)
                src = bT if i == 0 else xsT[:, i - 1, :]
                for b in range(NBLK):
                    m = pe.transpose(bank[5][:, b * P:(b + 1) * P], src[:, b * P:(b + 1) * P], ident)
                m.then_inc(tr_t, 1)

            def decay_sums():
                pe.wait_ge(dt_a, 1)
                for b in range(NBLK):
                    for d in range(2):
                        a = 64 * b + 32 * d
                        mm(bank[6][:, a:a + 32], tri[d], dta[:, b, 32 * d:32 * d + 32], start=True, stop=True)
                    m = mm(bank[7][:, 64 * b:64 * b + 64], ones, dta[:, b, :], start=True, stop=True)
                m.then_inc(dt_t, 1)

            def cb(g):
                pe.wait_ge(cv_out, 6 * g + 2)
                if g > 0:
                    pe.wait_ge(st_done, g * NST)
                for b in range(2):
                    m = mm(bank[4][:, b * P:(b + 1) * P], bT[:, b * P:(b + 1) * P], cT[:, b * P:(b + 1) * P],
                           start=True, stop=True)
                m.then_inc(cb_t, 1)

            def bc(g, q):
                d, b, hq = ssd_idx[q]
                n = g * NQ + q
                if q == 0:
                    pe.wait_ge(pr_copy, 10 * g + 8)
                if n >= 2:
                    pe.wait_ge(sg_ready, n - 1)
                for i in range(4):
                    a = d * N_SSM_HEADS + g * HPG + hq * 4 + i
                    m = mm(bank[2 + q % 2][:, i * P:(i + 1) * P], dta[:, b, a:a + 1].to_broadcast((P, P)), tri[d],
                           start=True, stop=True)
                m.then_inc(bc_t, 1)

            def state(g, k):
                n = g * NST + k
                pe.wait_ge(xe_ready, n + 1)
                if k == 0:
                    pe.wait_ge(cb_m, g + 1)
                if n >= 1:
                    pe.wait_ge(st_done, n)
                mm(bank[4][:, :], btok[:, ssd_states[k][2], :], xE, start=True, stop=True).then_inc(st_t, 1)

            def yy(g, q):
                d, b, hq = ssd_idx[q]
                n = g * NQ + q
                pe.wait_ge(mt_ready, n + 1)
                pe.wait_ge(ce_ready, n + 1)
                pe.wait_ge(xdt_ready, g * 4 + q // 2 + 1)
                pe.wait_ge(st_done, g * NST + (2, 3, 5, 6)[q // 2])
                if q == 0 and g > 0:
                    pe.wait_ge(gy_v, 4 * g)
                for i in range(4):
                    h = hq * 4 + i
                    r = (h % 2) * 64
                    a = (i // 2) * SEQ + b * P
                    o = bank[6 + hq][r:r + 64, a:a + P]
                    mm(o, xdt[:, h * 64:h * 64 + 64], mt[q % 2][:, i * P:(i + 1) * P],
                       start=(q < 2 and i < 2), stop=False, skip_group_check=True)
                    m = mm(o, hst[d][:, h * 64:h * 64 + 64], ce[q % 2][:, i * P:(i + 1) * P],
                           start=False, stop=(q >= NQ - 2 and i >= 2), skip_group_check=True)
                m.then_inc(yy_t, 1)

            decay_sums()
            for g in range(N_GROUPS):
                proj(g, 0)
                proj(g, 1)
                to_tok(g, 0)
                cb(g)
                proj(g, 2)
                to_tok(g, 1)
                to_tok(g, 2)
                proj(g, 3)
                to_tok(g, 3)
                to_tok(g, 4)
                proj(g, 4)
                if g == 0:
                    pe.wait_ge(dt_x, 1)
                bc(g, 0)
                state(g, 0)
                state(g, 1)
                bc(g, 1)
                yy(g, 0)
                bc(g, 2)
                yy(g, 1)
                state(g, 2)
                bc(g, 3)
                yy(g, 2)
                state(g, 3)
                state(g, 4)
                bc(g, 4)
                yy(g, 3)
                bc(g, 5)
                yy(g, 4)
                bc(g, 6)
                yy(g, 5)
                state(g, 5)
                bc(g, 7)
                yy(g, 6)
                yy(g, 7)
                pe.wait_ge(gq_done, g + 1)
                pe.wait_ge(tr_copy, 5 * (g + 1))
                for c in range(4):
                    m = mm(bank[5][:, 0:SEQ], ones, xsT[:, c, 0:SEQ], start=(c == 0), stop=(c == 3))
                m.then_inc(gn_t, 1)

            pe.wait_ge(gf_done, 4)
            for q in range(U_MIXOUT):
                for kh in range(2):
                    for h in range(2):
                        p = 2 * (S_SSMOUT + 2 * q + kh) + h
                        pe.wait_ge(lo_ready, p + 1)
                        for b in range(2):
                            if kh == 0 and h == 0 and q >= 2:
                                pe.wait_ge(lin_evac, LIN_SSMOUT + (q - 2) * 2 + b + 1)
                            for t in range(4):
                                k = 8 * kh + 4 * h + t
                                m = tok3(bank[(q % 2) * 2 + b][:, 0:UCOL], xh16[:, k, b * P:(b + 1) * P],
                                         xl16[:, k, b * P:(b + 1) * P], *wpart(p, t, UCOL),
                                         first=(k == 0), last=(k == 15))
                        m.then_inc(piece_used, 1)
            pe.wait_ge(gy_v, 16)
            for r in (4, 5):
                grow_(r)
            norm_t(12)
            norm_t(13)

            pe.wait_ge(xsplit_done, 14)
            pe.wait_ge(ld_rw, 16)
            for b in range(2):
                for k in range(KC):
                    for x in (xh, xl):
                        m = mm(bank[4][:, 8 * b:8 * b + 8], x[:, k, b * P:(b + 1) * P].bitcast(F32), rw[:, k, :],
                               start=(k == 0 and x is xh), stop=(k == KC - 1 and x is xl))
            m.then_inc(lg_t, 1)
            pe.wait_ge(rt_v, 1)
            mm(bank[5][:, 0:8], strict, mask[:, 0, :], start=True, stop=True)
            mm(bank[5][:, 8:16], strict, mask[:, 1, :], start=True, stop=False)
            mm(bank[5][:, 8:16], ones, mask[:, 0, :], start=False, stop=True)
            mm(bank[5][:, 16:24], ones, mask[:, 0, :], start=True, stop=False)
            mm(bank[5][:, 16:24], ones, mask[:, 1, :], start=False, stop=True).then_inc(rt_t, 1)

            hcur[0] = mhb

            def gather(it):
                pe.wait_ge(slot_ready, it + 1)
                for k in range(KC):
                    for b in range(2):
                        m = mm(bank[2 + k // 4][:, (k % 4) * P:(k % 4 + 1) * P], mxn[b][:, k * P:(k + 1) * P],
                               slot1[:, b, :], start=(b == 0), stop=(b == 1))
                m.then_inc(gat_t, 1)

            def expert(it, wrap):
                pe.wait_ge(gat_lo, it + 1)

                def at_step(j):
                    if j == 3:
                        pe.wait_ge(gs_ready, it + 1)
                        for b in range(2):
                            m = pe.transpose(bank[2][:, b * P:(b + 1) * P], slotg[:, b, :], ident)
                        m.then_inc(gs_t, 1)
                    if j == MOE_STEPS and wrap:
                        pe.wait_ge(gT_ready, it + 1)
                        gather(it + 1)

                swiglu(S_MOE, it, 1, MOE_STEPS, pos_moe, 0, C_MOE, T_MOE, 2 * it + Y_MOE, at_step)
                pe.wait_ge(gT_ready, it + 1)
                pe.wait_ge(y_evac, 2 * it + Y_MOE + 2)
                if wrap:
                    pe.wait_ge(gat_mod, it + 2)
                for b in range(2):
                    for half in range(2):
                        if b == 1:
                            pe.wait_ge(cmb_add, 4 * it + 1 + half + 1)
                        mm(bank[2 + half][:, :], gT[:, b, :], yexp[:, half * 512:(half + 1) * 512],
                           start=True, stop=True).then_inc(cmb_t, 1)

            gather(0)
            with pe.Fori(0, N_EXPERTS - 1) as e:
                expert(e, True)
            expert(N_EXPERTS - 1, False)
            pe.wait_ge(rt_done, RT_N)
            with pe.Fori(0, N_EXPERTS) as e:
                n = pe.value_load(cnt[0:1, bass.ds(e, 1)], min_val=0, max_val=2 * P)
                with pe.If(n > CAP):
                    gather(e + N_EXPERTS)
                    expert(e + N_EXPERTS, False)
                with pe.Else():
                    it = e + N_EXPERTS
                    for s, before, per in ((piece_used, P_MOE + it * MOE_PIECES, MOE_PIECES),
                                           (ht_t, T_MOE + it * MOE_STEPS, MOE_STEPS),
                                           (gat_t, it, 1), (gs_t, it, 1), (cmb_t, 4 * it, 4)):
                        pe.wait_ge(s, before)
                        pe.sem_inc(s, per)

        @block.scalar
        def _(act):
            A_ = act.activation
            spl = [0]

            def hi_piece(p):
                u = unit_of_split(p // 2)
                if p % 2 == 0:
                    act.wait_ge(raw_landed[u % RAW], landed[u])
                if p >= SPL:
                    act.wait_ge(piece_used, p - SPL + 1)
                A_(hi[:, p % SPL, :], raw[:, u % RAW, (p % 2) * PIECE:(p % 2 + 1) * PIECE], ACT.Copy
                   ).then_inc(hi_ready, 1)

            def hi_to(n):
                while spl[0] < min(n, P_MOE):
                    hi_piece(spl[0])
                    spl[0] += 1
                if n > P_MOE:
                    for i in range(spl[0] - P_MOE, n - P_MOE):
                        hi_moe(i, 0)
                        spl[0] += 1

            def hi_moe(i, it):
                if i % 2 == 0:
                    u = U_MOE + i // 2
                    act.wait_ge(raw_landed[u % RAW], landed_moe(i // 2, it))
                p = P_MOE + i
                act.wait_ge(piece_used, it * MOE_PIECES + p - SPL + 1)
                u = (U_MOE + i // 2) % RAW
                A_(hi[:, p % SPL, :], raw[:, u, (i % 2) * PIECE:(i % 2 + 1) * PIECE], ACT.Copy).then_inc(hi_ready, 1)

            steps = [0]

            def own(ins):
                ins.then_inc(astep, 1)
                steps[0] += 1
                act.wait_ge(astep, steps[0])

            act.wait_ge(vec_cols, 3)
            act.wait_ge(zeroed, 1)
            A_(sc[:, :, 0], cols[:, V_C:V_C + KC], ACT.Silu).then_inc(sc_ready, 1)
            A_(sc[:, :, 1], cols[:, V_CC:V_CC + KC], ACT.Silu).then_inc(sc_ready, 1)

            def ada_copy(a):
                act.wait_ge(ada_used, a + 1)
                if a > 0:
                    act.wait_ge(ada_col, a)
                A_(part, bank[6][:, 0:UCOL], ACT.Copy).then_inc(ada_part, 1)

            def norm_a(n):
                if n < 4:
                    act.wait_ge(*((ld_x, 16) if n < 2 else (ld_ctx, 16)))
                else:
                    act.wait_ge(po_done, n - 3)
                if n >= 2:
                    act.wait_ge(xt_done, n - 1)
                if n == 0:
                    act.wait_ge(eps_ready, 1)
                A_(xn_of(n), xblk[NORMS[n][2]], ACT.Square, accum_out=ss[:, n:n + 1]).then_inc(n_ss, 1)
                act.wait_ge(n_ss, n + 1)
                A_(rms[:, n:n + 1], ss[:, n:n + 1], ACT.Sqrt, scale=1.0 / D_MODEL, bias=epsc[:, 0:1]).then_inc(n_rms, 1)

            def norm_b(n):
                m, s, b = NORMS[n]
                act.wait_ge(xt_done, n + 1)
                act.wait_ge(mod_ready, 1 if m == 0 else 8)
                if n >= 1:
                    act.wait_ge(xsplit_done, n)
                a_, b_ = mod_cols(m, s)
                for k in range(KC):
                    i = A_(t32_of(n)[:, k * P:(k + 1) * P], bank[2 * (n % 2) + k // 4][:, (k % 4) * P:(k % 4 + 1) * P],
                           ACT.Identity, scale=a_[:, k:k + 1], bias=b_[:, k:k + 1])
                i.then_inc(xmod_done, 1)

            def post_a(n):
                A_(pjunk if n < 8 else mpjunk, post_src(n), ACT.Square, accum_out=ss[:, 14 + n:15 + n]).then_inc(po_ss, 1)
                act.wait_ge(po_ss, n + 1)
                A_(rms[:, 14 + n:15 + n], ss[:, 14 + n:15 + n], ACT.Sqrt, scale=1.0 / D_MODEL, bias=epsc[:, 0:1]
                   ).then_inc(po_rms, 1)

            for a in range(ADA_FIRST):
                ada_copy(a)
                if a in (4, 5):
                    norm_a(a - 4)
            norm_b(0)
            norm_a(2)
            norm_b(1)
            norm_a(3)
            norm_b(2)
            hi_to(2)
            norm_b(3)
            hi_to(SPL)

            def lin_out(s0, lin0, dst):
                for u in range(U_MIXIN if s0 == S_MIXIN else U_MIXOUT):
                    hi_to(2 * (s0 + u) + 1 + SPL)
                    hi_to(2 * (s0 + u) + 2 + SPL)
                    act.wait_ge(piece_used, 2 * (s0 + u) + 2)
                    for b in range(NBLK):
                        A_(dst[:, b, u * UCOL:(u + 1) * UCOL], bank[(u % 2) * 4 + b][:, 0:UCOL], ACT.Copy
                           ).then_inc(lin_evac, 1)

            def lin_in():
                for u in range(U_MIXIN):
                    hi_to(min(2 * u + 2 + SPL, 2 * S_MIXOUT))
                    act.wait_ge(piece_used, 2 * u + 2)
                    for b in range(NBLK):
                        A_(px[:, b, u * UCOL:(u + 1) * UCOL], bank[(u % 2) * 4 + b][:, 0:UCOL], ACT.Copy
                           ).then_inc(lin_evac, 1)

            lin_in()

            def step(it):
                return ITERS[it] if 0 <= it < len(ITERS) else (None, 0)

            for it in range(len(ITERS) + 2):
                if it == 8:
                    for b in range(NBLK):
                        act.wait_ge(qk_t, b + 1)
                        A_(qT[:, b, :, :], bank[4][:, :].rearrange("p (c n) -> p c n", c=4), ACT.Copy).then_inc(qk_tc, 1)
                        A_(kT[:, :, b * P:(b + 1) * P], v3(bank[5][:, 0:2 * P], 2), ACT.Copy).then_inc(qk_tc, 1)
                k, i = step(it)
                if k == "dft":
                    act.wait_ge(dft_t1, i + 1)
                    if i >= 2:
                        act.wait_ge(dft_out, i - 1)
                    A_(t1s[i % 2], bank[i % 2][:, :], ACT.Copy).then_inc(dft_t1s, 1)
                    if i % 2 == 1:
                        b = i // 2
                        act.wait_ge(qk_ss, b + 1)
                        A_(qrms[:, b, :], qss[:, b, :], ACT.Sqrt, scale=1.0 / HEAD_DIM, bias=epsc[:, 0:1]
                           ).then_inc(qk_rms, 1)
                if k == "att":
                    nk = at_info(i)[3][1]
                    act.wait_ge(at_mx, i + 1)
                    if i >= 2:
                        act.wait_ge(at_t, i - 1)
                    A_(prob[i % 2][:, 0:nk * P], bank[i % 2][:, 0:nk * P], ACT.Exp, bias=nmx[:, i:i + 1], scale=AT_SCALE,
                       accum_out=rsum[:, i:i + 1]).then_inc(at_exp, 1)
                if it < len(ITERS):
                    ada_copy(ADA_FIRST + it)
                k, i = step(it - 1)
                if k == "dft":
                    s, g = divmod(i, 4)
                    act.wait_ge(dft_out, i + 1)
                    A_(xh[:, g, s * SEQ:(s + 1) * SEQ], bank[2 + i % 2][:, 0:SEQ], ACT.Copy).then_inc(dft_hi, 1)
                if k == "att":
                    nk = at_info(i)[3][1]
                    act.wait_ge(at_t, i + 1)
                    if i >= 2:
                        act.wait_ge(at_pv, i - 1)
                    A_(pts[i % 2][:, 0:nk * P], bank[2 + i % 2][:, 0:nk * P], ACT.Copy).then_inc(at_pt, 1)
                k, i = step(it - 2)
                if k == "att" and i % 8 == 7:
                    b = i // 8
                    act.wait_ge(at_pv, i + 1)
                    A_(xh[:, 4:8, b * P:(b + 1) * P], v3(bank[4 + b % 2][:, :], 4), ACT.Copy).then_inc(at_oh, 1)
            hi_to(2 * S_MIXOUT + SPL)
            lin_out(S_MIXOUT, LIN_MIXOUT, y)

            def grow_out(r):
                act.wait_ge(grow_t, r + 1)
                for k in range(2):
                    i = A_(grow_tile(r)[:, k * 512:(k + 1) * 512], bank[4 + 2 * (r % 2) + k][:, :], ACT.Copy)
                i.then_inc(grow_ready, 1)

            def residuals(n0):
                post_a(n0)
                post_a(n0 + 1)
                norm_a(n0 + 4)
                post_a(n0 + 2)
                norm_a(n0 + 5)
                norm_b(n0 + 4)
                post_a(n0 + 3)
                norm_a(n0 + 6)
                norm_b(n0 + 5)
                norm_a(n0 + 7)
                norm_b(n0 + 6)
                norm_b(n0 + 7)

            for r in range(4):
                grow_out(r)
            residuals(0)

            def swiglu(s0, it, nblk, n, pos, c0, t0, sgt, look, at_step=None):
                pd, cd, td = it * MOE_PIECES, it * MOE_STEPS, it * MOE_STEPS
                for j in range(n + 2):
                    if j < n:
                        for kind in ("g", "u"):
                            for h in range(2):
                                look(2 * pos[(kind, j)] + h)
                        act.wait_ge(piece_used, pd + 2 * (s0 + pos[("u", j)]) + 2)
                        for b in range(nblk):
                            c = c0 + j * nblk + b
                            if c >= 2:
                                act.wait_ge(h_done, cd + c - 1)
                            A_(sgt[c % 2], bank[4 + c % 2][:, 0:UCOL], ACT.Silu).then_inc(sil_done, 1)
                    if 1 <= j <= n:
                        tj = t0 + j - 1
                        act.wait_ge(ht_t, td + tj + 1)
                        if j >= 3:
                            act.wait_ge(piece_used, pd + 2 * (s0 + pos[("d", j - 3)]) + 2)
                        A_(hth[:, tj % 2, 0:2 * nblk * P], bank[6 + tj % 2][:, 0:2 * nblk * P], ACT.Copy
                           ).then_inc(ht_hi, 1)
                    if at_step:
                        at_step(j)
                    if j >= 2:
                        for h in range(2):
                            look(2 * pos[("d", j - 2)] + h)

            for ps in range(2):
                s0 = S_FFN + ps * FFN_N
                swiglu(s0, 0, 2, FFN_STEPS, pos_ffn, ps * 2 * FFN_STEPS, ps * FFN_STEPS, sg,
                       lambda i, s0=s0: hi_to(2 * s0 + i + 1 + SPL))
                act.wait_ge(piece_used, 2 * (s0 + FFN_N))
                for half in range(2):
                    A_(y[:, 2 * ps, half * 512:(half + 1) * 512], bank[half][:, :], ACT.Copy).then_inc(y_evac, 1)
            act.wait_ge(y_evac, 8)
            residuals(4)

            for h in range(2):
                hi_to(2 * S_DT + h + 1 + SPL)
            act.wait_ge(ld_ssm, 48)
            A_(arow, arow, ACT.Exp).then_inc(dt_e, 1)
            act.wait_ge(dt_v, 5)
            A_(st2, st2, ACT.Exp, scale=-1.0).then_inc(dt_e, 1)

            def group(g):
                def unit(ui):
                    for h in range(2):
                        hi_to(2 * (S_GRP + g * GROUP_UNITS + ui) + h + 1 + SPL)
                    act.wait_ge(piece_used, 2 * (S_GRP + g * GROUP_UNITS + ui) + 2)

                def conv_in(i):
                    n, ui = 6 * g + i, i // 2
                    if n == 0:
                        act.wait_ge(zeroed, 3)
                    if n >= 2:
                        act.wait_ge(cv_acc, n - 1)
                    ns = 1 if i == 1 else 2
                    A_(cpad[n % 2][:, 0:ns, 2:2 + SEQ], v3(bank[2 * (ui % 2) + i % 2][:, 0:ns * SEQ], ns), ACT.Copy
                       ).then_inc(pr_copy, 1)

                def conv_out(i):
                    n = 6 * g + i
                    act.wait_ge(cv_acc, n + 1)
                    dst = (bT, cT, xsT[:, 0, :], xsT[:, 1, :], xsT[:, 2, :], xsT[:, 3, :])[i]
                    ch = (16 + g, 20 + g, 4 * g, 4 * g + 1, 4 * g + 2, 4 * g + 3)[i]
                    w = SEQ if i == 1 else 512
                    A_(dst, cacc[n % 2][:, 0:w], ACT.Silu, bias=cols[:, V_CONVB + ch:V_CONVB + ch + 1]
                       ).then_inc(cv_out, 1)

                def tok(i):
                    act.wait_ge(tr_t, 5 * g + i + 1)
                    src = v3(bank[5][:, :], NBLK)
                    dst = btok[:, :, :] if i == 0 else xtok[:, :, (i - 1) * P:i * P]
                    A_(dst, src, ACT.Copy).then_inc(tr_copy, 1)

                def zs(ui):
                    for c in range(2):
                        k = 4 * g + 2 * (ui - 3) + c
                        A_(gy[:, k, :], bank[2 * (ui % 2) + c][:, 0:SEQ], ACT.Silu).then_inc(pr_copy, 1)

                unit(0)
                conv_in(0)
                conv_in(1)
                conv_out(0)
                unit(1)
                conv_in(2)
                conv_in(3)
                conv_out(1)
                tok(0)
                conv_out(2)
                unit(2)
                conv_in(4)
                conv_out(3)
                conv_in(5)
                tok(1)
                tok(2)
                conv_out(4)
                unit(3)
                zs(3)
                conv_out(5)
                tok(3)
                tok(4)
                unit(4)
                zs(4)
                if g == 0:
                    act.wait_ge(dt_v, 7)
                    A_(cdec[:, :, :], v3(bank[7][:, 0:256], 4), ACT.Exp).then_inc(dt_e, 1)
                    A_(eE[:, :, :], v3(st1, 4), ACT.Exp).then_inc(dt_e, 1)

                def ce_(q):
                    n = g * NQ + q
                    act.wait_ge(bc_t, n + 1)
                    if n >= 2:
                        act.wait_ge(yy_t, n - 1)
                    A_(ce[q % 2], bank[2 + q % 2][:, :], ACT.Exp).then_inc(ce_exp, 1)

                def m_(q):
                    act.wait_ge(sg_ready, g * NQ + q + 1)
                    A_(mt[q % 2], mt[q % 2], ACT.Exp).then_inc(mt_exp, 1)

                for q in range(NQ + 1):
                    if q < NQ:
                        ce_(q)
                    if q >= 1:
                        m_(q - 1)
                act.wait_ge(gy_done, g + 1)
                A_(xsT[:, :, 0:SEQ], gy[:, 4 * g:4 * g + 4, :], ACT.Square).then_inc(gq_done, 1)
                act.wait_ge(gn_t, g + 1)
                A_(ssg[g], bank[5][:, 0:SEQ], ACT.Copy).then_inc(gn_copy, 1)

            for g in range(N_GROUPS):
                group(g)
            act.wait_ge(gn_copy, 4)
            for g in range(N_GROUPS):
                A_(ssg[g], ssg[g], ACT.Sqrt, scale=1.0 / 512, bias=epsc[:, 0:1]).then_inc(gn_rms, 1)
            for g in range(N_GROUPS):
                act.wait_ge(gf_v, 4 * (g + 1))
                A_(xh16[:, 4 * g:4 * g + 4, :], gy[:, 4 * g:4 * g + 4, :], ACT.Copy).then_inc(gf_hi, 1)
            for q in range(U_MIXOUT):
                for i in range(4):
                    hi_to(2 * S_SSMOUT + 4 * q + i + 1 + SPL)
                act.wait_ge(piece_used, 2 * S_SSMOUT + 4 * q + 4)
                for b in range(2):
                    A_(yout[:, b, q * UCOL:(q + 1) * UCOL], bank[(q % 2) * 2 + b][:, 0:UCOL], ACT.Copy
                       ).then_inc(lin_evac, 1)
            act.wait_ge(lin_evac, LIN_SSMOUT + 8)
            for r in (4, 5):
                grow_out(r)
            post_a(8)
            post_a(9)
            norm_a(12)
            norm_a(13)
            norm_b(12)
            norm_b(13)
            act.wait_ge(rt_v, 2)
            A_(ge, gd, ACT.Exp).then_inc(rt_e, 1)

            def gather_mod(it):
                act.wait_ge(gat_t, it + 1)
                a_, b_ = mod_cols(3, 0)
                for k in range(KC):
                    i = A_(mt32[:, k * P:(k + 1) * P], bank[2 + k // 4][:, (k % 4) * P:(k % 4 + 1) * P],
                           ACT.Identity, scale=a_[:, k:k + 1], bias=b_[:, k:k + 1])
                i.then_inc(gat_mod, 1)

            def expert(it, wrap):
                def look(i):
                    if i + SPL < MOE_PIECES or wrap:
                        hi_moe(i + SPL, it)

                def at_step(j):
                    if j == 3:
                        act.wait_ge(gs_t, it + 1)
                        A_(gT[:, :, :], v3(bank[2][:, 0:2 * P], 2), ACT.Copy).then_inc(gT_ready, 1)
                    if j == MOE_STEPS and wrap:
                        gather_mod(it + 1)

                swiglu(S_MOE, it, 1, MOE_STEPS, pos_moe, C_MOE, T_MOE, msg, look, at_step)
                act.wait_ge(piece_used, P_MOE + (it + 1) * MOE_PIECES)
                A_(yexp[:, 0:512], bank[0][:, :], ACT.Copy).then_inc(y_evac, 1)

            act.wait_ge(xsplit_done, 14)
            gather_mod(0)
            with act.Fori(0, N_EXPERTS - 1) as e:
                expert(e, True)
            expert(N_EXPERTS - 1, False)
            with act.Fori(0, N_EXPERTS) as e:
                n = act.value_load(cnt[0:1, bass.ds(e, 1)], min_val=0, max_val=2 * P)
                with act.If(n > CAP):
                    for i in range(SPL):
                        hi_moe(i, e + N_EXPERTS)
                    gather_mod(e + N_EXPERTS)
                    expert(e + N_EXPERTS, False)
                with act.Else():
                    it = e + N_EXPERTS
                    for s, before, per in ((hi_ready, P_MOE + it * MOE_PIECES, MOE_PIECES),
                                           (sil_done, C_MOE + it * MOE_STEPS, MOE_STEPS),
                                           (ht_hi, T_MOE + it * MOE_STEPS, MOE_STEPS),
                                           (gat_mod, it, 1), (gT_ready, it, 1), (y_evac, Y_MOE + 2 * it, 1)):
                        act.wait_ge(s, before)
                        act.sem_inc(s, per)
            act.wait_ge(cmb_add, 4 * 2 * N_EXPERTS + 1)
            post_a(10)
            post_a(11)

        @block.vector
        def _(dve):
            TT, TS, STT = dve.tensor_tensor, dve.tensor_scalar, dve.scalar_tensor_tensor
            spl = [0]

            def lo_sub(p, u, h):
                TT(lo[:, p % SPL, :], raw[:, u, h * PIECE:(h + 1) * PIECE], hi[:, p % SPL, :].bitcast(F32), ALU.subtract
                   ).then_inc(lo_ready, 1)

            def lo_to(n):
                while spl[0] < n:
                    p = spl[0]
                    if p < P_MOE:
                        dve.wait_ge(hi_ready, p + 1)
                        lo_sub(p, unit_of_split(p // 2) % RAW, p % 2)
                    else:
                        lo_moe(p - P_MOE, 0)
                    spl[0] += 1

            def lo_moe(i, it):
                dve.wait_ge(hi_ready, it * MOE_PIECES + P_MOE + i + 1)
                lo_sub(P_MOE + i, (U_MOE + i // 2) % RAW, i % 2)

            steps = [0]

            def own(ins):
                ins.then_inc(vstep, 1)
                steps[0] += 1
                dve.wait_ge(vstep, steps[0])

            for i, (n, c) in enumerate(((96, V_NORM), (120, V_ADAB), (120, V_CONVW))):
                dve.wait_ge(vec_t, i + 1)
                dve.tensor_copy(cols[:, c:c + n], bank[5 + i][:, 0:n]).then_inc(vec_cols, 1)

            def ada_take(a):
                l, c = divmod(a, N_ADA // 2)
                dve.wait_ge(ada_col, a + 1)
                TT(ada[:, l, 2 * c:2 * c + 2, :], v3(bank[7][:, 0:4], 2),
                   cols[:, V_ADAB + l * 48 + 2 * c:V_ADAB + l * 48 + 2 * c + 2].unsqueeze(2).to_broadcast((P, 2, 2)),
                   ALU.add).then_inc(ada_done, 1)

            def norm_w(l, i):
                a = V_NORM + (l * 4 + i) * KC
                return cols[:, a:a + KC].unsqueeze(2).to_broadcast((P, KC, 2))

            def scale_cols(m):
                l, w = divmod(m, 2)
                STT(moda[:, m, :, :], ada[:, l, 24 * w + KC:24 * w + 2 * KC, :], 1.0, norm_w(l, 2 * w),
                    ALU.add, ALU.mult).then_inc(mod_ready, 1)

            def gate_cols(m):
                l, w = divmod(m, 2)
                TT(gatec[:, m, :, :], ada[:, l, 24 * w + 2 * KC:24 * w + 3 * KC, :], norm_w(l, 2 * w + 1), ALU.mult
                   ).then_inc(mod_ready, 1)

            def norm_a(n):
                dve.wait_ge(n_rms, n + 1)
                dve.reciprocal(rstd[:, n:n + 1], rms[:, n:n + 1]).then_inc(n_rstd, 1)
                dve.wait_ge(n_rstd, n + 1)
                TS(xn_of(n), xblk[NORMS[n][2]], rstd[:, n:n + 1], None, ALU.mult).then_inc(xn_ready, 1)

            def norm_b(n):
                b = NORMS[n][2]
                dve.wait_ge(xmod_done, n + 1)
                dve.tensor_copy(xh[:, :, b * P:(b + 1) * P], v3(t32_of(n), KC)).then_inc(xsplit_hi, 1)
                dve.wait_ge(xsplit_hi, n + 1)
                TT(xl[:, :, b * P:(b + 1) * P], v3(t32_of(n), KC), xh[:, :, b * P:(b + 1) * P].bitcast(F32), ALU.subtract
                   ).then_inc(xsplit_done, 1)

            def post(n):
                m, s, b = POSTS[n]
                t = ptmp if n < 8 else mptmp
                dve.wait_ge(po_rms, n + 1)
                dve.reciprocal(rstd[:, 14 + n:15 + n], rms[:, 14 + n:15 + n]).then_inc(po_rstd, 1)
                dve.wait_ge(po_rstd, n + 1)
                dve.wait_ge(grow_ready, grow_of(n) + 1)
                STT(t, post_src(n), rstd[:, 14 + n:15 + n], grow_tile(grow_of(n)), ALU.mult, ALU.mult
                    ).then_inc(po_t, 1)
                dve.wait_ge(po_t, n + 1)
                TT(xblk[b], xblk[b], t, ALU.add).then_inc(po_done, 1)

            for a in range(ADA_FIRST):
                ada_take(a)
                if a in (4, 5):
                    norm_a(a - 4)
            dve.wait_ge(ada_done, ADA_FIRST)
            scale_cols(0)
            norm_b(0)
            norm_a(2)
            norm_b(1)
            norm_a(3)
            norm_b(2)
            lo_to(2)
            norm_b(3)
            lo_to(SPL)
            for u in range(U_MIXIN):
                lo_to(min(2 * u + 2 + SPL, 2 * S_MIXOUT))

            dve.wait_ge(lin_evac, LIN_MIXOUT)
            dve.wait_ge(ld_qkw, 32)
            dve.wait_ge(ld_first, 16)

            def heads(b, n0=0, n1=10):
                a = F_WIDTH
                return px[:, b, a + n0 * 64:a + n1 * 64].rearrange("p (h n) -> p h n", n=64)

            def qk_1(b):
                own(TT(qsq, px[:, b, F_WIDTH:F_WIDTH + 640], px[:, b, F_WIDTH:F_WIDTH + 640], ALU.mult))
                dve.tensor_reduce(qss[:, b, :], qsq.rearrange("p (h n) -> p h n", n=64), AX.X, ALU.add
                                  ).then_inc(qk_ss, 1)

            def qk_2(b):
                dve.wait_ge(qk_rms, b + 1)
                own(dve.reciprocal(qrs[:, b, :], qrms[:, b, :]))
                own(TT(heads(b), heads(b), qrs[:, b, :].unsqueeze(2).to_broadcast((P, 10, 64)), ALU.mult))
                TT(heads(b, 0, 8), heads(b, 0, 8), qkw[:, 0:1, :].to_broadcast((P, 8, 64)), ALU.mult)
                own(TT(heads(b, 8, 10), heads(b, 8, 10), qkw[:, 1:2, :].to_broadcast((P, 2, 64)), ALU.mult))

            def qk_3(b):
                if b in LAT:
                    x = px[:, b, F_WIDTH:F_WIDTH + 640].rearrange("p (h n two) -> p h n two", n=32, two=2)
                    x1, x2 = x[:, :, :, 0], x[:, :, :, 1]
                    c, s = (rope[:, i, b, :].unsqueeze(1).to_broadcast((P, 10, 32)) for i in range(2))
                    r = [rtmp[:, i * 320:(i + 1) * 320].rearrange("p (h n) -> p h n", n=32) for i in range(4)]
                    TT(r[0], x1, c, ALU.mult)
                    TT(r[1], x2, s, ALU.mult)
                    TT(r[2], x1, s, ALU.mult)
                    own(TT(r[3], x2, c, ALU.mult))
                    TT(x1, r[0], r[1], ALU.subtract)
                    own(TT(x2, r[2], r[3], ALU.add))

            def qk_4(b):
                if b >= 1:
                    dve.wait_ge(qk_t, b)
                a = F_WIDTH + Q_WIDTH
                dve.tensor_copy(kdup.rearrange("p (v two n) -> p v two n", v=2, two=2),
                                px[:, b, a:a + 2 * 64].rearrange("p (v n) -> p v n", v=2).unsqueeze(2)
                                .to_broadcast((P, 2, 2, 64))).then_inc(qk_ready, 1)

            def step(it):
                return ITERS[it] if 0 <= it < len(ITERS) else (None, 0)

            for it in range(len(ITERS) + 2):
                k, i = step(it)
                if k == "dft":
                    if i % 2 == 0:
                        qk_1(i // 2)
                    else:
                        qk_2(i // 2)
                        qk_3(i // 2)
                if it == 8:
                    for b in range(NBLK):
                        qk_4(b)
                k1, i1 = step(it - 1)
                if k1 == "att":
                    dve.wait_ge(at_exp, i1 + 1)
                    nk = at_info(i1)[3][1]
                    dve.reciprocal(rinv[:, i1:i1 + 1], rsum[:, i1:i1 + 1]).then_inc(at_r, 1)
                    dve.wait_ge(at_r, i1 + 1)
                    TS(prob[i1 % 2][:, 0:nk * P], prob[i1 % 2][:, 0:nk * P], rinv[:, i1:i1 + 1], None, ALU.mult
                       ).then_inc(at_nrm, 1)
                if k == "att":
                    nk = at_info(i)[3][1]
                    dve.wait_ge(at_s, i + 1)
                    dve.tensor_reduce(mx[:, i:i + 1], bank[i % 2][:, 0:nk * P], AX.X, ALU.max).then_inc(at_m, 1)
                    dve.wait_ge(at_m, i + 1)
                    TS(nmx[:, i:i + 1], mx[:, i:i + 1], -AT_SCALE, None, ALU.mult).then_inc(at_mx, 1)
                if k1 == "dft":
                    s, g = divmod(i1, 4)
                    dve.wait_ge(dft_hi, i1 + 1)
                    TT(xl[:, g, s * SEQ:(s + 1) * SEQ], bank[2 + i1 % 2][:, 0:SEQ],
                       xh[:, g, s * SEQ:(s + 1) * SEQ].bitcast(F32), ALU.subtract).then_inc(dft_lo, 1)
                if 1 <= it <= len(ITERS):
                    ada_take(ADA_FIRST + it - 1)
                k, i = step(it - 2)
                if k == "att" and i % 8 == 7:
                    b = i // 8
                    dve.wait_ge(at_oh, b + 1)
                    TT(xl[:, 4:8, b * P:(b + 1) * P], v3(bank[4 + b % 2][:, :], 4),
                       xh[:, 4:8, b * P:(b + 1) * P].bitcast(F32), ALU.subtract).then_inc(at_ol, 1)
            lo_to(2 * S_MIXOUT + SPL)
            dve.wait_ge(ada_done, N_ADA)
            for m in range(1, 4):
                scale_cols(m)
            for m in range(4):
                gate_cols(m)
            for u in range(U_MIXOUT):
                lo_to(2 * (S_MIXOUT + u) + 2 + SPL)

            def residuals(n0):
                post(n0)
                post(n0 + 1)
                norm_a(n0 + 4)
                post(n0 + 2)
                norm_a(n0 + 5)
                norm_b(n0 + 4)
                post(n0 + 3)
                norm_a(n0 + 6)
                norm_b(n0 + 5)
                norm_a(n0 + 7)
                norm_b(n0 + 6)
                norm_b(n0 + 7)

            residuals(0)

            def swiglu(s0, it, nblk, n, pos, c0, t0, sgt, ht, look, at_step=None):
                cd, td = it * MOE_STEPS, it * MOE_STEPS
                for j in range(n + 2):
                    if j < n:
                        for kind in ("g", "u"):
                            for h in range(2):
                                look(2 * pos[(kind, j)] + h)
                        for b in range(nblk):
                            c = c0 + j * nblk + b
                            dve.wait_ge(sil_done, cd + c + 1)
                            free = t0 + j - (2 // nblk) + 1
                            if free >= 1:
                                dve.wait_ge(ht_t, td + free)
                            TT(ht[c % 2], sgt[c % 2], bank[4 + c % 2][:, UCOL:2 * UCOL], ALU.mult).then_inc(h_done, 1)
                    if 1 <= j <= n:
                        tj = t0 + j - 1
                        dve.wait_ge(ht_hi, td + tj + 1)
                        w = 2 * nblk * P
                        TT(htl[:, tj % 2, 0:w], bank[6 + tj % 2][:, 0:w], hth[:, tj % 2, 0:w].bitcast(F32), ALU.subtract
                           ).then_inc(ht_lo, 1)
                    if at_step:
                        at_step(j)
                    if j >= 2:
                        for h in range(2):
                            look(2 * pos[("d", j - 2)] + h)

            for ps in range(2):
                s0 = S_FFN + ps * FFN_N
                swiglu(s0, 0, 2, FFN_STEPS, pos_ffn, ps * 2 * FFN_STEPS, ps * FFN_STEPS, sg, hb,
                       lambda i, s0=s0: lo_to(2 * s0 + i + 1 + SPL))
                dve.wait_ge(piece_used, 2 * (s0 + FFN_N))
                for half in range(2):
                    dve.tensor_copy(y[:, 2 * ps + 1, half * 512:(half + 1) * 512], bank[2 + half][:, :]).then_inc(y_evac, 1)
            residuals(4)

            for h in range(2):
                lo_to(2 * S_DT + h + 1 + SPL)
            dve.wait_ge(ld_ssm, 48)
            dve.wait_ge(piece_used, 2 * S_DT + 2)
            for b in range(NBLK):
                TT(st1[:, 64 * b:64 * b + 64], bank[b][:, 0:64], dbias, ALU.add).then_inc(dt_v, 1)
            dve.wait_ge(dt_v, 4)
            STT(st2, st1, -1.0, st1, ALU.mult, ALU.max).then_inc(dt_v, 1)
            dve.tensor_copy(dcol[0:64, :], drow[0:64, 0:32:2])
            own(dve.tensor_copy(dcol[64:128, :], drow[64:128, 1:32:2]))
            dve.wait_ge(dt_e, 2)
            own(TS(st3, st2, 2.0, None, ALU.add))
            own(dve.reciprocal(st3, st3))
            own(TT(st2, st2, st3, ALU.mult))
            own(TT(st3, st2, st2, ALU.mult))
            p_ = acum[:, :, :].rearrange("p b n -> p (b n)")
            own(TS(p_, st3, 1.0 / 17, None, ALU.mult))
            for k in range(7, 0, -1):
                own(STT(p_, p_, 1.0 / (2 * k + 1), st3, ALU.add, ALU.mult))
            own(STT(p_, p_, 1.0, st2, ALU.add, ALU.mult))
            own(TS(st1, st1, 0.0, None, ALU.max))
            d_ = dt_[:, :, :].rearrange("p b n -> p (b n)")
            own(STT(d_, p_, 2.0, st1, ALU.mult, ALU.add))
            STT(dta[:, :, :], dt_[:, :, :], -1.0, arow.unsqueeze(1).to_broadcast((P, NBLK, 64)), ALU.mult, ALU.mult
                ).then_inc(dt_a, 1)
            dve.wait_ge(dt_t, 1)
            dve.tensor_copy(p_, bank[6][:, 0:256]).then_inc(dt_v, 1)
            dve.wait_ge(dt_v, 6)
            TT(st1, bank[7][:, 0:256], p_, ALU.subtract).then_inc(dt_v, 1)

            def group(g):
                def look(ui):
                    for h in range(2):
                        lo_to(2 * (S_GRP + g * GROUP_UNITS + ui) + h + 1 + SPL)

                def conv(i):
                    n = 6 * g + i
                    ch = (16 + g, 20 + g, 4 * g, 4 * g + 1, 4 * g + 2, 4 * g + 3)[i]
                    ns = 1 if i == 1 else 2
                    dve.wait_ge(pr_copy, 10 * g + i + 1)
                    if n >= 2:
                        dve.wait_ge(cv_out, n - 1)
                    o = v3(cacc[n % 2][:, 0:ns * SEQ], ns)

                    def tap(t):
                        a = V_CONVW + t * 24 + ch
                        return cpad[n % 2][:, 0:ns, t:t + SEQ], cols[:, a:a + 1]

                    x, w = tap(0)
                    TS(o, x, w, None, ALU.mult).then_inc(cv_v, 1)
                    for t in range(1, D_CONV):
                        dve.wait_ge(cv_v, 4 * n + t)
                        x, w = tap(t)
                        STT(o, x, w, o, ALU.mult, ALU.add).then_inc(cv_v if t < D_CONV - 1 else cv_acc, 1)

                look(0)
                conv(0)
                conv(1)
                look(1)
                conv(2)
                conv(3)
                dve.wait_ge(cb_t, g + 1)
                for d in range(2):
                    i = TT(cbm[:, d, :, :], v3(bank[4][:, 0:2 * P], 2), tri[d].unsqueeze(1).to_broadcast((P, 2, P)),
                           ALU.mult)
                i.then_inc(cb_m, 1)
                look(2)
                conv(4)
                conv(5)
                look(3)
                look(4)
                if g == 0:
                    dve.wait_ge(dt_e, 4)
                    TT(eE[:, :, :], eE[:, :, :], dt_[:, :, :], ALU.mult).then_inc(dt_x, 1)

                def seg(q):
                    d, b, hq = ssd_idx[q]
                    n = g * NQ + q
                    dve.wait_ge(ce_exp, n + 1)
                    if n >= 2:
                        dve.wait_ge(yy_t, n - 1)
                    for i in range(4):
                        a = d * N_SSM_HEADS + g * HPG + hq * 4 + i
                        m = TS(mt[q % 2][:, i * P:(i + 1) * P], bank[2 + q % 2][:, i * P:(i + 1) * P],
                               acum[:, b, a:a + 1], 0.0, ALU.subtract, ALU.min)
                    m.then_inc(sg_ready, 1)

                def mul(q):
                    d, b, _ = ssd_idx[q]
                    dve.wait_ge(mt_exp, g * NQ + q + 1)
                    TT(v3(mt[q % 2], 4), v3(mt[q % 2], 4), cbm[:, d, b:b + 1, :].to_broadcast((P, 4, P)), ALU.mult
                       ).then_inc(mt_ready, 1)

                def state(k):
                    d, kk, b = ssd_states[k]
                    n = g * NST + k
                    dve.wait_ge(st_t, n + 1)
                    if kk == 0:
                        dve.tensor_copy(hst[d], bank[4][:, :]).then_inc(st_done, 1)
                        return
                    if kk == 2:
                        dve.wait_ge(yy_t, g * NQ + (2 if d == 0 else 6))
                    dve.wait_ge(st_done, n)
                    a = d * N_SSM_HEADS + g * HPG
                    hv = hst[d].rearrange("p (h q) -> p h q", h=HPG)
                    own(TT(hv, hv, cdec[:, b, a:a + HPG].unsqueeze(2).to_broadcast((P, HPG, 64)), ALU.mult))
                    TT(hst[d], hst[d], bank[4][:, :], ALU.add).then_inc(st_done, 1)

                seg(0)
                state(0)
                state(1)
                seg(1)
                mul(0)
                seg(2)
                mul(1)
                state(2)
                seg(3)
                mul(2)
                state(3)
                state(4)
                seg(4)
                mul(3)
                seg(5)
                mul(4)
                seg(6)
                mul(5)
                state(5)
                seg(7)
                mul(6)
                mul(7)
                dve.wait_ge(yy_t, (g + 1) * NQ)
                for c in range(4):
                    STT(xsT[:, c, 0:SEQ], xsT[:, c, 0:SEQ], dcol[:, 4 * g + c:4 * g + c + 1],
                        bank[6 + c // 2][:, (c % 2) * SEQ:(c % 2 + 1) * SEQ], ALU.mult, ALU.add).then_inc(gy_v, 1)
                dve.wait_ge(gy_v, 4 * (g + 1))
                TT(gy[:, 4 * g:4 * g + 4, :], gy[:, 4 * g:4 * g + 4, :], xsT[:, :, 0:SEQ], ALU.mult).then_inc(gy_done, 1)

            for g in range(N_GROUPS):
                group(g)
            for g in range(N_GROUPS):
                dve.wait_ge(gn_rms, g + 1)
                dve.reciprocal(ssg[g], ssg[g]).then_inc(gn_rstd, 1)
                dve.wait_ge(gn_rstd, g + 1)
                for c in range(4):
                    k = 4 * g + c
                    STT(gy[:, k, :], gy[:, k, :], cols[:, V_SNORM + k:V_SNORM + k + 1], ssg[g], ALU.mult, ALU.mult
                        ).then_inc(gf_v, 1)
                dve.wait_ge(gf_hi, g + 1)
                TT(xl16[:, 4 * g:4 * g + 4, :], gy[:, 4 * g:4 * g + 4, :], xh16[:, 4 * g:4 * g + 4, :].bitcast(F32),
                   ALU.subtract).then_inc(gf_done, 1)
            for i in range(16):
                lo_to(2 * S_SSMOUT + i + 1 + SPL)
            post(8)
            post(9)
            norm_a(12)
            norm_a(13)
            norm_b(12)
            norm_b(13)

            dve.memset(yout[:, :, :], 0.0).then_inc(cmb_add, 1)
            dve.wait_ge(lg_t, 1)
            own(dve.tensor_copy(lg[:, :, :], v3(bank[4][:, 0:16], 2)))
            for b in range(2):
                own(dve.max(top[:, b, :], lg[:, b, :]))
                own(dve.max_index(idx8[:, b, :], top[:, b, :], lg[:, b, :]))
            own(dve.tensor_copy(idxf[:, :, :], idx8[:, :, :]))
            for b in range(2):
                TS(sel1[:, b, :], iota8, idxf[:, b, 0:1], None, ALU.is_equal)
                own(TS(sel2[:, b, :], iota8, idxf[:, b, 1:2], None, ALU.is_equal))
            TT(mask[:, :, :], sel1[:, :, :], sel2[:, :, :], ALU.add).then_inc(rt_v, 1)
            TT(gd, top[:, :, 1], top[:, :, 0], ALU.subtract).then_inc(rt_v, 1)
            dve.wait_ge(rt_e, 1)
            own(TS(gs, ge, 1.0, None, ALU.add))
            own(dve.reciprocal(g1, gs))
            own(TT(g2, ge, g1, ALU.mult))
            for b in range(2):
                own(TS(sel1[:, b, :], sel1[:, b, :], g1[:, b:b + 1], None, ALU.mult))
                own(STT(comb[:, b, :], sel2[:, b, :], g2[:, b:b + 1], sel1[:, b, :], ALU.mult, ALU.add))
            dve.wait_ge(rt_t, 1)
            own(STT(posm[:, :, :], mask[:, :, :], -1000.0, v3(bank[5][:, 0:16], 2), ALU.mult, ALU.add))
            own(TS(posm[:, :, :], posm[:, :, :], 1000.0, None, ALU.add))
            own(TS(posm2[:, :, :], posm[:, :, :], -float(CAP), None, ALU.add))
            dve.tensor_copy(cnt[:, :], bank[5][:, 16:24]).then_inc(rt_done, 1)

            def slots(e, it, pm):
                for b in range(2):
                    i = TS(slot1[:, b, :], iota, pm[:, b, bass.ds(e, 1)], None, ALU.is_equal)
                i.then_inc(slot_ready, 1)

            def gather_split(it):
                dve.wait_ge(gat_mod, it + 1)
                dve.tensor_copy(xh[:, :, 0:P], v3(mt32, KC)).then_inc(gat_hi, 1)
                dve.wait_ge(gat_hi, it + 1)
                TT(xl[:, :, 0:P], v3(mt32, KC), xh[:, :, 0:P].bitcast(F32), ALU.subtract).then_inc(gat_lo, 1)

            def expert(e, it, wrap):
                def look(i):
                    if i + SPL < MOE_PIECES or wrap:
                        lo_moe(i + SPL, it)

                def at_step(j):
                    if j == 1:
                        dve.wait_ge(slot_ready, it + 1)
                        for b in range(2):
                            i = TS(slotg[:, b, :], slot1[:, b, :], comb[:, b, bass.ds(e, 1)], None, ALU.mult)
                        i.then_inc(gs_ready, 1)
                    if j == MOE_STEPS // 2 and wrap:
                        slots(e + 1, it + 1, posm)
                    if j == MOE_STEPS and wrap:
                        gather_split(it + 1)

                swiglu(S_MOE, it, 1, MOE_STEPS, pos_moe, C_MOE, T_MOE, msg, mhb, look, at_step)
                dve.wait_ge(piece_used, P_MOE + (it + 1) * MOE_PIECES)
                dve.tensor_copy(yexp[:, 512:1024], bank[1][:, :]).then_inc(y_evac, 1)
                for b in range(2):
                    for half in range(2):
                        i = 2 * b + half
                        dve.wait_ge(cmb_t, 4 * it + i + 1)
                        dve.wait_ge(cmb_add, 4 * it + i + 1)
                        o = yout[:, b, half * 512:(half + 1) * 512]
                        TT(o, o, bank[2 + half][:, :], ALU.add).then_inc(cmb_add, 1)

            slots(0, 0, posm)
            gather_split(0)
            with dve.Fori(0, N_EXPERTS - 1) as e:
                expert(e, e, True)
            expert(N_EXPERTS - 1, N_EXPERTS - 1, False)
            with dve.Fori(0, N_EXPERTS) as e:
                n = dve.value_load(cnt[0:1, bass.ds(e, 1)], min_val=0, max_val=2 * P)
                with dve.If(n > CAP):
                    slots(e, e + N_EXPERTS, posm2)
                    for i in range(SPL):
                        lo_moe(i, e + N_EXPERTS)
                    gather_split(e + N_EXPERTS)
                    expert(e, e + N_EXPERTS, False)
                with dve.Else():
                    it = e + N_EXPERTS
                    for s, before, per in ((lo_ready, P_MOE + it * MOE_PIECES, MOE_PIECES),
                                           (h_done, C_MOE + it * MOE_STEPS, MOE_STEPS),
                                           (ht_lo, T_MOE + it * MOE_STEPS, MOE_STEPS),
                                           (slot_ready, it, 1), (gs_ready, it, 1), (gat_hi, it, 1), (gat_lo, it, 1),
                                           (y_evac, Y_MOE + 2 * it, 1), (cmb_add, 4 * it + 1, 4)):
                        dve.wait_ge(s, before)
                        dve.sem_inc(s, per)
            post(10)
            post(11)


_INS = ["x", "c", "ctx", "c_ctx", "ada_w", "ada_b", "norm_w", "mix_in_w", "q_norm_w", "k_norm_w", "mix_out_w",
        "ffn_gu_w", "ffn_down_w", "ssm_in_w", "ssm_conv_w", "ssm_conv_b", "ssm_dt_bias", "ssm_a_log", "ssm_d",
        "ssm_norm_w", "ssm_out_w", "router_w", "moe_gu_w", "moe_down_w"]


def kernel(**inputs):
    import numpy as _np
    import concourse.bacc as _bacc
    from concourse import mybir as _mybir
    from concourse.bass_utils import run_bass_kernel_spmd as _run

    nc = _bacc.Bacc("TRN2", target_bir_lowering=False, num_devices=1)
    const, first = shape_constants()
    arrays, aps = {}, {}
    for name in _INS + ["const", "first"]:
        a = _np.ascontiguousarray({"const": const, "first": first}[name] if name in ("const", "first") else inputs[name])
        arrays[f"in_{name}_dram"] = a
        aps[name] = nc.dram_tensor(f"in_{name}_dram", a.shape, _mybir.dt.from_np(a.dtype), kind="ExternalInput").ap()
    out = nc.dram_tensor("out_0_dram", (1, SEQ, D_MODEL), F32, kind="ExternalOutput").ap()
    build(nc, aps, out)
    r = _run(nc, [arrays], core_ids=[0])
    return r.results[0]["out_0_dram"]
```

```python
from contextlib import ExitStack

import numpy as np
import concourse.bass as bass
from concourse import mybir

P = 128
D_MODEL = 1024
SEQ = 256
CTX_LEN = 256
GRID_W = 64
F_GROUPS = 4
F_GROUP_DIM = D_MODEL // 8
F_WIDTH = F_GROUPS * F_GROUP_DIM
HEAD_DIM = 64
N_HEADS = 8
N_KV = 2
Q_WIDTH = N_HEADS * HEAD_DIM
MIX_IN = F_WIDTH + Q_WIDTH + 2 * N_KV * HEAD_DIM
ROPE_THETA = 10000.0
D_INNER = 2 * D_MODEL
N_SSM_HEADS = 32
N_GROUPS = 4
HPG = 8
D_STATE = 128
D_CONV = 5
CONV_DIM = D_INNER + 2 * N_GROUPS * D_STATE
SSM_IN = D_INNER + CONV_DIM + 2 * N_SSM_HEADS
D_FF = 2816
N_EXPERTS = 8
D_FF_EXPERT = 3584
EPS = 1e-6

KC = D_MODEL // P
LAT, CTX = (0, 1), (2, 3)
NBLK = 4

UNIT = 2048
PIECE = 1024
RAW = 6
SPL = 4
UCOL = 256

N_ADA = 2 * 6 * D_MODEL // UCOL
ADA_FIRST = 2 * D_MODEL // UCOL
U_MIXIN = MIX_IN // UCOL
U_MIXOUT = D_MODEL // UCOL
FFN_STEPS = D_FF // UCOL
MOE_STEPS = D_FF_EXPERT // UCOL
MOE_UNITS = 3 * MOE_STEPS
MOE_PIECES = 2 * MOE_UNITS
GROUP_UNITS = 5
S_MIXIN = 0
S_MIXOUT = S_MIXIN + U_MIXIN
S_FFN = S_MIXOUT + U_MIXOUT
S_DT = S_FFN + 2 * 3 * FFN_STEPS
S_GRP = S_DT + 1
S_SSMOUT = S_GRP + N_GROUPS * GROUP_UNITS
S_MOE = S_SSMOUT + 2 * U_MIXOUT
U_MOE = S_MOE + N_ADA

CAP = 128

C_ID, C_ONE, C_TF, C_TB, C_ST, C_IO, C_I8, C_SEL = 0, 128, 256, 384, 512, 640, 768, 776
N_CONST = 778
V_ADAB, V_CONVB, V_NORM, V_SNORM, V_C, V_CC, V_CONVW = 0, 96, 120, 184, 200, 208, 216
N_COLS = 336

F32 = mybir.dt.float32
F32R = mybir.dt.float32r
I32 = mybir.dt.int32
U32 = mybir.dt.uint32
ALU = mybir.AluOpType
ACT = mybir.ActivationFunctionType
AX = mybir.AxisListType


def swiglu_order(n):
    order = []
    for j in range(n + 2):
        if j < n:
            order += [("g", j), ("u", j)]
        if j >= 2:
            order.append(("d", j - 2))
    return order


def shape_constants():
    i = np.arange(P)
    c = np.zeros((P, N_CONST), np.float32)
    c[:, C_ID:C_ID + P] = np.eye(P)
    c[:, C_ONE:C_ONE + P] = 1.0
    c[:, C_TF:C_TF + P] = i[:, None] <= i[None, :]
    c[:, C_TB:C_TB + P] = i[:, None] >= i[None, :]
    c[:, C_ST:C_ST + P] = i[:, None] < i[None, :]
    c[:, C_IO:C_IO + P] = i[None, :]
    c[:, C_I8:C_I8 + 8] = np.arange(8)[None, :]
    for g in range(4):
        c[32 * g, C_SEL] = 1.0
        c[32 * g + 1, C_SEL + 1] = 1.0
    n = np.arange(SEQ)
    ang = 2 * np.pi * ((n[:, None] * n[None, :]) % SEQ) / SEQ
    s = 1.0 / np.sqrt(float(SEQ * F_GROUP_DIM))
    pos = np.concatenate([np.cos(ang) * s, np.sin(ang) * s], axis=1)
    pos = pos.reshape(2, P, 2 * SEQ).transpose(1, 0, 2).reshape(P, 4 * SEQ)
    angc = 2 * np.pi * ((i[:, None] * i[None, :]) % P) / P
    ch = np.concatenate([np.cos(angc), -np.sin(angc)], axis=1)
    t = np.arange(SEQ)
    freqs = np.float32(ROPE_THETA) ** (-np.arange(0, HEAD_DIM // 2, 2, dtype=np.float32) / np.float32(HEAD_DIM // 2))
    rang = np.concatenate([(t // GRID_W).astype(np.float32)[:, None] * freqs,
                           (t % GRID_W).astype(np.float32)[:, None] * freqs], axis=1).astype(np.float32)
    rope = np.stack([np.cos(rang), np.sin(rang)], axis=0).astype(np.float32)
    rope = rope.reshape(2, 2, P, 32).transpose(2, 0, 1, 3).reshape(P, 128)
    first = np.concatenate([pos, ch, rope], axis=1).astype(np.float32)
    return c, first


N_FIRST = 4 * SEQ + 2 * P + 128


def build(nc, A, out):
    es = ExitStack()
    with es:
        def sb(name, shape, dt=F32):
            return es.enter_context(nc.sbuf_tensor(name, shape, dt))

        def sem(name):
            return es.enter_context(nc.semaphore(name))

        bank = [es.enter_context(nc.psum_tensor(f"bank{i}", [P, 512], F32)) for i in range(8)]

        raw = sb("raw", [P, RAW, UNIT])
        hi = sb("hi", [P, SPL, PIECE], F32R)
        lo = sb("lo", [P, SPL, PIECE], F32R)
        xh_t = sb("xh_t", [P, KC * 512], F32R)
        xl_t = sb("xl_t", [P, KC * 512], F32R)
        hth = sb("hth", [P, 2, 512], F32R)
        htl = sb("htl", [P, 2, 512], F32R)
        xres = sb("xres", [P, 2, D_MODEL])
        con = sb("con", [P, N_CONST])
        cols = sb("cols", [P, N_COLS])
        ada = sb("ada", [P, 2, 48, 2])
        moda = sb("moda", [P, 4, KC, 2])
        gatec = sb("gatec", [P, 4, KC, 2])
        sc = sb("sc", [P, KC, 32])
        ss = sb("ss", [P, 32])
        rms = sb("rms", [P, 32])
        rstd = sb("rstd", [P, 32])
        epsc = sb("epsc", [P, 1])
        AR = 18400
        ar = sb("ar", [P, AR])

        xh = xh_t[:, :].rearrange("p (k n) -> p k n", k=KC)
        xl = xl_t[:, :].rearrange("p (k n) -> p k n", k=KC)
        xh16 = xh_t[:, :].rearrange("p (k n) -> p k n", k=16)
        xl16 = xl_t[:, :].rearrange("p (k n) -> p k n", k=16)

        ident = con[:, C_ID:C_ID + P]
        ones = con[:, C_ONE:C_ONE + P]
        tri = [con[:, C_TF:C_TF + P], con[:, C_TB:C_TB + P]]
        strict = con[:, C_ST:C_ST + P]
        iota = con[:, C_IO:C_IO + P]
        iota8 = con[:, C_I8:C_I8 + 8]
        sel = con[:, C_SEL:C_SEL + 2]

        class Arena:
            def __init__(self, base=0, mem=ar, size=AR):
                self.at, self.mem, self.size = base, mem, size

            def take(self, n):
                a = self.mem[:, self.at:self.at + n]
                self.at += n
                assert self.at <= self.size, self.at
                return a

        def v3(a, k):
            return a.rearrange("p (k n) -> p k n", k=k)

        m0 = Arena()
        xctx = v3(m0.take(2 * D_MODEL), 2)
        base0 = m0.at
        xn = [m0.take(D_MODEL) for _ in range(2)]
        t32 = m0.take(D_MODEL)
        px = v3(m0.take(NBLK * MIX_IN), NBLK)
        first = m0.take(N_FIRST)
        dpos = v3(first[:, 0:4 * SEQ], 2)
        dch = v3(first[:, 4 * SEQ:4 * SEQ + 2 * P], 2)
        rope = first[:, 4 * SEQ + 2 * P:N_FIRST].rearrange("p (t b n) -> p t b n", t=2, b=2)
        qkw = v3(m0.take(2 * HEAD_DIM), 2)
        part = m0.take(UCOL)
        vec_at = m0.at
        m1 = Arena(base0)
        t1s = [m1.take(512) for _ in range(2)]
        prob = [m1.take(512) for _ in range(2)]
        pts = [m1.take(512) for _ in range(2)]
        assert m1.at <= base0 + 3 * D_MODEL
        m2 = Arena(vec_at)
        qT = m2.take(NBLK * 512).rearrange("p (b c n) -> p b c n", b=NBLK, c=4)
        kT = v3(m2.take(2 * 512), 2)
        qsq = m2.take(640)
        kdup = m2.take(256)
        rtmp = m2.take(4 * 320)
        qss = v3(m2.take(40), 4)
        qrms = v3(m2.take(40), 4)
        qrs = v3(m2.take(40), 4)
        mx = m2.take(32)
        nmx = m2.take(32)
        rsum = m2.take(32)
        rinv = m2.take(32)
        m3 = Arena(vec_at)
        va, vb, vc = m3.take(P), m3.take(P), m3.take(P)
        m4 = Arena(base0 + 3 * D_MODEL)
        y = v3(m4.take(NBLK * D_MODEL), NBLK)
        m5 = Arena(m4.at)
        grow = [m5.take(D_MODEL) for _ in range(4)]
        sg = [m5.take(UCOL) for _ in range(2)]
        hb = [m5.take(UCOL) for _ in range(2)]
        ptmp = m5.take(D_MODEL)
        pjunk = m5.take(D_MODEL)

        s0 = Arena(0)
        gy = v3(s0.take(16 * SEQ), 16)
        dt_ = v3(s0.take(256), 4)
        dta = v3(s0.take(256), 4)
        acum = v3(s0.take(256), 4)
        cdec = v3(s0.take(256), 4)
        eE = v3(s0.take(256), 4)
        st1, st2, st3 = s0.take(256), s0.take(256), s0.take(256)
        dbias, arow = s0.take(64), s0.take(64)
        drow = s0.take(32)
        dcol = s0.take(16)
        sx = Arena(0, raw[:, RAW // 2:, :].rearrange("p a b -> p (a b)"), RAW // 2 * UNIT)
        cT = [s0.take(256), sx.take(256)]
        bT = s0.take(512)
        xs = sx.take(3 * 4 * SEQ).rearrange("p (s c n) -> p s c n", s=3, c=4)
        btok = [v3(s0.take(512), 4), v3(sx.take(512), 4)]
        xtok = [v3(s0.take(4 * 512), 4) for _ in range(2)]
        cbm = [a.take(512).rearrange("p (d b n) -> p d b n", d=2, b=2) for a in (s0, sx)]
        cpad = [s0.take(2 * 260).rearrange("p (s n) -> p s n", s=2) for _ in range(2)]
        cacc = [s0.take(512) for _ in range(2)]
        xE = [s0.take(512), sx.take(512)]
        xdt = [s0.take(512), sx.take(512)]
        mt = [s0.take(512) for _ in range(2)]
        ce = [s0.take(512) for _ in range(2)]
        hst = [s0.take(512) for _ in range(2)]
        o0 = Arena(0)
        yout = v3(o0.take(2 * D_MODEL), 2)
        mgrow = [o0.take(D_MODEL) for _ in range(2)]
        mptmp = o0.take(D_MODEL)
        mpjunk = o0.take(D_MODEL)
        mxn = [o0.take(D_MODEL) for _ in range(2)]
        mt32 = o0.take(D_MODEL)
        yexp = o0.take(D_MODEL)
        msg = [o0.take(UCOL) for _ in range(2)]
        mhb = [o0.take(UCOL) for _ in range(2)]
        slot1 = v3(o0.take(256), 2)
        slotg = v3(o0.take(256), 2)
        gT = v3(o0.take(256), 2)
        rw = v3(o0.take(64), 8)
        lg = v3(o0.take(16), 2)
        top = v3(o0.take(16), 2)
        idxf = v3(o0.take(16), 2)
        sel1 = v3(o0.take(16), 2)
        sel2 = v3(o0.take(16), 2)
        comb = v3(o0.take(16), 2)
        mask = v3(o0.take(16), 2)
        posm = v3(o0.take(16), 2)
        posm2 = v3(o0.take(16), 2)
        gd, ge, gs, g1, g2 = (o0.take(2) for _ in range(5))
        cntf = o0.take(8)
        idx8 = sb("idx8", [P, 2, 8], U32)
        cnt = sb("cnt", [P, 8], I32)

        raw_landed = [sem(f"raw_landed{i}") for i in range(RAW)]
        hi_ready, lo_ready, piece_used = sem("hi_ready"), sem("lo_ready"), sem("piece_used")
        ada_used, ada_part, ada_col, ada_done = (sem(n) for n in ("ada_used", "ada_part", "ada_col", "ada_done"))
        ld_x, ld_ctx, ld_con, ld_first, ld_vec, ld_qkw, ld_ssm, ld_rw = (
            sem(n) for n in ("ld_x", "ld_ctx", "ld_con", "ld_first", "ld_vec", "ld_qkw", "ld_ssm", "ld_rw"))
        zeroed, vec_t, vec_cols, sc_ready, eps_ready = (
            sem(n) for n in ("zeroed", "vec_t", "vec_cols", "sc_ready", "eps_ready"))
        mod_ready = sem("mod_ready")
        n_ss, n_rms, n_rstd, xn_ready, xt_done, xmod_done, xsplit_hi, xsplit_done = (
            sem(n) for n in ("n_ss", "n_rms", "n_rstd", "xn_ready", "xt_done", "xmod_done", "xsplit_hi", "xsplit_done"))
        lin_evac = sem("lin_evac")
        dft_t1, dft_t1s, dft_out, dft_hi, dft_lo = (sem(n) for n in ("dft_t1", "dft_t1s", "dft_out", "dft_hi", "dft_lo"))
        qk_v, qk_ss, qk_rms, qk_ready, qk_t, qk_tc = (
            sem(n) for n in ("qk_v", "qk_ss", "qk_rms", "qk_ready", "qk_t", "qk_tc"))
        at_s, at_m, at_mx, at_exp, at_r, at_nrm, at_t, at_pt, at_pv, at_oh, at_ol = (
            sem(n) for n in ("at_s", "at_m", "at_mx", "at_exp", "at_r", "at_nrm", "at_t", "at_pt", "at_pv", "at_oh", "at_ol"))
        grow_t, grow_ready = sem("grow_t"), sem("grow_ready")
        po_ss, po_rms, po_rstd, po_t, po_done = (sem(n) for n in ("po_ss", "po_rms", "po_rstd", "po_t", "po_done"))
        sil_done, h_done, ht_t, ht_hi, ht_lo, y_evac = (
            sem(n) for n in ("sil_done", "h_done", "ht_t", "ht_hi", "ht_lo", "y_evac"))
        dt_v, dt_e, dt_a, dt_t, dt_x = (sem(n) for n in ("dt_v", "dt_e", "dt_a", "dt_t", "dt_x"))
        pr_copy, cv_v, cv_acc, cv_out, tr_t, tr_copy, cb_t, cb_m = (
            sem(n) for n in ("pr_copy", "cv_v", "cv_acc", "cv_out", "tr_t", "tr_copy", "cb_t", "cb_m"))
        zs_done = sem("zs_done")
        xe_ready, st_t, st_v, st_done = (sem(n) for n in ("xe_ready", "st_t", "st_v", "st_done"))
        xdt_ready, bc_t, ce_exp, sg_ready, mt_exp, mt_ready, ce_ready, yy_t = (
            sem(n) for n in ("xdt_ready", "bc_t", "ce_exp", "sg_ready", "mt_exp", "mt_ready", "ce_ready", "yy_t"))
        gy_v, gy_done, gq_done, gn_t, gn_copy, gn_rms, gn_rstd, gf_v, gf_hi, gf_done = (
            sem(n) for n in ("gy_v", "gy_done", "gq_done", "gn_t", "gn_copy", "gn_rms", "gn_rstd", "gf_v", "gf_hi", "gf_done"))
        lg_t, rt_v, rt_e, rt_t, rt_done = (sem(n) for n in ("lg_t", "rt_v", "rt_e", "rt_t", "rt_done"))
        slot_ready, gat_t, gat_mod, gat_hi, gat_lo, gs_ready, gs_t, gT_ready, cmb_t, cmb_add = (
            sem(n) for n in ("slot_ready", "gat_t", "gat_mod", "gat_hi", "gat_lo", "gs_ready", "gs_t", "gT_ready", "cmb_t", "cmb_add"))
        stored = sem("stored")
        vstep, astep = sem("vstep"), sem("astep")
        ssg = [st1, st2, st3, sc[:, :, :].rearrange("p k n -> p (k n)")]

        def unit_of_split(s):
            return s + ADA_FIRST if s < S_MIXOUT else s + N_ADA

        def wcols(w, c0, n):
            return w.rearrange("(t p) n -> p t n", p=P)[:, :, c0:c0 + n]

        def slot(u):
            first_u, end_u = unit_of_split(S_DT), unit_of_split(S_SSMOUT)
            return (u - first_u) % (RAW // 2) if first_u <= u < end_u else u % RAW

        def rawv(u, t):
            return raw[:, slot(u), :].rearrange("p (t n) -> p t n", t=t)

        order_ffn = swiglu_order(FFN_STEPS)
        order_moe = swiglu_order(MOE_STEPS)

        def pos_of(order):
            return {k: i for i, k in enumerate(order)}

        pos_ffn, pos_moe = pos_of(order_ffn), pos_of(order_moe)

        xblk = [xres[:, 0, :], xres[:, 1, :], xctx[:, 0, :], xctx[:, 1, :]]
        NORMS = ([(0, b // 2, b) for b in range(4)] + [(1, b // 2, b) for b in range(4)] +
                 [(2, b // 2, b) for b in range(4)] + [(3, 0, b) for b in range(2)])
        N_MLP, N_SSM, N_MOE = 4, 8, 12
        POSTS = ([(0, b // 2, b) for b in range(4)] + [(1, b // 2, b) for b in range(4)] +
                 [(2, 0, b) for b in range(2)] + [(3, 0, b) for b in range(2)])
        GROWS = [(0, 0), (0, 1), (1, 0), (1, 1), (2, 0), (3, 0)]

        def grow_tile(r):
            return grow[r] if r < 4 else mgrow[r - 4]

        def grow_of(n):
            return GROWS.index(POSTS[n][:2])

        def post_src(n):
            b = POSTS[n][2]
            return y[:, b, :] if n < 8 else yout[:, b, :]

        def xn_of(n):
            return mxn[n % 2] if n >= N_MOE else xn[n % 2]

        def t32_of(n):
            return mt32 if n >= N_MOE else t32

        def mod_cols(m, s):
            l, w = m // 2, m % 2
            return moda[:, m, :, s], ada[:, l, 24 * w:24 * w + KC, s]

        AT_SCALE = HEAD_DIM ** -0.5
        ITERS = [("dft", i) for i in range(8)] + [("att", i) for i in range(32)]

        def at_info(i):
            s, b, h = i // 16, i // 8, i % 8
            return s, b, h, (0, 4) if s == 0 else (2, 2)

        ssd_idx = [(d, b, q) for d, bs in ((0, (0, 1)), (1, (1, 0))) for b in bs for q in range(2)]
        ssd_states = [(d, k, b) for d, bs in ((0, (2, 3, 0)), (1, (3, 2, 1))) for k, b in enumerate(bs)]
        NQ = len(ssd_idx)
        NST = len(ssd_states)

        SLOTS = 10
        USED = (2, 3, 4, 5, 6, 7, 9, 10, 10, 10)

        def split_by(g, k):
            return 2 * (S_GRP + g * GROUP_UNITS) + (USED[k - 1] if k else 0) + SPL


        LIN_MIXOUT = U_MIXIN * NBLK
        LIN_SSMOUT = LIN_MIXOUT + U_MIXOUT * NBLK
        RT_N = 1

        def is_pair_unit(s):
            return S_GRP <= s < S_SSMOUT and (s - S_GRP) % GROUP_UNITS == 0

        split_unit = {unit_of_split(s): s for s in range(S_MOE)}
        landed, total = {}, [0] * RAW
        for u in range(U_MOE):
            total[slot(u)] += 32 if u in split_unit and is_pair_unit(split_unit[u]) else 16
            landed[u] = total[slot(u)]
        PER_SLOT = 16 * (MOE_UNITS // RAW)

        def landed_moe(i, it):
            return total[(U_MOE + i) % RAW] + 16 * (i // RAW + 1) + it * PER_SLOT

        P_MOE = 2 * S_MOE
        FFN_N = len(order_ffn)
        C_MOE, T_MOE, Y_MOE = 2 * 2 * FFN_STEPS, 2 * FFN_STEPS, 8

        block = es.enter_context(nc.Block())

        @block.sync
        def _(sp):
            sp.dma_start(vb[0:64, :], A["norm_w"].rearrange("i n (k q) -> (i n k) q", q=P)).then_inc(ld_vec, 16)
            sp.dma_start(vb[64:80, :], A["ssm_norm_w"].rearrange("i (k q) -> (i k) q", q=P)).then_inc(ld_vec, 16)
            sp.dma_start(vb[80:88, :], A["c"].rearrange("i (k q) -> (i k) q", q=P)).then_inc(ld_vec, 16)
            sp.dma_start(vb[88:96, :], A["c_ctx"].rearrange("(k q) -> k q", q=P)).then_inc(ld_vec, 16)
            sp.dma_start(con[:, :], A["const"]).then_inc(ld_con, 16)
            sp.dma_start(va[0:96, :], A["ada_b"].rearrange("l (c q) -> (l c) q", q=P)).then_inc(ld_vec, 16)
            sp.dma_start(va[96:120, :], A["ssm_conv_b"].rearrange("l (c q) -> (l c) q", q=P)).then_inc(ld_vec, 16)
            sp.dma_start(vc[0:120, :], A["ssm_conv_w"].rearrange("l t (c q) -> (l t c) q", q=P)).then_inc(ld_vec, 16)

            owner = {}

            def free(u):
                if slot(u) in owner:
                    kind, n = owner[slot(u)]
                    if kind == "ada":
                        sp.wait_ge(ada_used, n + 1)
                    else:
                        sp.wait_ge(lo_ready, 2 * (n + 1))

            def load(u, kind, n, dst, src):
                free(u)
                sp.dma_start(dst, src).then_inc(raw_landed[slot(u)], 16)
                owner[slot(u)] = (kind, n)

            def load_ada(a0, a1):
                for a in range(a0, a1):
                    l, c = divmod(a, N_ADA // 2)
                    u = a if a < ADA_FIRST else a + U_MIXIN
                    load(u, "ada", a, rawv(u, 8), wcols(A["ada_w"][l], c * UCOL, UCOL))

            def load_cols(s, w, c0, n=UCOL):
                u = unit_of_split(s)
                load(u, "split", s, rawv(u, 8)[:, :, 0:n], wcols(w, c0, n))

            load_ada(0, 3)
            sp.dma_start(xres[:, :, :], A["x"].rearrange("o (b p) n -> p (o b) n", p=P)).then_inc(ld_x, 16)
            sp.dma_start(xctx, A["ctx"].rearrange("o (b p) n -> p (o b) n", p=P)).then_inc(ld_ctx, 16)
            load_ada(3, ADA_FIRST)
            for i in range(U_MIXIN):
                load_cols(S_MIXIN + i, A["mix_in_w"][0], i * UCOL)
            sp.dma_start(first, A["first"]).then_inc(ld_first, 16)
            sp.dma_start(qkw[:, 0, :], A["q_norm_w"][0].partition_broadcast(P)).then_inc(ld_qkw, 16)
            sp.dma_start(qkw[:, 1, :], A["k_norm_w"][0].partition_broadcast(P)).then_inc(ld_qkw, 16)
            load_ada(ADA_FIRST, N_ADA)
            for i in range(U_MIXOUT):
                load_cols(S_MIXOUT + i, A["mix_out_w"][0], i * UCOL)
            gu, dn = A["ffn_gu_w"][0], A["ffn_down_w"][0]
            for ps in range(2):
                for i, (k, j) in enumerate(order_ffn):
                    s = S_FFN + ps * FFN_N + i
                    if k == "d":
                        u = unit_of_split(s)
                        load(u, "split", s, rawv(u, 2),
                             dn[j * UCOL:(j + 1) * UCOL, :].rearrange("(t p) n -> p t n", p=P))
                    else:
                        load_cols(s, gu, j * UCOL + (D_FF if k == "u" else 0))
            w_in = A["ssm_in_w"][0]
            x0, b0, c0 = D_INNER, 2 * D_INNER, 2 * D_INNER + N_GROUPS * D_STATE
            load_cols(S_DT, w_in, D_INNER + CONV_DIM, 2 * N_SSM_HEADS)
            for g in range(N_GROUPS):
                s = S_GRP + g * GROUP_UNITS
                u = unit_of_split(s)
                load(u, "split", s, rawv(u, 8)[:, :, 0:P], wcols(w_in, b0 + g * P, P))
                sp.dma_start(rawv(u, 8)[:, :, P:2 * P], wcols(w_in, c0 + g * P, P)).then_inc(raw_landed[slot(u)], 16)
                for i in range(2):
                    load_cols(s + 1 + i, w_in, x0 + g * 512 + i * UCOL)
                for i in range(2):
                    load_cols(s + 3 + i, w_in, g * 512 + i * UCOL)
                if g == 0:
                    sp.wait_ge(xsplit_done, N_SSM + 4)
                    for dst, src in ((dbias, A["ssm_dt_bias"].rearrange("l d h -> (l d h)")),
                                     (arow, A["ssm_a_log"].rearrange("l d h -> (l d h)")),
                                     (drow, A["ssm_d"][0])):
                        sp.dma_start(dst, src.partition_broadcast(P)).then_inc(ld_ssm, 16)
            for i in range(2 * U_MIXOUT):
                q, kh = divmod(i, 2)
                if i == RAW // 2:
                    sp.wait_ge(gn_t, N_GROUPS)
                load_cols(S_SSMOUT + i, A["ssm_out_w"][0][kh * D_MODEL:(kh + 1) * D_MODEL, :], q * UCOL)
            sp.wait_ge(gf_done, 4)
            sp.dma_start(rw, A["router_w"][0].rearrange("(t p) n -> p t n", p=P)).then_inc(ld_rw, 16)

            def expert_weights(e, it):
                gu = A["moe_gu_w"][0][bass.ds(e, 1)].rearrange("o k n -> (o k) n")
                dn = A["moe_down_w"][0][bass.ds(e, 1)].rearrange("o k n -> (o k) n")
                for i, (k, j) in enumerate(order_moe):
                    u = U_MOE + i
                    sp.wait_ge(lo_ready, it * MOE_PIECES + 2 * (S_MOE + i - RAW + 1))
                    if k == "d":
                        sp.dma_start(rawv(u, 2), dn[j * UCOL:(j + 1) * UCOL, :].rearrange("(t p) n -> p t n", p=P)
                                     ).then_inc(raw_landed[u % RAW], 16)
                    else:
                        sp.dma_start(rawv(u, 8), wcols(gu, j * UCOL + (D_FF_EXPERT if k == "u" else 0), UCOL)
                                     ).then_inc(raw_landed[u % RAW], 16)

            with sp.Fori(0, N_EXPERTS) as e:
                expert_weights(e, e)
            sp.wait_ge(rt_done, RT_N)
            with sp.Fori(0, N_EXPERTS) as e:
                n = sp.value_load(cnt[0:1, bass.ds(e, 1)], min_val=0, max_val=2 * P)
                with sp.If(n > CAP):
                    expert_weights(e, e + N_EXPERTS)
                with sp.Else():
                    for k in range(RAW):
                        s = raw_landed[(U_MOE + k) % RAW]
                        sp.wait_ge(s, landed_moe(k, e + N_EXPERTS) - 16)
                        sp.sem_inc(s, PER_SLOT)
            for b in range(2):
                sp.wait_ge(po_done, 11 + b)
                sp.dma_start(out.rearrange("o (b p) n -> p (o b) n", p=P)[:, b, :], xres[:, b, :]).then_inc(stored, 16)
            sp.wait_ge(stored, 32)

        @block.gpsimd
        def _(pool):
            pool.memset(sc[:, :, :], 0.0).then_inc(zeroed, 1)
            pool.memset(epsc[:, :], EPS).then_inc(eps_ready, 1)
            pool.wait_ge(xsplit_done, N_SSM + 4)
            for t in cpad:
                pool.memset(t, 0.0).then_inc(zeroed, 1)
            for g in range(N_GROUPS):
                def scaled_x(dst, blk, scale, d, done):
                    a = d * N_SSM_HEADS + g * HPG
                    pool.tensor_tensor(dst.rearrange("p (h q) -> p h q", h=HPG),
                                       xtok[g % 2][:, blk, :].rearrange("p (h q) -> p h q", h=HPG),
                                       scale[:, blk, a:a + HPG].unsqueeze(2).to_broadcast((P, HPG, 64)),
                                       ALU.mult).then_inc(done, 1)

                pool.wait_ge(dt_x, 1)
                pool.wait_ge(tr_copy, 5 * (g + 1))
                pool.wait_ge(cv_out, 6 * (g + 1))

                def xE_(k):
                    d, _, blk = ssd_states[k]
                    n = g * NST + k
                    if n >= 2:
                        pool.wait_ge(st_t, n - 1)
                    scaled_x(xE[k % 2], blk, eE, d, xe_ready)

                def xdt_(m):
                    d, b, _ = ssd_idx[2 * m]
                    n = g * NQ // 2 + m
                    if n >= 2:
                        pool.wait_ge(yy_t, 2 * (n - 1))
                    scaled_x(xdt[m % 2], b, dt_, d, xdt_ready)

                def ce_(q):
                    d, b, _ = ssd_idx[q]
                    pool.wait_ge(ce_exp, g * NQ + q + 1)
                    pool.tensor_tensor(v3(ce[q % 2], 4), v3(ce[q % 2], 4),
                                       cT[g % 2][:, b * P:(b + 1) * P].unsqueeze(1).to_broadcast((P, 4, P)),
                                       ALU.mult).then_inc(ce_ready, 1)

                xE_(0)
                xE_(1)
                xdt_(0)
                xdt_(1)
                ce_(0)
                ce_(1)
                xE_(2)
                ce_(2)
                xE_(3)
                xdt_(2)
                ce_(3)
                xE_(4)
                ce_(4)
                xdt_(3)
                ce_(5)
                xE_(5)
                ce_(6)
                ce_(7)

        @block.tensor
        def _(pe):
            mm = pe.matmul

            def tok3(o, a_hi, a_lo, w_hi, w_lo, first, last):
                mm(o, a_hi, w_hi, start=first, stop=False)
                mm(o, a_hi, w_lo, start=False, stop=False)
                return mm(o, a_lo, w_hi, start=False, stop=last)

            def wpart(p, t, n, off=0, width=None):
                a = t * n + off
                return hi[:, p % SPL, a:a + (width or n)], lo[:, p % SPL, a:a + (width or n)]

            pe.wait_ge(ld_vec, 16 * 7)
            pe.wait_ge(ld_con, 16)
            for t, n, c in ((vb, 96, 0), (va, 120, 1), (vc, 120, 2)):
                pe.transpose(bank[5 + c][:, 0:n], t[0:n, :], ident[0:n, 0:n]).then_inc(vec_t, 1)

            def ada_a(a):
                u = a if a < ADA_FIRST else a + U_MIXIN
                pe.wait_ge(raw_landed[slot(u)], landed[u])
                if a == 0:
                    pe.wait_ge(sc_ready, 2)
                if a > 0:
                    pe.wait_ge(ada_part, a)
                w = rawv(u, 8)
                for t in range(2):
                    for g in range(4):
                        m = mm(bank[6][32 * g:32 * g + 32, 0:UCOL], sc[:, 2 * g + t, :], w[:, 2 * g + t, :],
                               start=(t == 0), stop=(t == 1), tile_position=(0, 32 * g))
                m.then_inc(ada_used, 1)

            def ada_b(a):
                pe.wait_ge(ada_part, a + 1)
                if a > 0:
                    pe.wait_ge(ada_done, a)
                for i in range(2):
                    m = mm(bank[7][:, 2 * i:2 * i + 2], part[:, i * P:(i + 1) * P], sel, start=True, stop=True)
                m.then_inc(ada_col, 1)

            pe.wait_ge(vec_cols, 3)
            for a in range(ADA_FIRST + 1):
                if a < ADA_FIRST:
                    ada_a(a)
                if a >= 1:
                    ada_b(a - 1)

            def norm_t(n):
                pe.wait_ge(xn_ready, n + 1)
                if n >= 2:
                    pe.wait_ge(xmod_done, n - 1)
                for k in range(KC):
                    m = pe.transpose(bank[2 * (n % 2) + k // 4][:, (k % 4) * P:(k % 4 + 1) * P],
                                     xn_of(n)[:, k * P:(k + 1) * P], ident)
                m.then_inc(xt_done, 1)

            def linear(s0, lin0):
                for u in range(U_MIXIN if s0 == S_MIXIN else U_MIXOUT):
                    for h in range(2):
                        p = 2 * (s0 + u) + h
                        pe.wait_ge(lo_ready, p + 1)
                        for b in range(NBLK):
                            if h == 0 and u >= 2:
                                pe.wait_ge(lin_evac, lin0 + (u - 2) * NBLK + b + 1)
                            for t in range(4):
                                k = 4 * h + t
                                m = tok3(bank[(u % 2) * 4 + b][:, 0:UCOL], xh[:, k, b * P:(b + 1) * P],
                                         xl[:, k, b * P:(b + 1) * P], *wpart(p, t, UCOL),
                                         first=(k == 0), last=(k == KC - 1))
                        m.then_inc(piece_used, 1)

            for n in range(4):
                norm_t(n)
            pe.wait_ge(xsplit_done, 4)
            pe.wait_ge(ada_done, ADA_FIRST)
            linear(S_MIXIN, 0)

            pe.wait_ge(ld_first, 16)
            pe.wait_ge(lin_evac, LIN_MIXOUT)

            def dft_1(i):
                s, g = divmod(i, 4)
                if i >= 2:
                    pe.wait_ge(dft_t1s, i - 1)
                for b in range(2):
                    m = mm(bank[i % 2][:, :], px[:, 2 * s + b, g * P:(g + 1) * P], dpos[:, b, :],
                           start=(b == 0), stop=(b == 1))
                m.then_inc(dft_t1, 1)

            def dft_2(i):
                pe.wait_ge(dft_t1s, i + 1)
                if i >= 2:
                    pe.wait_ge(dft_lo, i - 1)
                o = bank[2 + i % 2][:, 0:SEQ]
                mm(o, dch[:, 0, :], t1s[i % 2][:, 0:SEQ], start=True, stop=False)
                mm(o, dch[:, 1, :], t1s[i % 2][:, SEQ:2 * SEQ], start=False, stop=True).then_inc(dft_out, 1)

            def qk_t_(b):
                pe.wait_ge(qk_ready, b + 1)
                if b >= 1:
                    pe.wait_ge(qk_tc, 2 * b)
                for c in range(4):
                    a = F_WIDTH + c * P
                    pe.transpose(bank[4][:, c * P:(c + 1) * P], px[:, b, a:a + P], ident)
                for v in range(N_KV):
                    m = pe.transpose(bank[5][:, v * P:(v + 1) * P], kdup[:, v * P:(v + 1) * P], ident)
                m.then_inc(qk_t, 1)

            def att_s(i):
                s, b, h, (k0, nk) = at_info(i)
                if i >= 2:
                    pe.wait_ge(at_exp, i - 1)
                r = (h % 2) * 64
                mm(bank[i % 2][:, 0:nk * P], qT[r:r + 64, b, h // 2, :], kT[r:r + 64, h // 4, k0 % 4 * P:(k0 % 4 + nk) * P],
                   start=True, stop=True).then_inc(at_s, 1)

            def att_t(i):
                nk = at_info(i)[3][1]
                pe.wait_ge(at_nrm, i + 1)
                if i >= 2:
                    pe.wait_ge(at_pt, i - 1)
                for c in range(nk):
                    m = pe.transpose(bank[2 + i % 2][:, c * P:(c + 1) * P], prob[i % 2][:, c * P:(c + 1) * P], ident)
                m.then_inc(at_t, 1)

            def att_pv(i):
                s, b, h, (k0, nk) = at_info(i)
                pe.wait_ge(at_pt, i + 1)
                if h == 0 and b >= 2:
                    pe.wait_ge(at_ol, b - 1)
                r = (h % 2) * 64
                for c in range(nk):
                    a = F_WIDTH + Q_WIDTH + (N_KV + h // 4) * 64
                    m = mm(bank[4 + b % 2][r:r + 64, (h // 2) * P:(h // 2 + 1) * P], px[:, k0 + c, a:a + 64],
                           pts[i % 2][:, c * P:(c + 1) * P], start=(c == 0), stop=(c == nk - 1))
                m.then_inc(at_pv, 1)

            def step(it):
                return ITERS[it] if 0 <= it < len(ITERS) else (None, 0)

            for it in range(len(ITERS) + 2):
                if it == 8:
                    for b in range(NBLK):
                        qk_t_(b)
                    pe.wait_ge(qk_tc, 2 * NBLK)
                k, i = step(it)
                if k == "dft":
                    dft_1(i)
                if k == "att":
                    att_s(i)
                if it < len(ITERS):
                    ada_a(ADA_FIRST + it)
                k, i = step(it - 1)
                if k == "dft":
                    dft_2(i)
                if k == "att":
                    att_t(i)
                k, i = step(it - 2)
                if k == "att":
                    att_pv(i)
                if 1 <= it <= len(ITERS):
                    ada_b(ADA_FIRST + it - 1)
            pe.wait_ge(at_ol, 4)
            pe.wait_ge(dft_lo, 8)
            pe.wait_ge(ada_done, N_ADA)
            linear(S_MIXOUT, LIN_MIXOUT)

            def grow_(r):
                m_, s = GROWS[r]
                if r >= 2:
                    pe.wait_ge(grow_ready, r - 1)
                for k in range(KC):
                    m = mm(bank[4 + 2 * (r % 2) + k // 4][:, (k % 4) * P:(k % 4 + 1) * P],
                           gatec[:, m_, k, s:s + 1].to_broadcast((P, P)), ident, start=True, stop=True)
                m.then_inc(grow_t, 1)

            pe.wait_ge(mod_ready, 8)
            pe.wait_ge(lin_evac, LIN_SSMOUT)
            for r in range(4):
                grow_(r)
            for n in range(4, 8):
                norm_t(n)
            pe.wait_ge(grow_ready, 4)

            def swiglu(s0, it, nblk, n, pos, xoff, c0, t0, y_free, at_step=None):
                pd, cd, td = it * MOE_PIECES, it * MOE_STEPS, it * MOE_STEPS
                for j in range(n + 2):
                    for kind in ("g", "u") if j < n else ():
                        for h in range(2):
                            p = 2 * (s0 + pos[(kind, j)]) + h
                            pe.wait_ge(lo_ready, pd + p + 1)
                            for b in range(nblk):
                                c = c0 + j * nblk + b
                                if kind == "g" and h == 0 and c >= 2:
                                    pe.wait_ge(h_done, cd + c - 1)
                                o = bank[4 + c % 2][:, 0:UCOL] if kind == "g" else bank[4 + c % 2][:, UCOL:2 * UCOL]
                                for t in range(4):
                                    k = 4 * h + t
                                    a = xoff + b * P
                                    m = tok3(o, xh[:, k, a:a + P], xl[:, k, a:a + P], *wpart(p, t, UCOL),
                                             first=(k == 0), last=(k == KC - 1))
                            m.then_inc(piece_used, 1)
                    if 1 <= j <= n:
                        tj = t0 + j - 1
                        pe.wait_ge(h_done, cd + c0 + j * nblk)
                        if tj >= 2:
                            pe.wait_ge(ht_lo, td + tj - 1)
                        for b in range(nblk):
                            for i in range(2):
                                m = pe.transpose(bank[6 + tj % 2][:, (2 * b + i) * P:(2 * b + i + 1) * P],
                                                 hbuf((c0 + (j - 1) * nblk + b) % 2)[:, i * P:(i + 1) * P], ident)
                        m.then_inc(ht_t, 1)
                    if at_step:
                        at_step(j)
                    if j >= 2:
                        tj = t0 + j - 2
                        pe.wait_ge(ht_lo, td + tj + 1)
                        if j == 2 and y_free is not None:
                            pe.wait_ge(y_evac, y_free)
                        for h in range(2):
                            p = 2 * (s0 + pos[("d", j - 2)]) + h
                            pe.wait_ge(lo_ready, pd + p + 1)
                            for b in range(nblk):
                                a = (2 * b + h) * P
                                for half in range(2):
                                    m = tok3(bank[2 * b + half][:, :], hth[:, tj % 2, a:a + P], htl[:, tj % 2, a:a + P],
                                             *wpart(p, 0, 1024, half * 512, 512),
                                             first=(j == 2 and h == 0), last=(j == n + 1 and h == 1))
                            m.then_inc(piece_used, 1)

            def hbuf(i):
                return hcur[0][i]

            hcur = [hb]
            pe.wait_ge(xsplit_done, 8)
            for ps in range(2):
                swiglu(S_FFN + ps * FFN_N, 0, 2, FFN_STEPS, pos_ffn, ps * 2 * P, ps * 2 * FFN_STEPS, ps * FFN_STEPS,
                       4 if ps else None)

            for n in range(8, 12):
                norm_t(n)
            pe.wait_ge(xsplit_done, 12)
            for h in range(2):
                p = 2 * S_DT + h
                pe.wait_ge(lo_ready, p + 1)
                for b in range(NBLK):
                    for t in range(4):
                        k = 4 * h + t
                        m = tok3(bank[b][:, 0:64], xh[:, k, b * P:(b + 1) * P], xl[:, k, b * P:(b + 1) * P],
                                 *wpart(p, t, UCOL, 0, 64), first=(k == 0), last=(k == KC - 1))
                m.then_inc(piece_used, 1)

            def proj(g, ui, h):
                p = 2 * (S_GRP + g * GROUP_UNITS + ui) + h
                pe.wait_ge(lo_ready, p + 1)
                if h == 0 and g + ui > 0:
                    pe.wait_ge(pr_copy, 10 * g + 2 * ui)
                if h == 0 and g + ui == 0:
                    pe.wait_ge(dt_v, 4)
                for c in range(2):
                    n = 512 if ui in (1, 2) or (ui == 0 and c == 0) else SEQ
                    o = bank[c][:, 0:n]
                    for t in range(4):
                        k = 4 * h + t
                        w_hi, w_lo = wpart(p, t, UCOL, c * P, P)
                        mm(o, w_hi, xh[:, k, 0:n], start=(k == 0), stop=False)
                        mm(o, w_hi, xl[:, k, 0:n], start=False, stop=False)
                        m = mm(o, w_lo, xh[:, k, 0:n], start=False, stop=(k == KC - 1))
                m.then_inc(piece_used, 1)

            def to_tok(g, i):
                pe.wait_ge(cv_out, 6 * g + (1 if i == 0 else i + 2))
                if g * 5 + i > 0:
                    pe.wait_ge(tr_copy, g * 5 + i)
                if i == 0 and g > 1:
                    pe.wait_ge(gn_copy, g - 1)
                for b in range(NBLK):
                    src = bT[:, b * P:(b + 1) * P] if i == 0 else \
                        xs[:, g % 2 if b in LAT else 2, i - 1, (b % 2) * P:(b % 2 + 1) * P]
                    m = pe.transpose(bank[5][:, b * P:(b + 1) * P], src, ident)
                m.then_inc(tr_t, 1)

            def decay_sums():
                pe.wait_ge(dt_a, 1)
                for b in range(NBLK):
                    for d in range(2):
                        a = 64 * b + 32 * d
                        mm(bank[6][:, a:a + 32], tri[d], dta[:, b, 32 * d:32 * d + 32], start=True, stop=True)
                    m = mm(bank[7][:, 64 * b:64 * b + 64], ones, dta[:, b, :], start=True, stop=True)
                m.then_inc(dt_t, 1)

            def cb(g):
                pe.wait_ge(cv_out, 6 * g + 2)
                if g > 0:
                    pe.wait_ge(st_done, g * NST)
                for b in range(2):
                    m = mm(bank[4][:, b * P:(b + 1) * P], bT[:, b * P:(b + 1) * P],
                           cT[g % 2][:, b * P:(b + 1) * P],
                           start=True, stop=True)
                m.then_inc(cb_t, 1)

            def bc(g, q):
                d, b, hq = ssd_idx[q]
                n = g * NQ + q
                if n >= 2:
                    pe.wait_ge(sg_ready, n - 1)
                for i in range(4):
                    a = d * N_SSM_HEADS + g * HPG + hq * 4 + i
                    m = mm(bank[2 + q % 2][:, i * P:(i + 1) * P], dta[:, b, a:a + 1].to_broadcast((P, P)), tri[d],
                           start=True, stop=True)
                m.then_inc(bc_t, 1)

            def state(g, k):
                n = g * NST + k
                pe.wait_ge(xe_ready, n + 1)
                if k == 0:
                    pe.wait_ge(cb_m, g + 1)
                if n >= 1:
                    pe.wait_ge(st_done, n)
                mm(bank[4][:, :], btok[g % 2][:, ssd_states[k][2], :], xE[k % 2], start=True, stop=True).then_inc(st_t, 1)

            def yy(g, q):
                d, b, hq = ssd_idx[q]
                n = g * NQ + q
                pe.wait_ge(mt_ready, n + 1)
                pe.wait_ge(ce_ready, n + 1)
                pe.wait_ge(xdt_ready, g * 4 + q // 2 + 1)
                pe.wait_ge(st_done, g * NST + (2, 3, 5, 6)[q // 2])
                if q == 0 and g > 0:
                    pe.wait_ge(gy_v, 4 * g)
                for i0 in (0, 2):
                    for x, y_, last in ((xdt[q // 2 % 2], mt, False), (hst[d], ce, True)):
                        for i in (i0, i0 + 1):
                            h = hq * 4 + i
                            r = (h % 2) * 64
                            a = (i // 2) * SEQ + b * P
                            m = mm(bank[6 + hq][r:r + 64, a:a + P], x[:, h * 64:h * 64 + 64],
                                   y_[q % 2][:, i * P:(i + 1) * P], start=(q < 2 and i < 2 and not last),
                                   stop=(q >= NQ - 2 and i >= 2 and last), skip_group_check=True)
                m.then_inc(yy_t, 1)

            def project(g, k):
                if g == N_GROUPS:
                    return
                if k == 0:
                    proj(g, 0, 0)
                    proj(g, 0, 1)
                if k in (1, 2):
                    proj(g, 1, k - 1)
                if k == 3:
                    proj(g, 2, 0)
                if k == 4:
                    to_tok(g, 0)
                    proj(g, 2, 1)
                if k == 5:
                    proj(g, 3, 0)
                if k == 6:
                    proj(g, 3, 1)
                    to_tok(g, 1)
                    proj(g, 4, 0)
                if k == 7:
                    proj(g, 4, 1)
                    to_tok(g, 2)
                if k == 8:
                    to_tok(g, 3)
                if k == 9:
                    to_tok(g, 4)
                    cb(g)

            def scan(g, k):
                if k == 0:
                    bc(g, 0)
                    project(g + 1, k)
                    state(g, 0)
                    state(g, 1)
                    bc(g, 1)
                elif k <= NQ:
                    q = k - 1
                    if q + 2 < NQ:
                        bc(g, q + 2)
                    project(g + 1, k)
                    yy(g, q)
                    for i in {1: (2,), 2: (3, 4), 5: (5,)}.get(q, ()):
                        state(g, i)
                else:
                    project(g + 1, k)

            def late(g, k):
                if k == 1:
                    pe.wait_ge(gq_done, g + 1)
                    pe.wait_ge(tr_copy, min(5 * (g + 2), 5 * N_GROUPS))
                    for c in range(4):
                        m = mm(bank[5][:, 0:SEQ], ones, xs[:, g % 2, c, :], start=(c == 0), stop=(c == 3))
                    m.then_inc(gn_t, 1)

            for k in range(SLOTS):
                project(0, k)
            decay_sums()
            pe.wait_ge(dt_x, 1)
            for g in range(N_GROUPS):
                for k in range(SLOTS):
                    if g > 0:
                        late(g - 1, k)
                    scan(g, k)
            late(N_GROUPS - 1, 1)

            pe.wait_ge(gf_done, 4)
            for q in range(U_MIXOUT):
                for kh in range(2):
                    for h in range(2):
                        p = 2 * (S_SSMOUT + 2 * q + kh) + h
                        pe.wait_ge(lo_ready, p + 1)
                        for b in range(2):
                            if kh == 0 and h == 0 and q >= 2:
                                pe.wait_ge(lin_evac, LIN_SSMOUT + (q - 2) * 2 + b + 1)
                            for t in range(4):
                                k = 8 * kh + 4 * h + t
                                m = tok3(bank[(q % 2) * 2 + b][:, 0:UCOL], xh16[:, k, b * P:(b + 1) * P],
                                         xl16[:, k, b * P:(b + 1) * P], *wpart(p, t, UCOL),
                                         first=(k == 0), last=(k == 15))
                        m.then_inc(piece_used, 1)
            pe.wait_ge(gy_v, 16)
            for r in (4, 5):
                grow_(r)
            norm_t(12)
            norm_t(13)

            pe.wait_ge(xsplit_done, 14)
            pe.wait_ge(ld_rw, 16)
            for b in range(2):
                for k in range(KC):
                    for x in (xh, xl):
                        m = mm(bank[4][:, 8 * b:8 * b + 8], x[:, k, b * P:(b + 1) * P].bitcast(F32), rw[:, k, :],
                               start=(k == 0 and x is xh), stop=(k == KC - 1 and x is xl))
            m.then_inc(lg_t, 1)
            pe.wait_ge(rt_v, 1)
            mm(bank[5][:, 0:8], strict, mask[:, 0, :], start=True, stop=True)
            mm(bank[5][:, 8:16], strict, mask[:, 1, :], start=True, stop=False)
            mm(bank[5][:, 8:16], ones, mask[:, 0, :], start=False, stop=True)
            mm(bank[5][:, 16:24], ones, mask[:, 0, :], start=True, stop=False)
            mm(bank[5][:, 16:24], ones, mask[:, 1, :], start=False, stop=True).then_inc(rt_t, 1)

            hcur[0] = mhb

            def gather(it):
                pe.wait_ge(slot_ready, it + 1)
                for k in range(KC):
                    for b in range(2):
                        m = mm(bank[2 + k // 4][:, (k % 4) * P:(k % 4 + 1) * P], mxn[b][:, k * P:(k + 1) * P],
                               slot1[:, b, :], start=(b == 0), stop=(b == 1))
                m.then_inc(gat_t, 1)

            def expert(it, wrap):
                pe.wait_ge(gat_lo, it + 1)

                def at_step(j):
                    if j == 3:
                        pe.wait_ge(gs_ready, it + 1)
                        for b in range(2):
                            m = pe.transpose(bank[2][:, b * P:(b + 1) * P], slotg[:, b, :], ident)
                        m.then_inc(gs_t, 1)
                    if j == MOE_STEPS and wrap:
                        pe.wait_ge(gT_ready, it + 1)
                        gather(it + 1)

                swiglu(S_MOE, it, 1, MOE_STEPS, pos_moe, 0, C_MOE, T_MOE, 2 * it + Y_MOE, at_step)
                pe.wait_ge(gT_ready, it + 1)
                pe.wait_ge(y_evac, 2 * it + Y_MOE + 2)
                if wrap:
                    pe.wait_ge(gat_mod, it + 2)
                for b in range(2):
                    for half in range(2):
                        if b == 1:
                            pe.wait_ge(cmb_add, 4 * it + 1 + half + 1)
                        mm(bank[2 + half][:, :], gT[:, b, :], yexp[:, half * 512:(half + 1) * 512],
                           start=True, stop=True).then_inc(cmb_t, 1)

            gather(0)
            with pe.Fori(0, N_EXPERTS - 1) as e:
                expert(e, True)
            expert(N_EXPERTS - 1, False)
            pe.wait_ge(rt_done, RT_N)
            with pe.Fori(0, N_EXPERTS) as e:
                n = pe.value_load(cnt[0:1, bass.ds(e, 1)], min_val=0, max_val=2 * P)
                with pe.If(n > CAP):
                    gather(e + N_EXPERTS)
                    expert(e + N_EXPERTS, False)
                with pe.Else():
                    it = e + N_EXPERTS
                    for s, before, per in ((piece_used, P_MOE + it * MOE_PIECES, MOE_PIECES),
                                           (ht_t, T_MOE + it * MOE_STEPS, MOE_STEPS),
                                           (gat_t, it, 1), (gs_t, it, 1), (cmb_t, 4 * it, 4)):
                        pe.wait_ge(s, before)
                        pe.sem_inc(s, per)

        @block.scalar
        def _(act):
            A_ = act.activation
            spl = [0]

            def hi_piece(p):
                u = unit_of_split(p // 2)
                if p % 2 == 0:
                    act.wait_ge(raw_landed[slot(u)], landed[u])
                if p >= SPL:
                    act.wait_ge(piece_used, p - SPL + 1)
                A_(hi[:, p % SPL, :], raw[:, slot(u), (p % 2) * PIECE:(p % 2 + 1) * PIECE], ACT.Copy
                   ).then_inc(hi_ready, 1)

            def hi_to(n):
                while spl[0] < min(n, P_MOE):
                    hi_piece(spl[0])
                    spl[0] += 1
                if n > P_MOE:
                    for i in range(spl[0] - P_MOE, n - P_MOE):
                        hi_moe(i, 0)
                        spl[0] += 1

            def hi_moe(i, it):
                if i % 2 == 0:
                    u = U_MOE + i // 2
                    act.wait_ge(raw_landed[u % RAW], landed_moe(i // 2, it))
                p = P_MOE + i
                act.wait_ge(piece_used, it * MOE_PIECES + p - SPL + 1)
                u = (U_MOE + i // 2) % RAW
                A_(hi[:, p % SPL, :], raw[:, u, (i % 2) * PIECE:(i % 2 + 1) * PIECE], ACT.Copy).then_inc(hi_ready, 1)

            steps = [0]

            def own(ins):
                ins.then_inc(astep, 1)
                steps[0] += 1
                act.wait_ge(astep, steps[0])

            act.wait_ge(vec_cols, 3)
            act.wait_ge(zeroed, 1)
            A_(sc[:, :, 0], cols[:, V_C:V_C + KC], ACT.Silu).then_inc(sc_ready, 1)
            A_(sc[:, :, 1], cols[:, V_CC:V_CC + KC], ACT.Silu).then_inc(sc_ready, 1)

            def ada_copy(a):
                act.wait_ge(ada_used, a + 1)
                if a > 0:
                    act.wait_ge(ada_col, a)
                A_(part, bank[6][:, 0:UCOL], ACT.Copy).then_inc(ada_part, 1)

            def norm_a(n):
                if n < 4:
                    act.wait_ge(*((ld_x, 16) if n < 2 else (ld_ctx, 16)))
                else:
                    act.wait_ge(po_done, n - 3)
                if n >= 2:
                    act.wait_ge(xt_done, n - 1)
                if n == 0:
                    act.wait_ge(eps_ready, 1)
                A_(xn_of(n), xblk[NORMS[n][2]], ACT.Square, accum_out=ss[:, n:n + 1]).then_inc(n_ss, 1)
                act.wait_ge(n_ss, n + 1)
                A_(rms[:, n:n + 1], ss[:, n:n + 1], ACT.Sqrt, scale=1.0 / D_MODEL, bias=epsc[:, 0:1]).then_inc(n_rms, 1)

            def norm_b(n):
                m, s, b = NORMS[n]
                act.wait_ge(xt_done, n + 1)
                act.wait_ge(mod_ready, 1 if m == 0 else 8)
                if n >= 1:
                    act.wait_ge(xsplit_done, n)
                a_, b_ = mod_cols(m, s)
                for k in range(KC):
                    i = A_(t32_of(n)[:, k * P:(k + 1) * P], bank[2 * (n % 2) + k // 4][:, (k % 4) * P:(k % 4 + 1) * P],
                           ACT.Identity, scale=a_[:, k:k + 1], bias=b_[:, k:k + 1])
                i.then_inc(xmod_done, 1)

            def post_a(n):
                A_(pjunk if n < 8 else mpjunk, post_src(n), ACT.Square, accum_out=ss[:, 14 + n:15 + n]).then_inc(po_ss, 1)
                act.wait_ge(po_ss, n + 1)
                A_(rms[:, 14 + n:15 + n], ss[:, 14 + n:15 + n], ACT.Sqrt, scale=1.0 / D_MODEL, bias=epsc[:, 0:1]
                   ).then_inc(po_rms, 1)

            for a in range(ADA_FIRST):
                ada_copy(a)
                if a in (4, 5):
                    norm_a(a - 4)
            norm_b(0)
            norm_a(2)
            norm_b(1)
            norm_a(3)
            norm_b(2)
            hi_to(2)
            norm_b(3)
            hi_to(SPL)

            def lin_out(s0, lin0, dst):
                for u in range(U_MIXIN if s0 == S_MIXIN else U_MIXOUT):
                    hi_to(2 * (s0 + u) + 1 + SPL)
                    hi_to(2 * (s0 + u) + 2 + SPL)
                    act.wait_ge(piece_used, 2 * (s0 + u) + 2)
                    for b in range(NBLK):
                        A_(dst[:, b, u * UCOL:(u + 1) * UCOL], bank[(u % 2) * 4 + b][:, 0:UCOL], ACT.Copy
                           ).then_inc(lin_evac, 1)

            def lin_in():
                for u in range(U_MIXIN):
                    hi_to(min(2 * u + 2 + SPL, 2 * S_MIXOUT))
                    act.wait_ge(piece_used, 2 * u + 2)
                    for b in range(NBLK):
                        A_(px[:, b, u * UCOL:(u + 1) * UCOL], bank[(u % 2) * 4 + b][:, 0:UCOL], ACT.Copy
                           ).then_inc(lin_evac, 1)

            lin_in()

            def step(it):
                return ITERS[it] if 0 <= it < len(ITERS) else (None, 0)

            for it in range(len(ITERS) + 2):
                if it == 8:
                    for b in range(NBLK):
                        act.wait_ge(qk_t, b + 1)
                        A_(qT[:, b, :, :], bank[4][:, :].rearrange("p (c n) -> p c n", c=4), ACT.Copy).then_inc(qk_tc, 1)
                        A_(kT[:, :, b * P:(b + 1) * P], v3(bank[5][:, 0:2 * P], 2), ACT.Copy).then_inc(qk_tc, 1)
                k, i = step(it)
                if k == "dft":
                    act.wait_ge(dft_t1, i + 1)
                    if i >= 2:
                        act.wait_ge(dft_out, i - 1)
                    A_(t1s[i % 2], bank[i % 2][:, :], ACT.Copy).then_inc(dft_t1s, 1)
                    if i % 2 == 1:
                        b = i // 2
                        act.wait_ge(qk_ss, b + 1)
                        A_(qrms[:, b, :], qss[:, b, :], ACT.Sqrt, scale=1.0 / HEAD_DIM, bias=epsc[:, 0:1]
                           ).then_inc(qk_rms, 1)
                if k == "att":
                    nk = at_info(i)[3][1]
                    act.wait_ge(at_mx, i + 1)
                    if i >= 2:
                        act.wait_ge(at_t, i - 1)
                    A_(prob[i % 2][:, 0:nk * P], bank[i % 2][:, 0:nk * P], ACT.Exp, bias=nmx[:, i:i + 1], scale=AT_SCALE,
                       accum_out=rsum[:, i:i + 1]).then_inc(at_exp, 1)
                if it < len(ITERS):
                    ada_copy(ADA_FIRST + it)
                k, i = step(it - 1)
                if k == "dft":
                    s, g = divmod(i, 4)
                    act.wait_ge(dft_out, i + 1)
                    A_(xh[:, g, s * SEQ:(s + 1) * SEQ], bank[2 + i % 2][:, 0:SEQ], ACT.Copy).then_inc(dft_hi, 1)
                if k == "att":
                    nk = at_info(i)[3][1]
                    act.wait_ge(at_t, i + 1)
                    if i >= 2:
                        act.wait_ge(at_pv, i - 1)
                    A_(pts[i % 2][:, 0:nk * P], bank[2 + i % 2][:, 0:nk * P], ACT.Copy).then_inc(at_pt, 1)
                k, i = step(it - 2)
                if k == "att" and i % 8 == 7:
                    b = i // 8
                    act.wait_ge(at_pv, i + 1)
                    A_(xh[:, 4:8, b * P:(b + 1) * P], v3(bank[4 + b % 2][:, :], 4), ACT.Copy).then_inc(at_oh, 1)
            hi_to(2 * S_MIXOUT + SPL)
            lin_out(S_MIXOUT, LIN_MIXOUT, y)

            def grow_out(r):
                act.wait_ge(grow_t, r + 1)
                for k in range(2):
                    i = A_(grow_tile(r)[:, k * 512:(k + 1) * 512], bank[4 + 2 * (r % 2) + k][:, :], ACT.Copy)
                i.then_inc(grow_ready, 1)

            def residuals(n0):
                post_a(n0)
                post_a(n0 + 1)
                norm_a(n0 + 4)
                post_a(n0 + 2)
                norm_a(n0 + 5)
                norm_b(n0 + 4)
                post_a(n0 + 3)
                norm_a(n0 + 6)
                norm_b(n0 + 5)
                norm_a(n0 + 7)
                norm_b(n0 + 6)
                norm_b(n0 + 7)

            for r in range(4):
                grow_out(r)
            residuals(0)

            def swiglu(s0, it, nblk, n, pos, c0, t0, sgt, look, at_step=None):
                pd, cd, td = it * MOE_PIECES, it * MOE_STEPS, it * MOE_STEPS
                for j in range(n + 2):
                    if j < n:
                        for kind in ("g", "u"):
                            for h in range(2):
                                look(2 * pos[(kind, j)] + h)
                        act.wait_ge(piece_used, pd + 2 * (s0 + pos[("u", j)]) + 2)
                        for b in range(nblk):
                            c = c0 + j * nblk + b
                            if c >= 2:
                                act.wait_ge(h_done, cd + c - 1)
                            A_(sgt[c % 2], bank[4 + c % 2][:, 0:UCOL], ACT.Silu).then_inc(sil_done, 1)
                    if 1 <= j <= n:
                        tj = t0 + j - 1
                        act.wait_ge(ht_t, td + tj + 1)
                        if j >= 3:
                            act.wait_ge(piece_used, pd + 2 * (s0 + pos[("d", j - 3)]) + 2)
                        A_(hth[:, tj % 2, 0:2 * nblk * P], bank[6 + tj % 2][:, 0:2 * nblk * P], ACT.Copy
                           ).then_inc(ht_hi, 1)
                    if at_step:
                        at_step(j)
                    if j >= 2:
                        for h in range(2):
                            look(2 * pos[("d", j - 2)] + h)

            for ps in range(2):
                s0 = S_FFN + ps * FFN_N
                swiglu(s0, 0, 2, FFN_STEPS, pos_ffn, ps * 2 * FFN_STEPS, ps * FFN_STEPS, sg,
                       lambda i, s0=s0: hi_to(2 * s0 + i + 1 + SPL))
                act.wait_ge(piece_used, 2 * (s0 + FFN_N))
                for half in range(2):
                    A_(y[:, 2 * ps, half * 512:(half + 1) * 512], bank[half][:, :], ACT.Copy).then_inc(y_evac, 1)
            act.wait_ge(y_evac, 8)
            residuals(4)

            for h in range(2):
                hi_to(2 * S_DT + h + 1 + SPL)
            act.wait_ge(ld_ssm, 48)
            A_(arow, arow, ACT.Exp).then_inc(dt_e, 1)
            act.wait_ge(dt_v, 5)
            A_(st2, st2, ACT.Exp, scale=-1.0).then_inc(dt_e, 1)

            def conv_in(g, i):
                n, ui = 6 * g + i, i // 2
                act.wait_ge(piece_used, 2 * (S_GRP + g * GROUP_UNITS + ui) + 2)
                if n == 0:
                    act.wait_ge(zeroed, 3)
                if n >= 2:
                    act.wait_ge(cv_acc, n - 1)
                ns = 1 if i == 1 else 2
                A_(cpad[n % 2][:, 0:ns, 2:2 + SEQ], v3(bank[i % 2][:, 0:ns * SEQ], ns), ACT.Copy).then_inc(pr_copy, 1)

            def conv_out(g, i):
                n = 6 * g + i
                act.wait_ge(cv_acc, n + 1)
                if i == 0 and g > 0:
                    act.wait_ge(cb_t, g)
                src = cacc[n % 2] if i != 1 else cacc[n % 2][:, 0:SEQ]
                if i >= 2:
                    src = v3(src, 2)
                dst = bT if i == 0 else cT[g % 2] if i == 1 else xs[:, g % 2::2 - g % 2, i - 2, :]
                ch = (16 + g, 20 + g, 4 * g, 4 * g + 1, 4 * g + 2, 4 * g + 3)[i]
                A_(dst, src, ACT.Silu, bias=cols[:, V_CONVB + ch:V_CONVB + ch + 1]).then_inc(cv_out, 1)

            def tok(g, i):
                act.wait_ge(tr_t, 5 * g + i + 1)
                dst = btok[g % 2][:, :, :] if i == 0 else xtok[g % 2][:, :, (i - 1) * P:i * P]
                A_(dst, v3(bank[5][:, :], NBLK), ACT.Copy).then_inc(tr_copy, 1)

            def zs(g, ui, func):
                act.wait_ge(piece_used, 2 * (S_GRP + g * GROUP_UNITS + ui) + 2)
                for c in range(2):
                    A_(gy[:, 4 * g + 2 * (ui - 3) + c, :], bank[c][:, 0:SEQ], func).then_inc(pr_copy, 1)

            def project(g, k):
                if g == N_GROUPS:
                    return
                hi_to(split_by(g, k))
                if k == 0:
                    conv_in(g, 0)
                    conv_in(g, 1)
                if k == 2:
                    conv_in(g, 2)
                    conv_in(g, 3)
                if k == 3:
                    conv_out(g, 0)
                    conv_out(g, 1)
                if k == 4:
                    tok(g, 0)
                    conv_in(g, 4)
                if k == 5:
                    conv_in(g, 5)
                    conv_out(g, 2)
                    conv_out(g, 3)
                if k == 6:
                    zs(g, 3, ACT.Copy)
                    tok(g, 1)
                if k == 7:
                    conv_out(g, 4)
                    conv_out(g, 5)
                    z01 = gy[:, 4 * g:4 * g + 2, :]
                    act.wait_ge(pr_copy, 10 * g + 8)
                    A_(z01, z01, ACT.Silu).then_inc(zs_done, 1)
                    zs(g, 4, ACT.Silu)
                    tok(g, 2)
                if k == 8:
                    tok(g, 3)
                if k == 9:
                    tok(g, 4)

            def ce_(g, q):
                n = g * NQ + q
                act.wait_ge(bc_t, n + 1)
                if n >= 2:
                    act.wait_ge(yy_t, n - 1)
                A_(ce[q % 2], bank[2 + q % 2][:, :], ACT.Exp).then_inc(ce_exp, 1)

            def m_(g, q):
                act.wait_ge(sg_ready, g * NQ + q + 1)
                A_(mt[q % 2], mt[q % 2], ACT.Exp).then_inc(mt_exp, 1)

            def scan(g, k):
                if k == 0:
                    ce_(g, 0)
                    project(g + 1, k)
                    ce_(g, 1)
                elif k <= NQ:
                    q = k - 1
                    m_(g, q)
                    project(g + 1, k)
                    if q + 2 < NQ:
                        ce_(g, q + 2)
                else:
                    project(g + 1, k)

            def late(g, k):
                x = xs[:, g % 2, :, :]
                if k == 0:
                    act.wait_ge(gy_done, g + 1)
                    A_(x, gy[:, 4 * g:4 * g + 4, :], ACT.Square).then_inc(gq_done, 1)
                if k == 2:
                    act.wait_ge(gn_t, g + 1)
                    A_(ssg[g], bank[5][:, 0:SEQ], ACT.Copy).then_inc(gn_copy, 1)

            for k in range(SLOTS):
                project(0, k)
            act.wait_ge(dt_v, 7)
            A_(cdec[:, :, :], v3(bank[7][:, 0:256], 4), ACT.Exp).then_inc(dt_e, 1)
            A_(eE[:, :, :], v3(st1, 4), ACT.Exp).then_inc(dt_e, 1)
            for g in range(N_GROUPS):
                for k in range(SLOTS):
                    if g > 0:
                        late(g - 1, k)
                    scan(g, k)
            late(N_GROUPS - 1, 0)
            late(N_GROUPS - 1, 2)
            act.wait_ge(gn_copy, 4)
            for g in range(N_GROUPS):
                A_(ssg[g], ssg[g], ACT.Sqrt, scale=1.0 / 512, bias=epsc[:, 0:1]).then_inc(gn_rms, 1)
            for g in range(N_GROUPS):
                act.wait_ge(gf_v, 4 * (g + 1))
                A_(xh16[:, 4 * g:4 * g + 4, :], gy[:, 4 * g:4 * g + 4, :], ACT.Copy).then_inc(gf_hi, 1)
            for q in range(U_MIXOUT):
                for i in range(4):
                    hi_to(2 * S_SSMOUT + 4 * q + i + 1 + SPL)
                act.wait_ge(piece_used, 2 * S_SSMOUT + 4 * q + 4)
                for b in range(2):
                    A_(yout[:, b, q * UCOL:(q + 1) * UCOL], bank[(q % 2) * 2 + b][:, 0:UCOL], ACT.Copy
                       ).then_inc(lin_evac, 1)
            act.wait_ge(lin_evac, LIN_SSMOUT + 8)
            for r in (4, 5):
                grow_out(r)
            post_a(8)
            post_a(9)
            norm_a(12)
            norm_a(13)
            norm_b(12)
            norm_b(13)
            act.wait_ge(rt_v, 2)
            A_(ge, gd, ACT.Exp).then_inc(rt_e, 1)

            def gather_mod(it):
                act.wait_ge(gat_t, it + 1)
                a_, b_ = mod_cols(3, 0)
                for k in range(KC):
                    i = A_(mt32[:, k * P:(k + 1) * P], bank[2 + k // 4][:, (k % 4) * P:(k % 4 + 1) * P],
                           ACT.Identity, scale=a_[:, k:k + 1], bias=b_[:, k:k + 1])
                i.then_inc(gat_mod, 1)

            def expert(it, wrap):
                def look(i):
                    if i + SPL < MOE_PIECES or wrap:
                        hi_moe(i + SPL, it)

                def at_step(j):
                    if j == 3:
                        act.wait_ge(gs_t, it + 1)
                        A_(gT[:, :, :], v3(bank[2][:, 0:2 * P], 2), ACT.Copy).then_inc(gT_ready, 1)
                    if j == MOE_STEPS and wrap:
                        gather_mod(it + 1)

                swiglu(S_MOE, it, 1, MOE_STEPS, pos_moe, C_MOE, T_MOE, msg, look, at_step)
                act.wait_ge(piece_used, P_MOE + (it + 1) * MOE_PIECES)
                A_(yexp[:, 0:512], bank[0][:, :], ACT.Copy).then_inc(y_evac, 1)

            act.wait_ge(xsplit_done, 14)
            gather_mod(0)
            with act.Fori(0, N_EXPERTS - 1) as e:
                expert(e, True)
            expert(N_EXPERTS - 1, False)
            with act.Fori(0, N_EXPERTS) as e:
                n = act.value_load(cnt[0:1, bass.ds(e, 1)], min_val=0, max_val=2 * P)
                with act.If(n > CAP):
                    for i in range(SPL):
                        hi_moe(i, e + N_EXPERTS)
                    gather_mod(e + N_EXPERTS)
                    expert(e + N_EXPERTS, False)
                with act.Else():
                    it = e + N_EXPERTS
                    for s, before, per in ((hi_ready, P_MOE + it * MOE_PIECES, MOE_PIECES),
                                           (sil_done, C_MOE + it * MOE_STEPS, MOE_STEPS),
                                           (ht_hi, T_MOE + it * MOE_STEPS, MOE_STEPS),
                                           (gat_mod, it, 1), (gT_ready, it, 1), (y_evac, Y_MOE + 2 * it, 1)):
                        act.wait_ge(s, before)
                        act.sem_inc(s, per)
            act.wait_ge(cmb_add, 4 * 2 * N_EXPERTS + 1)
            post_a(10)
            post_a(11)

        @block.vector
        def _(dve):
            TT, TS, STT = dve.tensor_tensor, dve.tensor_scalar, dve.scalar_tensor_tensor
            spl = [0]

            def lo_sub(p, u, h):
                TT(lo[:, p % SPL, :], raw[:, u, h * PIECE:(h + 1) * PIECE], hi[:, p % SPL, :].bitcast(F32), ALU.subtract
                   ).then_inc(lo_ready, 1)

            def lo_to(n):
                while spl[0] < n:
                    p = spl[0]
                    if p < P_MOE:
                        dve.wait_ge(hi_ready, p + 1)
                        lo_sub(p, slot(unit_of_split(p // 2)), p % 2)
                    else:
                        lo_moe(p - P_MOE, 0)
                    spl[0] += 1

            def lo_moe(i, it):
                dve.wait_ge(hi_ready, it * MOE_PIECES + P_MOE + i + 1)
                lo_sub(P_MOE + i, (U_MOE + i // 2) % RAW, i % 2)

            steps = [0]

            def own(ins):
                ins.then_inc(vstep, 1)
                steps[0] += 1
                dve.wait_ge(vstep, steps[0])

            for i, (n, c) in enumerate(((96, V_NORM), (120, V_ADAB), (120, V_CONVW))):
                dve.wait_ge(vec_t, i + 1)
                dve.tensor_copy(cols[:, c:c + n], bank[5 + i][:, 0:n]).then_inc(vec_cols, 1)

            def ada_take(a):
                l, c = divmod(a, N_ADA // 2)
                dve.wait_ge(ada_col, a + 1)
                TT(ada[:, l, 2 * c:2 * c + 2, :], v3(bank[7][:, 0:4], 2),
                   cols[:, V_ADAB + l * 48 + 2 * c:V_ADAB + l * 48 + 2 * c + 2].unsqueeze(2).to_broadcast((P, 2, 2)),
                   ALU.add).then_inc(ada_done, 1)

            def norm_w(l, i):
                a = V_NORM + (l * 4 + i) * KC
                return cols[:, a:a + KC].unsqueeze(2).to_broadcast((P, KC, 2))

            def scale_cols(m):
                l, w = divmod(m, 2)
                STT(moda[:, m, :, :], ada[:, l, 24 * w + KC:24 * w + 2 * KC, :], 1.0, norm_w(l, 2 * w),
                    ALU.add, ALU.mult).then_inc(mod_ready, 1)

            def gate_cols(m):
                l, w = divmod(m, 2)
                TT(gatec[:, m, :, :], ada[:, l, 24 * w + 2 * KC:24 * w + 3 * KC, :], norm_w(l, 2 * w + 1), ALU.mult
                   ).then_inc(mod_ready, 1)

            def norm_a(n):
                dve.wait_ge(n_rms, n + 1)
                dve.reciprocal(rstd[:, n:n + 1], rms[:, n:n + 1]).then_inc(n_rstd, 1)
                dve.wait_ge(n_rstd, n + 1)
                TS(xn_of(n), xblk[NORMS[n][2]], rstd[:, n:n + 1], None, ALU.mult).then_inc(xn_ready, 1)

            def norm_b(n):
                b = NORMS[n][2]
                dve.wait_ge(xmod_done, n + 1)
                dve.tensor_copy(xh[:, :, b * P:(b + 1) * P], v3(t32_of(n), KC)).then_inc(xsplit_hi, 1)
                dve.wait_ge(xsplit_hi, n + 1)
                TT(xl[:, :, b * P:(b + 1) * P], v3(t32_of(n), KC), xh[:, :, b * P:(b + 1) * P].bitcast(F32), ALU.subtract
                   ).then_inc(xsplit_done, 1)

            def post(n):
                m, s, b = POSTS[n]
                t = ptmp if n < 8 else mptmp
                dve.wait_ge(po_rms, n + 1)
                dve.reciprocal(rstd[:, 14 + n:15 + n], rms[:, 14 + n:15 + n]).then_inc(po_rstd, 1)
                dve.wait_ge(po_rstd, n + 1)
                dve.wait_ge(grow_ready, grow_of(n) + 1)
                STT(t, post_src(n), rstd[:, 14 + n:15 + n], grow_tile(grow_of(n)), ALU.mult, ALU.mult
                    ).then_inc(po_t, 1)
                dve.wait_ge(po_t, n + 1)
                TT(xblk[b], xblk[b], t, ALU.add).then_inc(po_done, 1)

            for a in range(ADA_FIRST):
                ada_take(a)
                if a in (4, 5):
                    norm_a(a - 4)
            dve.wait_ge(ada_done, ADA_FIRST)
            scale_cols(0)
            norm_b(0)
            norm_a(2)
            norm_b(1)
            norm_a(3)
            norm_b(2)
            lo_to(2)
            norm_b(3)
            lo_to(SPL)
            for u in range(U_MIXIN):
                lo_to(min(2 * u + 2 + SPL, 2 * S_MIXOUT))

            dve.wait_ge(lin_evac, LIN_MIXOUT)
            dve.wait_ge(ld_qkw, 32)
            dve.wait_ge(ld_first, 16)

            def heads(b, n0=0, n1=10):
                a = F_WIDTH
                return px[:, b, a + n0 * 64:a + n1 * 64].rearrange("p (h n) -> p h n", n=64)

            def qk_1(b):
                own(TT(qsq, px[:, b, F_WIDTH:F_WIDTH + 640], px[:, b, F_WIDTH:F_WIDTH + 640], ALU.mult))
                dve.tensor_reduce(qss[:, b, :], qsq.rearrange("p (h n) -> p h n", n=64), AX.X, ALU.add
                                  ).then_inc(qk_ss, 1)

            def qk_2(b):
                dve.wait_ge(qk_rms, b + 1)
                own(dve.reciprocal(qrs[:, b, :], qrms[:, b, :]))
                own(TT(heads(b), heads(b), qrs[:, b, :].unsqueeze(2).to_broadcast((P, 10, 64)), ALU.mult))
                TT(heads(b, 0, 8), heads(b, 0, 8), qkw[:, 0:1, :].to_broadcast((P, 8, 64)), ALU.mult)
                own(TT(heads(b, 8, 10), heads(b, 8, 10), qkw[:, 1:2, :].to_broadcast((P, 2, 64)), ALU.mult))

            def qk_3(b):
                if b in LAT:
                    x = px[:, b, F_WIDTH:F_WIDTH + 640].rearrange("p (h n two) -> p h n two", n=32, two=2)
                    x1, x2 = x[:, :, :, 0], x[:, :, :, 1]
                    c, s = (rope[:, i, b, :].unsqueeze(1).to_broadcast((P, 10, 32)) for i in range(2))
                    r = [rtmp[:, i * 320:(i + 1) * 320].rearrange("p (h n) -> p h n", n=32) for i in range(4)]
                    TT(r[0], x1, c, ALU.mult)
                    TT(r[1], x2, s, ALU.mult)
                    TT(r[2], x1, s, ALU.mult)
                    own(TT(r[3], x2, c, ALU.mult))
                    TT(x1, r[0], r[1], ALU.subtract)
                    own(TT(x2, r[2], r[3], ALU.add))

            def qk_4(b):
                if b >= 1:
                    dve.wait_ge(qk_t, b)
                a = F_WIDTH + Q_WIDTH
                dve.tensor_copy(kdup.rearrange("p (v two n) -> p v two n", v=2, two=2),
                                px[:, b, a:a + 2 * 64].rearrange("p (v n) -> p v n", v=2).unsqueeze(2)
                                .to_broadcast((P, 2, 2, 64))).then_inc(qk_ready, 1)

            def step(it):
                return ITERS[it] if 0 <= it < len(ITERS) else (None, 0)

            for it in range(len(ITERS) + 2):
                k, i = step(it)
                if k == "dft":
                    if i % 2 == 0:
                        qk_1(i // 2)
                    else:
                        qk_2(i // 2)
                        qk_3(i // 2)
                if it == 8:
                    for b in range(NBLK):
                        qk_4(b)
                k1, i1 = step(it - 1)
                if k1 == "att":
                    dve.wait_ge(at_exp, i1 + 1)
                    nk = at_info(i1)[3][1]
                    dve.reciprocal(rinv[:, i1:i1 + 1], rsum[:, i1:i1 + 1]).then_inc(at_r, 1)
                    dve.wait_ge(at_r, i1 + 1)
                    TS(prob[i1 % 2][:, 0:nk * P], prob[i1 % 2][:, 0:nk * P], rinv[:, i1:i1 + 1], None, ALU.mult
                       ).then_inc(at_nrm, 1)
                if k == "att":
                    nk = at_info(i)[3][1]
                    dve.wait_ge(at_s, i + 1)
                    dve.tensor_reduce(mx[:, i:i + 1], bank[i % 2][:, 0:nk * P], AX.X, ALU.max).then_inc(at_m, 1)
                    dve.wait_ge(at_m, i + 1)
                    TS(nmx[:, i:i + 1], mx[:, i:i + 1], -AT_SCALE, None, ALU.mult).then_inc(at_mx, 1)
                if k1 == "dft":
                    s, g = divmod(i1, 4)
                    dve.wait_ge(dft_hi, i1 + 1)
                    TT(xl[:, g, s * SEQ:(s + 1) * SEQ], bank[2 + i1 % 2][:, 0:SEQ],
                       xh[:, g, s * SEQ:(s + 1) * SEQ].bitcast(F32), ALU.subtract).then_inc(dft_lo, 1)
                if 1 <= it <= len(ITERS):
                    ada_take(ADA_FIRST + it - 1)
                k, i = step(it - 2)
                if k == "att" and i % 8 == 7:
                    b = i // 8
                    dve.wait_ge(at_oh, b + 1)
                    TT(xl[:, 4:8, b * P:(b + 1) * P], v3(bank[4 + b % 2][:, :], 4),
                       xh[:, 4:8, b * P:(b + 1) * P].bitcast(F32), ALU.subtract).then_inc(at_ol, 1)
            lo_to(2 * S_MIXOUT + SPL)
            dve.wait_ge(ada_done, N_ADA)
            for m in range(1, 4):
                scale_cols(m)
            for m in range(4):
                gate_cols(m)
            for u in range(U_MIXOUT):
                lo_to(2 * (S_MIXOUT + u) + 2 + SPL)

            def residuals(n0):
                post(n0)
                post(n0 + 1)
                norm_a(n0 + 4)
                post(n0 + 2)
                norm_a(n0 + 5)
                norm_b(n0 + 4)
                post(n0 + 3)
                norm_a(n0 + 6)
                norm_b(n0 + 5)
                norm_a(n0 + 7)
                norm_b(n0 + 6)
                norm_b(n0 + 7)

            residuals(0)

            def swiglu(s0, it, nblk, n, pos, c0, t0, sgt, ht, look, at_step=None):
                cd, td = it * MOE_STEPS, it * MOE_STEPS
                for j in range(n + 2):
                    if j < n:
                        for kind in ("g", "u"):
                            for h in range(2):
                                look(2 * pos[(kind, j)] + h)
                        for b in range(nblk):
                            c = c0 + j * nblk + b
                            dve.wait_ge(sil_done, cd + c + 1)
                            free = t0 + j - (2 // nblk) + 1
                            if free >= 1:
                                dve.wait_ge(ht_t, td + free)
                            TT(ht[c % 2], sgt[c % 2], bank[4 + c % 2][:, UCOL:2 * UCOL], ALU.mult).then_inc(h_done, 1)
                    if 1 <= j <= n:
                        tj = t0 + j - 1
                        dve.wait_ge(ht_hi, td + tj + 1)
                        w = 2 * nblk * P
                        TT(htl[:, tj % 2, 0:w], bank[6 + tj % 2][:, 0:w], hth[:, tj % 2, 0:w].bitcast(F32), ALU.subtract
                           ).then_inc(ht_lo, 1)
                    if at_step:
                        at_step(j)
                    if j >= 2:
                        for h in range(2):
                            look(2 * pos[("d", j - 2)] + h)

            for ps in range(2):
                s0 = S_FFN + ps * FFN_N
                swiglu(s0, 0, 2, FFN_STEPS, pos_ffn, ps * 2 * FFN_STEPS, ps * FFN_STEPS, sg, hb,
                       lambda i, s0=s0: lo_to(2 * s0 + i + 1 + SPL))
                dve.wait_ge(piece_used, 2 * (s0 + FFN_N))
                for half in range(2):
                    dve.tensor_copy(y[:, 2 * ps + 1, half * 512:(half + 1) * 512], bank[2 + half][:, :]).then_inc(y_evac, 1)
            residuals(4)

            for h in range(2):
                lo_to(2 * S_DT + h + 1 + SPL)
            dve.wait_ge(ld_ssm, 48)
            dve.wait_ge(piece_used, 2 * S_DT + 2)
            for b in range(NBLK):
                TT(st1[:, 64 * b:64 * b + 64], bank[b][:, 0:64], dbias, ALU.add).then_inc(dt_v, 1)
            dve.wait_ge(dt_v, 4)
            STT(st2, st1, -1.0, st1, ALU.mult, ALU.max).then_inc(dt_v, 1)
            dve.tensor_copy(dcol[0:64, :], drow[0:64, 0:32:2])
            own(dve.tensor_copy(dcol[64:128, :], drow[64:128, 1:32:2]))
            dve.wait_ge(dt_e, 2)
            own(TS(st3, st2, 2.0, None, ALU.add))
            own(dve.reciprocal(st3, st3))
            own(TT(st2, st2, st3, ALU.mult))
            own(TT(st3, st2, st2, ALU.mult))
            p_ = acum[:, :, :].rearrange("p b n -> p (b n)")
            own(TS(p_, st3, 1.0 / 17, None, ALU.mult))
            for k in range(7, 0, -1):
                own(STT(p_, p_, 1.0 / (2 * k + 1), st3, ALU.add, ALU.mult))
            own(STT(p_, p_, 1.0, st2, ALU.add, ALU.mult))
            own(TS(st1, st1, 0.0, None, ALU.max))
            d_ = dt_[:, :, :].rearrange("p b n -> p (b n)")
            own(STT(d_, p_, 2.0, st1, ALU.mult, ALU.add))
            STT(dta[:, :, :], dt_[:, :, :], -1.0, arow.unsqueeze(1).to_broadcast((P, NBLK, 64)), ALU.mult, ALU.mult
                ).then_inc(dt_a, 1)

            def conv(g, i):
                n = 6 * g + i
                ch = (16 + g, 20 + g, 4 * g, 4 * g + 1, 4 * g + 2, 4 * g + 3)[i]
                ns = 1 if i == 1 else 2
                dve.wait_ge(pr_copy, 10 * g + i + 1)
                if n >= 2:
                    dve.wait_ge(cv_out, n - 1)
                o = v3(cacc[n % 2][:, 0:ns * SEQ], ns)

                def tap(t):
                    a = V_CONVW + t * 24 + ch
                    return cpad[n % 2][:, 0:ns, t:t + SEQ], cols[:, a:a + 1]

                x, w = tap(0)
                TS(o, x, w, None, ALU.mult).then_inc(cv_v, 1)
                for t in range(1, D_CONV):
                    dve.wait_ge(cv_v, 4 * n + t)
                    x, w = tap(t)
                    STT(o, x, w, o, ALU.mult, ALU.add).then_inc(cv_v if t < D_CONV - 1 else cv_acc, 1)

            def project(g, k):
                if g == N_GROUPS:
                    return
                lo_to(split_by(g, k))
                if 1 <= k <= 6:
                    conv(g, k - 1)
                if k == 9:
                    dve.wait_ge(cb_t, g + 1)
                    for d in range(2):
                        i = TT(cbm[g % 2][:, d, :, :], v3(bank[4][:, 0:2 * P], 2),
                               tri[d].unsqueeze(1).to_broadcast((P, 2, P)), ALU.mult)
                    i.then_inc(cb_m, 1)

            def seg(g, q):
                d, b, hq = ssd_idx[q]
                n = g * NQ + q
                dve.wait_ge(ce_exp, n + 1)
                if n >= 2:
                    dve.wait_ge(yy_t, n - 1)
                for i in range(4):
                    a = d * N_SSM_HEADS + g * HPG + hq * 4 + i
                    m = TS(mt[q % 2][:, i * P:(i + 1) * P], bank[2 + q % 2][:, i * P:(i + 1) * P],
                           acum[:, b, a:a + 1], 0.0, ALU.subtract, ALU.min)
                m.then_inc(sg_ready, 1)

            def mul(g, q):
                d, b, _ = ssd_idx[q]
                dve.wait_ge(mt_exp, g * NQ + q + 1)
                TT(v3(mt[q % 2], 4), v3(mt[q % 2], 4), cbm[g % 2][:, d, b:b + 1, :].to_broadcast((P, 4, P)), ALU.mult
                   ).then_inc(mt_ready, 1)

            def state(g, k):
                d, kk, b = ssd_states[k]
                n = g * NST + k
                dve.wait_ge(st_t, n + 1)
                if kk == 0:
                    dve.tensor_copy(hst[d], bank[4][:, :]).then_inc(st_done, 1)
                    return
                if kk == 2:
                    dve.wait_ge(yy_t, g * NQ + (2 if d == 0 else 6))
                dve.wait_ge(st_done, n)
                a = d * N_SSM_HEADS + g * HPG
                hv = hst[d].rearrange("p (h q) -> p h q", h=HPG)
                own(TT(hv, hv, cdec[:, b, a:a + HPG].unsqueeze(2).to_broadcast((P, HPG, 64)), ALU.mult))
                TT(hst[d], hst[d], bank[4][:, :], ALU.add).then_inc(st_done, 1)

            def gated(g):
                dve.wait_ge(yy_t, (g + 1) * NQ)
                dve.wait_ge(cv_out, 6 * (g + 1))
                for c in range(4):
                    x = xs[:, g % 2, c, :]
                    STT(x, x, dcol[:, 4 * g + c:4 * g + c + 1], bank[6 + c // 2][:, (c % 2) * SEQ:(c % 2 + 1) * SEQ],
                        ALU.mult, ALU.add).then_inc(gy_v, 1)
                dve.wait_ge(gy_v, 4 * (g + 1))
                dve.wait_ge(pr_copy, 10 * (g + 1))
                dve.wait_ge(zs_done, g + 1)
                z = gy[:, 4 * g:4 * g + 4, :]
                TT(z, z, xs[:, g % 2, :, :], ALU.mult).then_inc(gy_done, 1)

            def scan(g, k):
                if k == 0:
                    seg(g, 0)
                    project(g + 1, k)
                    state(g, 0)
                    state(g, 1)
                    seg(g, 1)
                elif k <= NQ:
                    q = k - 1
                    mul(g, q)
                    project(g + 1, k)
                    if q == 1:
                        state(g, 2)
                    if q + 2 < NQ:
                        seg(g, q + 2)
                    for i in {2: (3, 4), 5: (5,)}.get(q, ()):
                        state(g, i)
                else:
                    project(g + 1, k)
                    gated(g)

            for k in range(SLOTS):
                project(0, k)
            dve.wait_ge(dt_t, 1)
            dve.tensor_copy(p_, bank[6][:, 0:256]).then_inc(dt_v, 1)
            dve.wait_ge(dt_v, 6)
            TT(st1, bank[7][:, 0:256], p_, ALU.subtract).then_inc(dt_v, 1)
            dve.wait_ge(dt_e, 4)
            TT(eE[:, :, :], eE[:, :, :], dt_[:, :, :], ALU.mult).then_inc(dt_x, 1)
            for g in range(N_GROUPS):
                for k in range(SLOTS):
                    scan(g, k)
            for g in range(N_GROUPS):
                dve.wait_ge(gn_rms, g + 1)
                dve.reciprocal(ssg[g], ssg[g]).then_inc(gn_rstd, 1)
                dve.wait_ge(gn_rstd, g + 1)
                for c in range(4):
                    k = 4 * g + c
                    STT(gy[:, k, :], gy[:, k, :], cols[:, V_SNORM + k:V_SNORM + k + 1], ssg[g], ALU.mult, ALU.mult
                        ).then_inc(gf_v, 1)
                dve.wait_ge(gf_hi, g + 1)
                TT(xl16[:, 4 * g:4 * g + 4, :], gy[:, 4 * g:4 * g + 4, :], xh16[:, 4 * g:4 * g + 4, :].bitcast(F32),
                   ALU.subtract).then_inc(gf_done, 1)
            for i in range(16):
                lo_to(2 * S_SSMOUT + i + 1 + SPL)
            post(8)
            post(9)
            norm_a(12)
            norm_a(13)
            norm_b(12)
            norm_b(13)

            dve.memset(yout[:, :, :], 0.0).then_inc(cmb_add, 1)
            dve.wait_ge(lg_t, 1)
            own(dve.tensor_copy(lg[:, :, :], v3(bank[4][:, 0:16], 2)))
            for b in range(2):
                own(dve.max(top[:, b, :], lg[:, b, :]))
                own(dve.max_index(idx8[:, b, :], top[:, b, :], lg[:, b, :]))
            own(dve.tensor_copy(idxf[:, :, :], idx8[:, :, :]))
            for b in range(2):
                TS(sel1[:, b, :], iota8, idxf[:, b, 0:1], None, ALU.is_equal)
                own(TS(sel2[:, b, :], iota8, idxf[:, b, 1:2], None, ALU.is_equal))
            TT(mask[:, :, :], sel1[:, :, :], sel2[:, :, :], ALU.add).then_inc(rt_v, 1)
            TT(gd, top[:, :, 1], top[:, :, 0], ALU.subtract).then_inc(rt_v, 1)
            dve.wait_ge(rt_e, 1)
            own(TS(gs, ge, 1.0, None, ALU.add))
            own(dve.reciprocal(g1, gs))
            own(TT(g2, ge, g1, ALU.mult))
            for b in range(2):
                own(TS(sel1[:, b, :], sel1[:, b, :], g1[:, b:b + 1], None, ALU.mult))
                own(STT(comb[:, b, :], sel2[:, b, :], g2[:, b:b + 1], sel1[:, b, :], ALU.mult, ALU.add))
            dve.wait_ge(rt_t, 1)
            own(STT(posm[:, :, :], mask[:, :, :], -1000.0, v3(bank[5][:, 0:16], 2), ALU.mult, ALU.add))
            own(TS(posm[:, :, :], posm[:, :, :], 1000.0, None, ALU.add))
            own(TS(posm2[:, :, :], posm[:, :, :], -float(CAP), None, ALU.add))
            dve.tensor_copy(cnt[:, :], bank[5][:, 16:24]).then_inc(rt_done, 1)

            def slots(e, it, pm):
                for b in range(2):
                    i = TS(slot1[:, b, :], iota, pm[:, b, bass.ds(e, 1)], None, ALU.is_equal)
                i.then_inc(slot_ready, 1)

            def gather_split(it):
                dve.wait_ge(gat_mod, it + 1)
                dve.tensor_copy(xh[:, :, 0:P], v3(mt32, KC)).then_inc(gat_hi, 1)
                dve.wait_ge(gat_hi, it + 1)
                TT(xl[:, :, 0:P], v3(mt32, KC), xh[:, :, 0:P].bitcast(F32), ALU.subtract).then_inc(gat_lo, 1)

            def expert(e, it, wrap):
                def look(i):
                    if i + SPL < MOE_PIECES or wrap:
                        lo_moe(i + SPL, it)

                def at_step(j):
                    if j == 1:
                        dve.wait_ge(slot_ready, it + 1)
                        for b in range(2):
                            i = TS(slotg[:, b, :], slot1[:, b, :], comb[:, b, bass.ds(e, 1)], None, ALU.mult)
                        i.then_inc(gs_ready, 1)
                    if j == MOE_STEPS // 2 and wrap:
                        slots(e + 1, it + 1, posm)
                    if j == MOE_STEPS and wrap:
                        gather_split(it + 1)

                swiglu(S_MOE, it, 1, MOE_STEPS, pos_moe, C_MOE, T_MOE, msg, mhb, look, at_step)
                dve.wait_ge(piece_used, P_MOE + (it + 1) * MOE_PIECES)
                dve.tensor_copy(yexp[:, 512:1024], bank[1][:, :]).then_inc(y_evac, 1)
                for b in range(2):
                    for half in range(2):
                        i = 2 * b + half
                        dve.wait_ge(cmb_t, 4 * it + i + 1)
                        dve.wait_ge(cmb_add, 4 * it + i + 1)
                        o = yout[:, b, half * 512:(half + 1) * 512]
                        TT(o, o, bank[2 + half][:, :], ALU.add).then_inc(cmb_add, 1)

            slots(0, 0, posm)
            gather_split(0)
            with dve.Fori(0, N_EXPERTS - 1) as e:
                expert(e, e, True)
            expert(N_EXPERTS - 1, N_EXPERTS - 1, False)
            with dve.Fori(0, N_EXPERTS) as e:
                n = dve.value_load(cnt[0:1, bass.ds(e, 1)], min_val=0, max_val=2 * P)
                with dve.If(n > CAP):
                    slots(e, e + N_EXPERTS, posm2)
                    for i in range(SPL):
                        lo_moe(i, e + N_EXPERTS)
                    gather_split(e + N_EXPERTS)
                    expert(e, e + N_EXPERTS, False)
                with dve.Else():
                    it = e + N_EXPERTS
                    for s, before, per in ((lo_ready, P_MOE + it * MOE_PIECES, MOE_PIECES),
                                           (h_done, C_MOE + it * MOE_STEPS, MOE_STEPS),
                                           (ht_lo, T_MOE + it * MOE_STEPS, MOE_STEPS),
                                           (slot_ready, it, 1), (gs_ready, it, 1), (gat_hi, it, 1), (gat_lo, it, 1),
                                           (y_evac, Y_MOE + 2 * it, 1), (cmb_add, 4 * it + 1, 4)):
                        dve.wait_ge(s, before)
                        dve.sem_inc(s, per)
            post(10)
            post(11)


_INS = ["x", "c", "ctx", "c_ctx", "ada_w", "ada_b", "norm_w", "mix_in_w", "q_norm_w", "k_norm_w", "mix_out_w",
        "ffn_gu_w", "ffn_down_w", "ssm_in_w", "ssm_conv_w", "ssm_conv_b", "ssm_dt_bias", "ssm_a_log", "ssm_d",
        "ssm_norm_w", "ssm_out_w", "router_w", "moe_gu_w", "moe_down_w"]


def kernel(**inputs):
    import numpy as _np
    import concourse.bacc as _bacc
    from concourse import mybir as _mybir
    from concourse.bass_utils import run_bass_kernel_spmd as _run

    nc = _bacc.Bacc("TRN2", target_bir_lowering=False, num_devices=1)
    const, first = shape_constants()
    arrays, aps = {}, {}
    for name in _INS + ["const", "first"]:
        a = _np.ascontiguousarray({"const": const, "first": first}[name] if name in ("const", "first") else inputs[name])
        arrays[f"in_{name}_dram"] = a
        aps[name] = nc.dram_tensor(f"in_{name}_dram", a.shape, _mybir.dt.from_np(a.dtype), kind="ExternalInput").ap()
    out = nc.dram_tensor("out_0_dram", (1, SEQ, D_MODEL), F32, kind="ExternalOutput").ap()
    build(nc, aps, out)
    r = _run(nc, [arrays], core_ids=[0])
    return r.results[0]["out_0_dram"]
```

```python
from contextlib import ExitStack

import numpy as np
import concourse.bass as bass
from concourse import mybir

P = 128
D_MODEL = 1024
SEQ = 256
CTX_LEN = 256
GRID_W = 64
F_GROUPS = 4
F_GROUP_DIM = D_MODEL // 8
F_WIDTH = F_GROUPS * F_GROUP_DIM
HEAD_DIM = 64
N_HEADS = 8
N_KV = 2
Q_WIDTH = N_HEADS * HEAD_DIM
MIX_IN = F_WIDTH + Q_WIDTH + 2 * N_KV * HEAD_DIM
ROPE_THETA = 10000.0
D_INNER = 2 * D_MODEL
N_SSM_HEADS = 32
N_GROUPS = 4
HPG = 8
D_STATE = 128
D_CONV = 5
CONV_DIM = D_INNER + 2 * N_GROUPS * D_STATE
SSM_IN = D_INNER + CONV_DIM + 2 * N_SSM_HEADS
D_FF = 2816
N_EXPERTS = 8
D_FF_EXPERT = 3584
EPS = 1e-6

KC = D_MODEL // P
LAT, CTX = (0, 1), (2, 3)
NBLK = 4

UNIT = 2048
PIECE = 1024
RAW = 6
SPL = 4
UCOL = 256

ACOL = 2 * UCOL
N_ADA = 2 * 6 * D_MODEL // ACOL
ADA_FIRST = 2 * D_MODEL // ACOL
U_MIXIN = MIX_IN // UCOL
U_MIXOUT = D_MODEL // UCOL
FFN_STEPS = D_FF // UCOL
MOE_STEPS = D_FF_EXPERT // UCOL
MOE_UNITS = 3 * MOE_STEPS
MOE_PIECES = 2 * MOE_UNITS
GROUP_UNITS = 5
S_MIXIN = 0
S_MIXOUT = S_MIXIN + U_MIXIN
S_FFN = S_MIXOUT + U_MIXOUT
S_DT = S_FFN + 2 * 3 * FFN_STEPS
S_GRP = S_DT + 1
S_SSMOUT = S_GRP + N_GROUPS * GROUP_UNITS
S_MOE = S_SSMOUT + 2 * U_MIXOUT

CAP = 128

C_ID, C_ONE, C_TF, C_TB, C_ST, C_IO, C_I8, C_SEL = 0, 128, 256, 384, 512, 640, 768, 776
N_CONST = 778
V_ADAB, V_CONVB, V_NORM, V_SNORM, V_C, V_CC, V_CONVW = 0, 96, 120, 184, 200, 208, 216
N_COLS = 336

F32 = mybir.dt.float32
F32R = mybir.dt.float32r
I32 = mybir.dt.int32
U32 = mybir.dt.uint32
ALU = mybir.AluOpType
ACT = mybir.ActivationFunctionType
AX = mybir.AxisListType


def swiglu_order(n):
    order = []
    for j in range(n + 2):
        if j < n:
            order += [("g", j), ("u", j)]
        if j >= 2:
            order.append(("d", j - 2))
    return order


def shape_constants():
    i = np.arange(P)
    c = np.zeros((P, N_CONST), np.float32)
    c[:, C_ID:C_ID + P] = np.eye(P)
    c[:, C_ONE:C_ONE + P] = 1.0
    c[:, C_TF:C_TF + P] = i[:, None] <= i[None, :]
    c[:, C_TB:C_TB + P] = i[:, None] >= i[None, :]
    c[:, C_ST:C_ST + P] = i[:, None] < i[None, :]
    c[:, C_IO:C_IO + P] = i[None, :]
    c[:, C_I8:C_I8 + 8] = np.arange(8)[None, :]
    for g in range(4):
        c[32 * g, C_SEL] = 1.0
        c[32 * g + 1, C_SEL + 1] = 1.0
    n = np.arange(SEQ)
    ang = 2 * np.pi * ((n[:, None] * n[None, :]) % SEQ) / SEQ
    s = 1.0 / np.sqrt(float(SEQ * F_GROUP_DIM))
    pos = np.concatenate([np.cos(ang) * s, np.sin(ang) * s], axis=1)
    pos = pos.reshape(2, P, 2 * SEQ).transpose(1, 0, 2).reshape(P, 4 * SEQ)
    angc = 2 * np.pi * ((i[:, None] * i[None, :]) % P) / P
    ch = np.concatenate([np.cos(angc), -np.sin(angc)], axis=1)
    t = np.arange(SEQ)
    freqs = np.float32(ROPE_THETA) ** (-np.arange(0, HEAD_DIM // 2, 2, dtype=np.float32) / np.float32(HEAD_DIM // 2))
    rang = np.concatenate([(t // GRID_W).astype(np.float32)[:, None] * freqs,
                           (t % GRID_W).astype(np.float32)[:, None] * freqs], axis=1).astype(np.float32)
    rope = np.stack([np.cos(rang), np.sin(rang)], axis=0).astype(np.float32)
    rope = rope.reshape(2, 2, P, 32).transpose(2, 0, 1, 3).reshape(P, 128)
    first = np.concatenate([pos, ch, rope], axis=1).astype(np.float32)
    return c, first


N_FIRST = 4 * SEQ + 2 * P + 128


def build(nc, A, out):
    es = ExitStack()
    with es:
        def sb(name, shape, dt=F32):
            return es.enter_context(nc.sbuf_tensor(name, shape, dt))

        def sem(name):
            return es.enter_context(nc.semaphore(name))

        bank = [es.enter_context(nc.psum_tensor(f"bank{i}", [P, 512], F32)) for i in range(8)]

        raw = sb("raw", [P, RAW, UNIT])
        hi = sb("hi", [P, SPL, PIECE], F32R)
        lo = sb("lo", [P, SPL, PIECE], F32R)
        xh_t = sb("xh_t", [P, KC * 512], F32R)
        xl_t = sb("xl_t", [P, KC * 512], F32R)
        hth = sb("hth", [P, 2, 512], F32R)
        htl = sb("htl", [P, 2, 512], F32R)
        xres = sb("xres", [P, 2, D_MODEL])
        con = sb("con", [P, N_CONST])
        cols = sb("cols", [P, N_COLS])
        ada = sb("ada", [P, 2, 48, 2])
        moda = sb("moda", [P, 4, KC, 2])
        gatec = sb("gatec", [P, 4, KC, 2])
        sc = sb("sc", [P, KC, 32])
        ss = sb("ss", [P, 32])
        rms = sb("rms", [P, 32])
        rstd = sb("rstd", [P, 32])
        epsc = sb("epsc", [P, 1])
        AR = 18400
        ar = sb("ar", [P, AR])

        xh = xh_t[:, :].rearrange("p (k n) -> p k n", k=KC)
        xl = xl_t[:, :].rearrange("p (k n) -> p k n", k=KC)
        xh16 = xh_t[:, :].rearrange("p (k n) -> p k n", k=16)
        xl16 = xl_t[:, :].rearrange("p (k n) -> p k n", k=16)

        ident = con[:, C_ID:C_ID + P]
        ones = con[:, C_ONE:C_ONE + P]
        tri = [con[:, C_TF:C_TF + P], con[:, C_TB:C_TB + P]]
        strict = con[:, C_ST:C_ST + P]
        iota = con[:, C_IO:C_IO + P]
        iota8 = con[:, C_I8:C_I8 + 8]
        sel = con[:, C_SEL:C_SEL + 2]

        class Arena:
            def __init__(self, base=0, mem=ar, size=AR):
                self.at, self.mem, self.size = base, mem, size

            def take(self, n):
                a = self.mem[:, self.at:self.at + n]
                self.at += n
                assert self.at <= self.size, self.at
                return a

        def v3(a, k):
            return a.rearrange("p (k n) -> p k n", k=k)

        m0 = Arena()
        xctx = v3(m0.take(2 * D_MODEL), 2)
        base0 = m0.at
        xn = [m0.take(D_MODEL) for _ in range(2)]
        t32 = m0.take(D_MODEL)
        t32b = ar[:, AR - D_MODEL:]
        px = v3(m0.take(NBLK * MIX_IN), NBLK)
        first = m0.take(N_FIRST)
        dpos = v3(first[:, 0:4 * SEQ], 2)
        dch = v3(first[:, 4 * SEQ:4 * SEQ + 2 * P], 2)
        rope = first[:, 4 * SEQ + 2 * P:N_FIRST].rearrange("p (t b n) -> p t b n", t=2, b=2)
        qkw = v3(m0.take(2 * HEAD_DIM), 2)
        part = m0.take(ACOL)
        vec_at = m0.at
        m1 = Arena(base0)
        t1s = [m1.take(512) for _ in range(2)]
        prob = [m1.take(512) for _ in range(2)]
        pts = [m1.take(512) for _ in range(2)]
        assert m1.at <= base0 + 3 * D_MODEL
        m2 = Arena(vec_at)
        qT = m2.take(NBLK * 512).rearrange("p (b c n) -> p b c n", b=NBLK, c=4)
        kT = v3(m2.take(2 * 512), 2)
        qsq = m2.take(640)
        rtmp = m2.take(4 * 320)
        kdup = v3(rtmp[:, 0:NBLK * 256], NBLK)
        qss = v3(m2.take(40), 4)
        qrms = v3(m2.take(40), 4)
        qrs = v3(m2.take(40), 4)
        mx = m2.take(32)
        nmx = m2.take(32)
        rsum = m2.take(32)
        rinv = m2.take(32)
        m3 = Arena(vec_at)
        va, vb, vc = m3.take(P), m3.take(P), m3.take(P)
        m4 = Arena(base0 + 3 * D_MODEL)
        y = v3(m4.take(NBLK * D_MODEL), NBLK)
        m5 = Arena(m4.at)
        grow = [m5.take(D_MODEL) for _ in range(4)]
        sg = [m5.take(UCOL) for _ in range(2)]
        hb = [m5.take(UCOL) for _ in range(2)]
        ptmp = m5.take(D_MODEL)
        pjunk = m5.take(D_MODEL)
        assert m5.at <= AR - D_MODEL

        s0 = Arena(0)
        gy = v3(s0.take(16 * SEQ), 16)
        dt_ = v3(s0.take(256), 4)
        dta = v3(s0.take(256), 4)
        acum = v3(s0.take(256), 4)
        cdec = v3(s0.take(256), 4)
        eE = v3(s0.take(256), 4)
        st1, st2, st3 = s0.take(256), s0.take(256), s0.take(256)
        dbias, arow = s0.take(64), s0.take(64)
        drow = s0.take(32)
        dcol = s0.take(16)
        sx = Arena(0, raw[:, RAW // 2:, :].rearrange("p a b -> p (a b)"), RAW // 2 * UNIT)
        btok = [v3(s0.take(512), 4), v3(sx.take(512), 4)]
        xtok = [v3(s0.take(4 * 512), 4) for _ in range(2)]
        cbm = [a.take(512).rearrange("p (d b n) -> p d b n", d=2, b=2) for a in (s0, sx)]
        cpad = [s0.take(2 * 260).rearrange("p (s n) -> p s n", s=2) for _ in range(2)]
        cacc = [s0.take(512) for _ in range(2)]
        xE = [s0.take(512), sx.take(512)]
        xdt = [s0.take(512), sx.take(512)]
        assert sx.at == UNIT
        xs = sx.take(3 * 4 * SEQ).rearrange("p (s c n) -> p s c n", s=3, c=4)
        cT = [s0.take(256), sx.take(256)]
        bT = s0.take(512)
        mt = [s0.take(512) for _ in range(2)]
        dtr = mt[0][0:64, :]
        ce = [s0.take(512) for _ in range(2)]
        hst = [s0.take(512) for _ in range(2)]
        o0 = Arena(0)
        yout = v3(o0.take(2 * D_MODEL), 2)
        mgrow = [o0.take(D_MODEL) for _ in range(2)]
        mptmp = o0.take(D_MODEL)
        mpjunk = o0.take(D_MODEL)
        mxn = [o0.take(D_MODEL) for _ in range(2)]
        mt32, mt32b = o0.take(D_MODEL), o0.take(D_MODEL)
        yexp = o0.take(D_MODEL)
        msg = [o0.take(UCOL) for _ in range(2)]
        mhb = [o0.take(UCOL) for _ in range(2)]
        slot1 = v3(o0.take(256), 2)
        lgT = o0.take(256)
        rwh, rwl = (v3(a[:, 0, 0:64], 8) for a in (hth, htl))
        slotg = v3(o0.take(256), 2)
        gT = v3(o0.take(256), 2)
        rw = v3(o0.take(64), 8)
        lg = v3(o0.take(16), 2)
        top = v3(o0.take(16), 2)
        idxf = v3(o0.take(16), 2)
        sel1 = v3(o0.take(16), 2)
        sel2 = v3(o0.take(16), 2)
        comb = v3(o0.take(16), 2)
        mask = v3(o0.take(16), 2)
        posm = v3(o0.take(16), 2)
        posm2 = v3(o0.take(16), 2)
        gd, ge, gs, g1, g2 = (o0.take(2) for _ in range(5))
        most_f = o0.take(1)
        idx8 = sb("idx8", [P, 2, 8], U32)
        cnt = sb("cnt", [P, 9], I32)

        raw_landed = [sem(f"raw_landed{i}") for i in range(RAW)]
        hi_ready, lo_ready, piece_used = sem("hi_ready"), sem("lo_ready"), sem("piece_used")
        ada_used, ada_part, ada_col, ada_done = (sem(n) for n in ("ada_used", "ada_part", "ada_col", "ada_done"))
        ld_x, ld_ctx, ld_con, ld_first, ld_vec, ld_qkw, ld_ssm, ld_rw = (
            sem(n) for n in ("ld_x", "ld_ctx", "ld_con", "ld_first", "ld_vec", "ld_qkw", "ld_ssm", "ld_rw"))
        zeroed, vec_t, vec_cols, sc_ready, eps_ready = (
            sem(n) for n in ("zeroed", "vec_t", "vec_cols", "sc_ready", "eps_ready"))
        mod_ready = sem("mod_ready")
        n_ss, n_rms, n_rstd, xn_ready, xt_done, xmod_done, xsplit_hi, xsplit_done = (
            sem(n) for n in ("n_ss", "n_rms", "n_rstd", "xn_ready", "xt_done", "xmod_done", "xsplit_hi", "xsplit_done"))
        lin_evac = sem("lin_evac")
        dft_t1, dft_t1s, dft_out, dft_hi, dft_lo = (sem(n) for n in ("dft_t1", "dft_t1s", "dft_out", "dft_hi", "dft_lo"))
        qk_ss, qk_rms, qk_ready, qk_t, qk_tc = (
            sem(n) for n in ("qk_ss", "qk_rms", "qk_ready", "qk_t", "qk_tc"))
        at_s, at_m, at_mx, at_exp, at_r, at_nrm, at_t, at_pt, at_pv, at_oh, at_ol = (
            sem(n) for n in ("at_s", "at_m", "at_mx", "at_exp", "at_r", "at_nrm", "at_t", "at_pt", "at_pv", "at_oh", "at_ol"))
        grow_t, grow_ready = sem("grow_t"), sem("grow_ready")
        po_ss, po_rms, po_rstd, po_t, po_done = (sem(n) for n in ("po_ss", "po_rms", "po_rstd", "po_t", "po_done"))
        sil_done, h_done, ht_t, ht_hi, ht_lo, y_evac = (
            sem(n) for n in ("sil_done", "h_done", "ht_t", "ht_hi", "ht_lo", "y_evac"))
        dt_rows, dt_cols = sem("dt_rows"), sem("dt_cols")
        dt_v, dt_e, dt_a, dt_t, dt_x = (sem(n) for n in ("dt_v", "dt_e", "dt_a", "dt_t", "dt_x"))
        pr_copy, cv_v, cv_acc, cv_out, tr_t, tr_copy, cb_t, cb_m = (
            sem(n) for n in ("pr_copy", "cv_v", "cv_acc", "cv_out", "tr_t", "tr_copy", "cb_t", "cb_m"))
        zs_done = sem("zs_done")
        xe_ready, st_t, st_done = (sem(n) for n in ("xe_ready", "st_t", "st_done"))
        xdt_ready, bc_t, ce_exp, sg_ready, mt_exp, mt_ready, ce_ready, yy_t = (
            sem(n) for n in ("xdt_ready", "bc_t", "ce_exp", "sg_ready", "mt_exp", "mt_ready", "ce_ready", "yy_t"))
        gy_v, gy_done, gq_done, gn_t, gn_copy, gn_rms, gn_rstd, gf_v, gf_hi, gf_done = (
            sem(n) for n in ("gy_v", "gy_done", "gq_done", "gn_t", "gn_copy", "gn_rms", "gn_rstd", "gf_v", "gf_hi", "gf_done"))
        lg_t, rt_v, rt_e, rt_t, rt_done = (sem(n) for n in ("lg_t", "rt_v", "rt_e", "rt_t", "rt_done"))
        slot_ready, gat_t, gat_mod, gat_hi, gat_lo, gs_ready, gs_t, gT_ready, cmb_t, cmb_add = (
            sem(n) for n in ("slot_ready", "gat_t", "gat_mod", "gat_hi", "gat_lo", "gs_ready", "gs_t", "gT_ready", "cmb_t", "cmb_add"))
        rw_hi, rw_lo, lg_rows, lg_copy = (sem(n) for n in ("rw_hi", "rw_lo", "lg_rows", "lg_copy"))
        stored = sem("stored")
        vstep, astep = sem("vstep"), sem("astep")
        ssg = [st1, st2, st3, sc[:, :, :].rearrange("p k n -> p (k n)")]

        def unit_of_split(s):
            return 2 * ADA_FIRST + s if s < S_MIXOUT else s + 2 * N_ADA + U_MIXIN % 2

        def unit_of_ada(a):
            return 2 * a if a < ADA_FIRST else 2 * a + U_MIXIN + U_MIXIN % 2

        U_MOE = unit_of_split(S_MOE)

        def wcols(w, c0, n):
            return w.rearrange("(t p) n -> p t n", p=P)[:, :, c0:c0 + n]

        def slot(u):
            first_u, end_u = unit_of_split(S_DT), unit_of_split(S_SSMOUT)
            if u < first_u:
                return u % RAW
            return (u - first_u) % (RAW // 2) if u < end_u else (u - end_u) % RAW

        def raw_ada(a):
            s = slot(unit_of_ada(a))
            return raw[:, s:s + 2, :].rearrange("p s n -> p (s n)").rearrange("p (t n) -> p t n", t=KC)

        def rawv(u, t):
            return raw[:, slot(u), :].rearrange("p (t n) -> p t n", t=t)

        order_ffn = swiglu_order(FFN_STEPS)
        order_moe = swiglu_order(MOE_STEPS)

        def pos_of(order):
            return {k: i for i, k in enumerate(order)}

        pos_ffn, pos_moe = pos_of(order_ffn), pos_of(order_moe)

        xblk = [xres[:, 0, :], xres[:, 1, :], xctx[:, 0, :], xctx[:, 1, :]]
        NORMS = ([(0, b // 2, b) for b in range(4)] + [(1, b // 2, b) for b in range(4)] +
                 [(2, b // 2, b) for b in range(4)] + [(3, 0, b) for b in range(2)])
        N_MLP, N_SSM, N_MOE = 4, 8, 12
        POSTS = ([(0, b // 2, b) for b in range(4)] + [(1, b // 2, b) for b in range(4)] +
                 [(2, 0, b) for b in range(2)] + [(3, 0, b) for b in range(2)])
        GROWS = [(0, 0), (0, 1), (1, 0), (1, 1), (2, 0), (3, 0)]

        def grow_tile(r):
            return grow[r] if r < 4 else mgrow[r - 4]

        def grow_bank(r, k):
            return bank[(0 if r in (2, 3) else 4) + 2 * (r % 2) + k]

        def grow_of(n):
            return GROWS.index(POSTS[n][:2])

        def post_src(n):
            b = POSTS[n][2]
            return y[:, b, :] if n < 8 else yout[:, b, :]

        def xn_of(n):
            return mxn[n % 2] if n >= N_MOE else xn[n % 2]

        def t32_of(n):
            return (mt32, mt32b)[n % 2] if n >= N_MOE else (t32, t32b)[n % 2]

        def mod_cols(m, s):
            l, w = m // 2, m % 2
            return moda[:, m, :, s], ada[:, l, 24 * w:24 * w + KC, s]

        AT_SCALE = HEAD_DIM ** -0.5
        ITERS = [("dft", i) for i in range(8)] + [("att", i) for i in range(32)]

        def at_info(i):
            s, b, h = i // 16, i // 8, i % 8
            return s, b, h, (0, 4) if s == 0 else (2, 2)

        def qk_banks(b):
            return (bank[0], bank[1]) if b % 2 else (bank[4], bank[5])

        N_PAIRS = len(ITERS) // 2
        assert N_PAIRS == N_ADA - ADA_FIRST

        def pair_of(j):
            return ITERS[2 * j:2 * j + 2] if 0 <= j < N_PAIRS else []

        ssd_idx = [(d, b, q) for d, bs in ((0, (0, 1)), (1, (1, 0))) for b in bs for q in range(2)]
        ssd_states = [(d, k, b) for d, bs in ((0, (2, 3, 0)), (1, (3, 2, 1))) for k, b in enumerate(bs)]
        NQ = len(ssd_idx)
        NST = len(ssd_states)

        SLOTS = 10
        USED = (2, 3, 4, 5, 6, 7, 9, 10, 10, 10)

        def split_by(g, k):
            return 2 * (S_GRP + g * GROUP_UNITS) + (USED[k - 1] if k else 0) + SPL


        LIN_MIXOUT = U_MIXIN * NBLK
        LIN_SSMOUT = LIN_MIXOUT + U_MIXOUT * NBLK
        RT_N = 1

        def is_pair_unit(s):
            return S_GRP <= s < S_SSMOUT and (s - S_GRP) % GROUP_UNITS == 0

        signals = {unit_of_ada(a): 16 for a in range(N_ADA)}
        signals.update({unit_of_split(s): 32 if is_pair_unit(s) else 16 for s in range(S_MOE)})
        landed, total = {}, [0] * RAW
        for u in sorted(signals):
            total[slot(u)] += signals[u]
            landed[u] = total[slot(u)]
        PER_SLOT = 16 * (MOE_UNITS // RAW)

        def landed_moe(i, it):
            return total[slot(U_MOE + i)] + 16 * (i // RAW + 1) + it * PER_SLOT

        P_MOE = 2 * S_MOE
        FFN_N = len(order_ffn)
        J_GATHER = 9
        C_MOE, T_MOE, Y_MOE = 2 * 2 * FFN_STEPS, 2 * FFN_STEPS, 8

        block = es.enter_context(nc.Block())

        @block.sync
        def _(sp):
            sp.dma_start(vb[0:64, :], A["norm_w"].rearrange("i n (k q) -> (i n k) q", q=P)).then_inc(ld_vec, 16)
            sp.dma_start(vb[64:80, :], A["ssm_norm_w"].rearrange("i (k q) -> (i k) q", q=P)).then_inc(ld_vec, 16)
            sp.dma_start(vb[80:88, :], A["c"].rearrange("i (k q) -> (i k) q", q=P)).then_inc(ld_vec, 16)
            sp.dma_start(vb[88:96, :], A["c_ctx"].rearrange("(k q) -> k q", q=P)).then_inc(ld_vec, 16)
            sp.dma_start(con[:, :], A["const"]).then_inc(ld_con, 16)
            sp.dma_start(va[0:96, :], A["ada_b"].rearrange("l (c q) -> (l c) q", q=P)).then_inc(ld_vec, 16)
            sp.dma_start(va[96:120, :], A["ssm_conv_b"].rearrange("l (c q) -> (l c) q", q=P)).then_inc(ld_vec, 16)
            sp.dma_start(vc[0:120, :], A["ssm_conv_w"].rearrange("l t (c q) -> (l t c) q", q=P)).then_inc(ld_vec, 16)

            owner = {}

            def free(u):
                if slot(u) in owner:
                    kind, n = owner[slot(u)]
                    if kind == "ada":
                        sp.wait_ge(ada_used, n + 1)
                    else:
                        sp.wait_ge(lo_ready, 2 * (n + 1))

            def load(u, kind, n, dst, src):
                free(u)
                sp.dma_start(dst, src).then_inc(raw_landed[slot(u)], 16)
                owner[slot(u)] = (kind, n)

            def load_ada(a0, a1):
                for a in range(a0, a1):
                    l, c = divmod(a, N_ADA // 2)
                    u = unit_of_ada(a)
                    free(u + 1)
                    load(u, "ada", a, raw_ada(a), wcols(A["ada_w"][l], c * ACOL, ACOL))
                    owner[slot(u + 1)] = ("ada", a)

            def load_cols(s, w, c0, n=UCOL):
                u = unit_of_split(s)
                load(u, "split", s, rawv(u, 8)[:, :, 0:n], wcols(w, c0, n))

            load_ada(0, 1)
            sp.dma_start(xres[:, :, :], A["x"].rearrange("o (b p) n -> p (o b) n", p=P)).then_inc(ld_x, 16)
            load_ada(1, 2)
            sp.dma_start(xctx, A["ctx"].rearrange("o (b p) n -> p (o b) n", p=P)).then_inc(ld_ctx, 16)
            load_ada(2, ADA_FIRST)
            for i in range(U_MIXIN):
                load_cols(S_MIXIN + i, A["mix_in_w"][0], i * UCOL)
            sp.dma_start(first, A["first"]).then_inc(ld_first, 16)
            sp.dma_start(qkw[:, 0, :], A["q_norm_w"][0].partition_broadcast(P)).then_inc(ld_qkw, 16)
            sp.dma_start(qkw[:, 1, :], A["k_norm_w"][0].partition_broadcast(P)).then_inc(ld_qkw, 16)
            load_ada(ADA_FIRST, N_ADA)
            for i in range(U_MIXOUT):
                load_cols(S_MIXOUT + i, A["mix_out_w"][0], i * UCOL)
            gu, dn = A["ffn_gu_w"][0], A["ffn_down_w"][0]
            for ps in range(2):
                for i, (k, j) in enumerate(order_ffn):
                    s = S_FFN + ps * FFN_N + i
                    if k == "d":
                        u = unit_of_split(s)
                        load(u, "split", s, rawv(u, 2),
                             dn[j * UCOL:(j + 1) * UCOL, :].rearrange("(t p) n -> p t n", p=P))
                    else:
                        load_cols(s, gu, j * UCOL + (D_FF if k == "u" else 0))
            w_in = A["ssm_in_w"][0]
            x0, b0, c0 = D_INNER, 2 * D_INNER, 2 * D_INNER + N_GROUPS * D_STATE
            load_cols(S_DT, w_in, D_INNER + CONV_DIM, 2 * N_SSM_HEADS)
            for g in range(N_GROUPS):
                s = S_GRP + g * GROUP_UNITS
                u = unit_of_split(s)
                load(u, "split", s, rawv(u, 8)[:, :, 0:P], wcols(w_in, b0 + g * P, P))
                sp.dma_start(rawv(u, 8)[:, :, P:2 * P], wcols(w_in, c0 + g * P, P)).then_inc(raw_landed[slot(u)], 16)
                for i in range(2):
                    load_cols(s + 1 + i, w_in, x0 + g * 512 + i * UCOL)
                for i in range(2):
                    load_cols(s + 3 + i, w_in, g * 512 + i * UCOL)
                if g == 0:
                    sp.wait_ge(xsplit_done, N_SSM + 4)
                    for dst, src in ((dbias, A["ssm_dt_bias"].rearrange("l d h -> (l d h)")),
                                     (arow, A["ssm_a_log"].rearrange("l d h -> (l d h)")),
                                     (drow, A["ssm_d"][0])):
                        sp.dma_start(dst, src.partition_broadcast(P)).then_inc(ld_ssm, 16)
            for i in range(2 * U_MIXOUT):
                kh, q = divmod(i, U_MIXOUT)
                if i == RAW // 2:
                    sp.wait_ge(yy_t, N_GROUPS * NQ)
                if i == RAW // 2 + 1:
                    sp.wait_ge(gn_t, N_GROUPS)
                load_cols(S_SSMOUT + i, A["ssm_out_w"][0][kh * D_MODEL:(kh + 1) * D_MODEL, :], q * UCOL)
            sp.wait_ge(gf_done, 4)
            sp.dma_start(rw, A["router_w"][0].rearrange("(t p) n -> p t n", p=P)).then_inc(ld_rw, 16)

            def expert_weights(e, it):
                gu = A["moe_gu_w"][0][bass.ds(e, 1)].rearrange("o k n -> (o k) n")
                dn = A["moe_down_w"][0][bass.ds(e, 1)].rearrange("o k n -> (o k) n")
                for i, (k, j) in enumerate(order_moe):
                    u = U_MOE + i
                    sp.wait_ge(lo_ready, it * MOE_PIECES + 2 * (S_MOE + i - RAW + 1))
                    if k == "d":
                        sp.dma_start(rawv(u, 2), dn[j * UCOL:(j + 1) * UCOL, :].rearrange("(t p) n -> p t n", p=P)
                                     ).then_inc(raw_landed[slot(u)], 16)
                    else:
                        sp.dma_start(rawv(u, 8), wcols(gu, j * UCOL + (D_FF_EXPERT if k == "u" else 0), UCOL)
                                     ).then_inc(raw_landed[slot(u)], 16)

            with sp.Fori(0, N_EXPERTS) as e:
                expert_weights(e, e)
            sp.wait_ge(rt_done, RT_N)
            most = sp.value_load(cnt[0:1, 8:9], min_val=0, max_val=2 * P)
            with sp.If(most > CAP):
                with sp.Fori(0, N_EXPERTS) as e:
                    n = sp.value_load(cnt[0:1, bass.ds(e, 1)], min_val=0, max_val=2 * P)
                    with sp.If(n > CAP):
                        expert_weights(e, e + N_EXPERTS)
                    with sp.Else():
                        for k in range(RAW):
                            s = raw_landed[slot(U_MOE + k)]
                            sp.wait_ge(s, landed_moe(k, e + N_EXPERTS) - 16)
                            sp.sem_inc(s, PER_SLOT)
            for b in range(2):
                sp.wait_ge(po_done, 11 + b)
                sp.dma_start(out.rearrange("o (b p) n -> p (o b) n", p=P)[:, b, :], xres[:, b, :]).then_inc(stored, 16)
            sp.wait_ge(stored, 32)

        @block.gpsimd
        def _(pool):
            pool.memset(sc[:, :, :], 0.0).then_inc(zeroed, 1)
            pool.memset(epsc[:, :], EPS).then_inc(eps_ready, 1)
            pool.wait_ge(xsplit_done, N_SSM + 4)
            for t in cpad:
                pool.memset(t, 0.0).then_inc(zeroed, 1)
            for g in range(N_GROUPS):
                def scaled_x(dst, blk, scale, d, done):
                    a = d * N_SSM_HEADS + g * HPG
                    pool.tensor_tensor(dst.rearrange("p (h q) -> p h q", h=HPG),
                                       xtok[g % 2][:, blk, :].rearrange("p (h q) -> p h q", h=HPG),
                                       scale[:, blk, a:a + HPG].unsqueeze(2).to_broadcast((P, HPG, 64)),
                                       ALU.mult).then_inc(done, 1)

                pool.wait_ge(dt_x, 1)
                pool.wait_ge(tr_copy, 5 * (g + 1))
                pool.wait_ge(cv_out, 6 * (g + 1))

                def xE_(k):
                    d, _, blk = ssd_states[k]
                    n = g * NST + k
                    if n >= 2:
                        pool.wait_ge(st_t, n - 1)
                    scaled_x(xE[k % 2], blk, eE, d, xe_ready)

                def xdt_(m):
                    d, b, _ = ssd_idx[2 * m]
                    n = g * NQ // 2 + m
                    if n >= 2:
                        pool.wait_ge(yy_t, 2 * (n - 1))
                    scaled_x(xdt[m % 2], b, dt_, d, xdt_ready)

                def ce_(q):
                    d, b, _ = ssd_idx[q]
                    pool.wait_ge(ce_exp, g * NQ + q + 1)
                    pool.tensor_tensor(v3(ce[q % 2], 4), v3(ce[q % 2], 4),
                                       cT[g % 2][:, b * P:(b + 1) * P].unsqueeze(1).to_broadcast((P, 4, P)),
                                       ALU.mult).then_inc(ce_ready, 1)

                xE_(0)
                xE_(1)
                xdt_(0)
                xdt_(1)
                ce_(0)
                ce_(1)
                xE_(2)
                ce_(2)
                xE_(3)
                xdt_(2)
                ce_(3)
                xE_(4)
                ce_(4)
                xdt_(3)
                ce_(5)
                xE_(5)
                ce_(6)
                ce_(7)

            pool.wait_ge(po_done, 10)
            pool.memset(yout[:, :, :], 0.0).then_inc(cmb_add, 1)

        @block.tensor
        def _(pe):
            mm = pe.matmul

            def tok3(o, a_hi, a_lo, w_hi, w_lo, first, last, group=True):
                kw = {} if group else {"skip_group_check": True}
                mm(o, a_hi, w_hi, start=first, stop=False, **kw)
                mm(o, a_hi, w_lo, start=False, stop=False, **kw)
                return mm(o, a_lo, w_hi, start=False, stop=last, **kw)

            def wpart(p, t, n, off=0, width=None):
                a = t * n + off
                return hi[:, p % SPL, a:a + (width or n)], lo[:, p % SPL, a:a + (width or n)]

            pe.wait_ge(ld_vec, 16 * 7)
            pe.wait_ge(ld_con, 16)
            for t, n, c in ((vb, 96, 0), (va, 120, 1), (vc, 120, 2)):
                pe.transpose(bank[5 + c][:, 0:n], t[0:n, :], ident[0:n, 0:n]).then_inc(vec_t, 1)

            def ada_a(a):
                u = unit_of_ada(a)
                pe.wait_ge(raw_landed[slot(u)], landed[u])
                if a == 0:
                    pe.wait_ge(sc_ready, 2)
                if a > 0:
                    pe.wait_ge(ada_part, a)
                w = raw_ada(a)
                for t in range(2):
                    for g in range(4):
                        m = mm(bank[6][32 * g:32 * g + 32, :], sc[:, 2 * g + t, :], w[:, 2 * g + t, :],
                               start=(t == 0), stop=(t == 1), tile_position=(0, 32 * g))
                m.then_inc(ada_used, 1)

            def ada_b(a):
                pe.wait_ge(ada_part, a + 1)
                if a > 0:
                    pe.wait_ge(ada_done, a)
                for i in range(ACOL // P):
                    m = mm(bank[7][:, 2 * i:2 * i + 2], part[:, i * P:(i + 1) * P], sel, start=True, stop=True)
                m.then_inc(ada_col, 1)

            pe.wait_ge(vec_cols, 3)
            def norm_t(n):
                pe.wait_ge(xn_ready, n + 1)
                if n >= 2:
                    pe.wait_ge(xmod_done, n - 1)
                for k in range(KC):
                    m = pe.transpose(bank[2 * (n % 2) + k // 4][:, (k % 4) * P:(k % 4 + 1) * P],
                                     xn_of(n)[:, k * P:(k + 1) * P], ident)
                m.then_inc(xt_done, 1)

            def linear(s0, lin0):
                for u in range(U_MIXIN if s0 == S_MIXIN else U_MIXOUT):
                    for h in range(2):
                        p = 2 * (s0 + u) + h
                        pe.wait_ge(lo_ready, p + 1)
                        for b in range(NBLK):
                            if h == 0 and u >= 2:
                                pe.wait_ge(lin_evac, lin0 + (u - 2) * NBLK + b + 1)
                            for t in range(4):
                                k = 4 * h + t
                                m = tok3(bank[(u % 2) * 4 + b][:, 0:UCOL], xh[:, k, b * P:(b + 1) * P],
                                         xl[:, k, b * P:(b + 1) * P], *wpart(p, t, UCOL),
                                         first=(k == 0), last=(k == KC - 1))
                        m.then_inc(piece_used, 1)

            ada_a(0)
            ada_a(1)
            ada_b(0)
            norm_t(0)
            norm_t(1)
            for a in range(2, ADA_FIRST):
                ada_a(a)
                ada_b(a - 1)
            ada_b(ADA_FIRST - 1)
            norm_t(2)
            norm_t(3)
            pe.wait_ge(xsplit_done, 4)
            pe.wait_ge(ada_done, ADA_FIRST)
            linear(S_MIXIN, 0)

            pe.wait_ge(ld_first, 16)
            pe.wait_ge(lin_evac, LIN_MIXOUT)

            def dft_1(i):
                s, g = divmod(i, 4)
                if i >= 2:
                    pe.wait_ge(dft_t1s, i - 1)
                for b in range(2):
                    m = mm(bank[i % 2][:, :], px[:, 2 * s + b, g * P:(g + 1) * P], dpos[:, b, :],
                           start=(b == 0), stop=(b == 1))
                m.then_inc(dft_t1, 1)

            def dft_2(i):
                pe.wait_ge(dft_t1s, i + 1)
                if i >= 2:
                    pe.wait_ge(dft_lo, i - 1)
                o = bank[2 + i % 2][:, 0:SEQ]
                mm(o, dch[:, 0, :], t1s[i % 2][:, 0:SEQ], start=True, stop=False)
                mm(o, dch[:, 1, :], t1s[i % 2][:, SEQ:2 * SEQ], start=False, stop=True).then_inc(dft_out, 1)

            def qk_t_(b):
                pe.wait_ge(qk_ready, b + 1)
                if b == 1:
                    pe.wait_ge(dft_t1s, 8)
                if b >= 2:
                    pe.wait_ge(qk_tc, 2 * (b - 1))
                q_, k_ = qk_banks(b)
                for c in range(4):
                    a = F_WIDTH + c * P
                    pe.transpose(q_[:, c * P:(c + 1) * P], px[:, b, a:a + P], ident)
                for v in range(N_KV):
                    m = pe.transpose(k_[:, v * P:(v + 1) * P], kdup[:, b, v * P:(v + 1) * P], ident)
                m.then_inc(qk_t, 1)

            def att_s(i):
                s, b, h, (k0, nk) = at_info(i)
                if i >= 2:
                    pe.wait_ge(at_exp, i - 1)
                r = (h % 2) * 64
                mm(bank[i % 2][:, 0:nk * P], qT[r:r + 64, b, h // 2, :], kT[r:r + 64, h // 4, k0 % 4 * P:(k0 % 4 + nk) * P],
                   start=True, stop=True).then_inc(at_s, 1)

            def att_t(i):
                nk = at_info(i)[3][1]
                pe.wait_ge(at_nrm, i + 1)
                if i >= 2:
                    pe.wait_ge(at_pt, i - 1)
                for c in range(nk):
                    m = pe.transpose(bank[2 + i % 2][:, c * P:(c + 1) * P], prob[i % 2][:, c * P:(c + 1) * P], ident)
                m.then_inc(at_t, 1)

            def att_pv(pair):
                s, b, h0, (k0, nk) = at_info(pair[0])
                pe.wait_ge(at_pt, pair[1] + 1)
                if h0 == 0 and b >= 2:
                    pe.wait_ge(at_ol, b - 1)
                for c in range(nk):
                    for i in pair:
                        h = at_info(i)[2]
                        r = (h % 2) * 64
                        a = F_WIDTH + Q_WIDTH + (N_KV + h // 4) * 64
                        m = mm(bank[4 + b % 2][r:r + 64, (h // 2) * P:(h // 2 + 1) * P], px[:, k0 + c, a:a + 64],
                               pts[i % 2][:, c * P:(c + 1) * P], start=(c == 0), stop=(c == nk - 1))
                        if c == nk - 1:
                            m.then_inc(at_pv, 1)

            for j in range(N_PAIRS + 1):
                if j == 4:
                    for b in range(NBLK):
                        qk_t_(b)
                    pe.wait_ge(qk_tc, 2 * NBLK)
                for k, i in pair_of(j):
                    (dft_1 if k == "dft" else att_s)(i)
                for k, i in pair_of(j - 1):
                    (dft_2 if k == "dft" else att_t)(i)
                if j >= 1:
                    ada_b(ADA_FIRST + j - 1)
                if j < N_PAIRS:
                    ada_a(ADA_FIRST + j)
                if ("att" in [k for k, _ in pair_of(j - 1)]):
                    att_pv([i for _, i in pair_of(j - 1)])
            pe.wait_ge(at_ol, 4)
            pe.wait_ge(dft_lo, 8)
            pe.wait_ge(ada_done, N_ADA)
            linear(S_MIXOUT, LIN_MIXOUT)

            def grow_(r):
                m_, s = GROWS[r]
                if r >= 4:
                    pe.wait_ge(grow_ready, r - 1)
                for k in range(KC):
                    m = mm(grow_bank(r, k // 4)[:, (k % 4) * P:(k % 4 + 1) * P],
                           gatec[:, m_, k, s:s + 1].to_broadcast((P, P)), ident, start=True, stop=True)
                m.then_inc(grow_t, 1)

            pe.wait_ge(mod_ready, 8)
            pe.wait_ge(lin_evac, LIN_SSMOUT)
            for r in range(2):
                grow_(r)
            for n in (4, 5):
                norm_t(n)
            pe.wait_ge(grow_ready, 2)

            def swiglu(s0, it, nblk, n, pos, xoff, c0, t0, y_free, at_step=None):
                pd, cd, td = it * MOE_PIECES, it * MOE_STEPS, it * MOE_STEPS
                for j in range(n + 2):
                    for kind in ("g", "u") if j < n else ():
                        for h in range(2):
                            p = 2 * (s0 + pos[(kind, j)]) + h
                            pe.wait_ge(lo_ready, pd + p + 1)
                            for b in range(nblk):
                                c = c0 + j * nblk + b
                                if kind == "g" and h == 0 and c >= 2:
                                    pe.wait_ge(h_done, cd + c - 1)
                                o = bank[4 + c % 2][:, 0:UCOL] if kind == "g" else bank[4 + c % 2][:, UCOL:2 * UCOL]
                                for t in range(4):
                                    k = 4 * h + t
                                    a = xoff + b * P
                                    m = tok3(o, xh[:, k, a:a + P], xl[:, k, a:a + P], *wpart(p, t, UCOL),
                                             first=(k == 0), last=(k == KC - 1))
                            m.then_inc(piece_used, 1)
                    if 1 <= j <= n:
                        tj = t0 + j - 1
                        pe.wait_ge(h_done, cd + c0 + j * nblk)
                        if tj >= 2:
                            pe.wait_ge(ht_lo, td + tj - 1)
                        for b in range(nblk):
                            for i in range(2):
                                m = pe.transpose(bank[6 + tj % 2][:, (2 * b + i) * P:(2 * b + i + 1) * P],
                                                 hbuf((c0 + (j - 1) * nblk + b) % 2)[:, i * P:(i + 1) * P], ident)
                        m.then_inc(ht_t, 1)
                    if at_step:
                        at_step(j)
                    if j >= 2:
                        tj = t0 + j - 2
                        pe.wait_ge(ht_lo, td + tj + 1)
                        if j == 2 and y_free is not None:
                            pe.wait_ge(y_evac, y_free)
                        for h in range(2):
                            p = 2 * (s0 + pos[("d", j - 2)]) + h
                            pe.wait_ge(lo_ready, pd + p + 1)
                            for b in range(nblk):
                                a = (2 * b + h) * P
                                for half in range(2):
                                    m = tok3(bank[2 * b + half][:, :], hth[:, tj % 2, a:a + P], htl[:, tj % 2, a:a + P],
                                             *wpart(p, 0, 1024, half * 512, 512),
                                             first=(j == 2 and h == 0), last=(j == n + 1 and h == 1))
                            m.then_inc(piece_used, 1)

            def hbuf(i):
                return hcur[0][i]

            hcur = [hb]
            def mlp_side(ps, j):
                if j == 0 and ps == 0:
                    grow_(2)
                    grow_(3)
                if j == 1:
                    if ps == 0:
                        pe.wait_ge(grow_ready, 4)
                    else:
                        pe.wait_ge(y_evac, 4)
                    norm_t(6 + 2 * ps)
                    norm_t(7 + 2 * ps)
                if j == 2:
                    pe.wait_ge(xmod_done, 8 + 2 * ps)

            for ps in range(2):
                pe.wait_ge(xsplit_done, 6 + 2 * ps)
                swiglu(S_FFN + ps * FFN_N, 0, 2, FFN_STEPS, pos_ffn, ps * 2 * P, ps * 2 * FFN_STEPS, ps * FFN_STEPS,
                       4 if ps else None, lambda j, ps=ps: mlp_side(ps, j))

            pe.wait_ge(y_evac, 8)
            for blocks, n in ((LAT, 10), (CTX, 12)):
                if blocks is CTX:
                    norm_t(10)
                    norm_t(11)
                pe.wait_ge(xsplit_done, n)
                for h in range(2):
                    p = 2 * S_DT + h
                    pe.wait_ge(lo_ready, p + 1)
                    a = blocks[0] * P
                    for t in range(4):
                        k = 4 * h + t
                        m = tok3(bank[4 + blocks[0] // 2][0:64, 0:2 * P], *wpart(p, t, UCOL, 0, 64),
                                 xh[:, k, a:a + 2 * P], xl[:, k, a:a + 2 * P], first=(k == 0), last=(k == KC - 1))
                    if blocks is CTX:
                        m.then_inc(piece_used, 1)
            pe.wait_ge(dt_rows, 2)
            for b in range(NBLK):
                m = pe.transpose(bank[6][:, 64 * b:64 * b + 64], dtr[:, b * P:(b + 1) * P], ident[0:64, 0:64])
            m.then_inc(dt_cols, 1)

            def proj(g, ui, h):
                p = 2 * (S_GRP + g * GROUP_UNITS + ui) + h
                pe.wait_ge(lo_ready, p + 1)
                if h == 0 and g + ui > 0:
                    pe.wait_ge(pr_copy, 10 * g + 2 * ui)
                if h == 0 and g + ui == 0:
                    pe.wait_ge(xmod_done, 12)
                for c in range(2):
                    n = 512 if ui in (1, 2) or (ui == 0 and c == 0) else SEQ
                    o = bank[c][:, 0:n]
                    for t in range(4):
                        k = 4 * h + t
                        w_hi, w_lo = wpart(p, t, UCOL, c * P, P)
                        mm(o, w_hi, xh[:, k, 0:n], start=(k == 0), stop=False)
                        mm(o, w_hi, xl[:, k, 0:n], start=False, stop=False)
                        m = mm(o, w_lo, xh[:, k, 0:n], start=False, stop=(k == KC - 1))
                m.then_inc(piece_used, 1)

            def to_tok(g, i):
                pe.wait_ge(cv_out, 6 * g + (1 if i == 0 else i + 2))
                if g * 5 + i > 0:
                    pe.wait_ge(tr_copy, g * 5 + i)
                if i == 0 and g > 1:
                    pe.wait_ge(gn_copy, g - 1)
                for b in range(NBLK):
                    src = bT[:, b * P:(b + 1) * P] if i == 0 else \
                        xs[:, g % 2 if b in LAT else 2, i - 1, (b % 2) * P:(b % 2 + 1) * P]
                    m = pe.transpose(bank[5][:, b * P:(b + 1) * P], src, ident)
                m.then_inc(tr_t, 1)

            def decay_sums():
                pe.wait_ge(dt_a, 1)
                for b in range(NBLK):
                    for d in range(2):
                        a = 64 * b + 32 * d
                        mm(bank[6][:, a:a + 32], tri[d], dta[:, b, 32 * d:32 * d + 32], start=True, stop=True)
                    m = mm(bank[7][:, 64 * b:64 * b + 64], ones, dta[:, b, :], start=True, stop=True)
                m.then_inc(dt_t, 1)

            def cb(g):
                pe.wait_ge(cv_out, 6 * g + 2)
                if g > 0:
                    pe.wait_ge(st_done, g * NST)
                for b in range(2):
                    m = mm(bank[4][:, b * P:(b + 1) * P], bT[:, b * P:(b + 1) * P],
                           cT[g % 2][:, b * P:(b + 1) * P],
                           start=True, stop=True)
                m.then_inc(cb_t, 1)

            def bc(g, q):
                d, b, hq = ssd_idx[q]
                n = g * NQ + q
                if n >= 2:
                    pe.wait_ge(sg_ready, n - 1)
                for i in range(4):
                    a = d * N_SSM_HEADS + g * HPG + hq * 4 + i
                    m = mm(bank[2 + q % 2][:, i * P:(i + 1) * P], dta[:, b, a:a + 1].to_broadcast((P, P)), tri[d],
                           start=True, stop=True)
                m.then_inc(bc_t, 1)

            def state(g, k):
                n = g * NST + k
                pe.wait_ge(xe_ready, n + 1)
                if k == 0:
                    pe.wait_ge(cb_m, g + 1)
                if n >= 1:
                    pe.wait_ge(st_done, n)
                mm(bank[4][:, :], btok[g % 2][:, ssd_states[k][2], :], xE[k % 2], start=True, stop=True).then_inc(st_t, 1)

            def yy(g, q):
                d, b, hq = ssd_idx[q]
                n = g * NQ + q
                pe.wait_ge(mt_ready, n + 1)
                pe.wait_ge(ce_ready, n + 1)
                pe.wait_ge(xdt_ready, g * 4 + q // 2 + 1)
                pe.wait_ge(st_done, g * NST + (2, 3, 5, 6)[q // 2])
                if q == 0 and g > 0:
                    pe.wait_ge(gy_v, 4 * g)
                for i0 in (0, 2):
                    for x, y_, last in ((xdt[q // 2 % 2], mt, False), (hst[d], ce, True)):
                        for i in (i0, i0 + 1):
                            h = hq * 4 + i
                            r = (h % 2) * 64
                            a = (i // 2) * SEQ + b * P
                            m = mm(bank[6 + hq][r:r + 64, a:a + P], x[:, h * 64:h * 64 + 64],
                                   y_[q % 2][:, i * P:(i + 1) * P], start=(q < 2 and i < 2 and not last),
                                   stop=(q >= NQ - 2 and i >= 2 and last), skip_group_check=True)
                m.then_inc(yy_t, 1)

            def ssm_out(i, h):
                kh, q = divmod(i, U_MIXOUT)
                p = 2 * (S_SSMOUT + i) + h
                pe.wait_ge(gf_done, 2 * kh + h + 1)
                pe.wait_ge(lo_ready, p + 1)
                for b in LAT:
                    for t in range(4):
                        k = 8 * kh + 4 * h + t
                        m = tok3(bank[q][:, b * UCOL:(b + 1) * UCOL], xh16[:, k, b * P:(b + 1) * P],
                                 xl16[:, k, b * P:(b + 1) * P], *wpart(p, t, UCOL),
                                 first=(k == 0 and b == 0), last=(k == 15 and b == 1), group=False)
                m.then_inc(piece_used, 1)

            def project(g, k):
                if g == N_GROUPS:
                    if 5 <= k <= 8:
                        ssm_out((k - 5) // 2, (k - 5) % 2)
                    return
                if k == 0:
                    proj(g, 0, 0)
                    proj(g, 0, 1)
                if k in (1, 2):
                    proj(g, 1, k - 1)
                if k == 3:
                    proj(g, 2, 0)
                if k == 4:
                    to_tok(g, 0)
                    proj(g, 2, 1)
                if k == 5:
                    proj(g, 3, 0)
                if k == 6:
                    proj(g, 3, 1)
                    to_tok(g, 1)
                    proj(g, 4, 0)
                if k == 7:
                    proj(g, 4, 1)
                    to_tok(g, 2)
                if k == 8:
                    to_tok(g, 3)
                if k == 9:
                    to_tok(g, 4)
                    cb(g)

            def scan(g, k):
                if k == 0:
                    bc(g, 0)
                    project(g + 1, k)
                    state(g, 0)
                    state(g, 1)
                    bc(g, 1)
                elif k <= NQ:
                    q = k - 1
                    if q + 2 < NQ:
                        bc(g, q + 2)
                    project(g + 1, k)
                    yy(g, q)
                    for i in {1: (2,), 2: (3, 4), 5: (5,)}.get(q, ()):
                        state(g, i)
                else:
                    project(g + 1, k)

            def late(g, k):
                if k == 1:
                    pe.wait_ge(gq_done, g + 1)
                    pe.wait_ge(tr_copy, min(5 * (g + 2), 5 * N_GROUPS))
                    for c in range(4):
                        m = mm(bank[5][:, 0:SEQ], ones, xs[:, g % 2, c, :], start=(c == 0), stop=(c == 3))
                    m.then_inc(gn_t, 1)

            for k in range(SLOTS):
                project(0, k)
                if k == 6:
                    decay_sums()
            pe.wait_ge(dt_x, 1)
            for g in range(N_GROUPS):
                for k in range(SLOTS):
                    if g > 0:
                        late(g - 1, k)
                    scan(g, k)
            pe.wait_ge(sg_ready, N_GROUPS * NQ)
            for i in range(2, 2 * U_MIXOUT):
                if i == 3:
                    late(N_GROUPS - 1, 1)
                for h in range(2):
                    ssm_out(i, h)
                if i == U_MIXOUT:
                    pe.wait_ge(gy_v, 4 * N_GROUPS)
                    pe.wait_ge(gn_copy, N_GROUPS)
                    for r in (4, 5):
                        grow_(r)
            norm_t(12)
            norm_t(13)

            pe.wait_ge(xsplit_done, 14)
            pe.wait_ge(rw_lo, 1)
            for k in range(KC):
                m = tok3(bank[4][0:8, 0:2 * P], rwh[:, k, :], rwl[:, k, :], xh[:, k, 0:2 * P], xl[:, k, 0:2 * P],
                         first=(k == 0), last=(k == KC - 1))
            m.then_inc(lg_rows, 1)
            pe.wait_ge(lg_copy, 1)
            for b in range(2):
                m = pe.transpose(bank[5][:, 32 + 8 * b:40 + 8 * b], lgT[0:8, b * P:(b + 1) * P], ident[0:8, 0:8])
            m.then_inc(lg_t, 1)
            pe.wait_ge(rt_v, 1)
            mm(bank[5][:, 0:8], strict, mask[:, 0, :], start=True, stop=True)
            mm(bank[5][:, 8:16], strict, mask[:, 1, :], start=True, stop=False)
            mm(bank[5][:, 8:16], ones, mask[:, 0, :], start=False, stop=True)
            mm(bank[5][:, 16:24], ones, mask[:, 0, :], start=True, stop=False)
            mm(bank[5][:, 16:24], ones, mask[:, 1, :], start=False, stop=True).then_inc(rt_t, 1)

            hcur[0] = mhb

            def gather(it):
                pe.wait_ge(slot_ready, it + 1)
                for k in range(KC):
                    for b in range(2):
                        m = mm(bank[2 + k // 4][:, (k % 4) * P:(k % 4 + 1) * P], mxn[b][:, k * P:(k + 1) * P],
                               slot1[:, b, :], start=(b == 0), stop=(b == 1))
                m.then_inc(gat_t, 1)

            def combine(it, b):
                if b == 0:
                    pe.wait_ge(gT_ready, it + 1)
                    pe.wait_ge(y_evac, 2 * it + Y_MOE + 2)
                for half in range(2):
                    if b == 1:
                        pe.wait_ge(cmb_add, 4 * it + 1 + half + 1)
                    mm(bank[2 + half][:, :], gT[:, b, :], yexp[:, half * 512:(half + 1) * 512],
                       start=True, stop=True).then_inc(cmb_t, 1)

            def expert(it, before, after):
                pe.wait_ge(gat_lo, it + 1)

                def at_step(j):
                    if j in (1, 2) and before:
                        combine(it - 1, j - 1)
                    if j == 3:
                        pe.wait_ge(gs_ready, it + 1)
                        if before:
                            pe.wait_ge(cmb_add, 4 * it + 1)
                        for b in range(2):
                            m = pe.transpose(bank[2][:, b * P:(b + 1) * P], slotg[:, b, :], ident)
                        m.then_inc(gs_t, 1)
                    if j == J_GATHER and after:
                        pe.wait_ge(gT_ready, it + 1)
                        gather(it + 1)

                swiglu(S_MOE, it, 1, MOE_STEPS, pos_moe, 0, C_MOE, T_MOE, 2 * it + Y_MOE, at_step)

            gather(0)
            expert(0, False, True)
            with pe.Fori(1, N_EXPERTS - 1) as e:
                expert(e, True, True)
            expert(N_EXPERTS - 1, True, False)
            for b in range(2):
                combine(N_EXPERTS - 1, b)
            pe.wait_ge(rt_done, RT_N)
            most = pe.value_load(cnt[0:1, 8:9], min_val=0, max_val=2 * P)
            with pe.If(most > CAP):
                with pe.Fori(0, N_EXPERTS) as e:
                    n = pe.value_load(cnt[0:1, bass.ds(e, 1)], min_val=0, max_val=2 * P)
                    with pe.If(n > CAP):
                        gather(e + N_EXPERTS)
                        expert(e + N_EXPERTS, False, False)
                        for b in range(2):
                            combine(e + N_EXPERTS, b)
                    with pe.Else():
                        it = e + N_EXPERTS
                        for s, before, per in ((piece_used, P_MOE + it * MOE_PIECES, MOE_PIECES),
                                               (ht_t, T_MOE + it * MOE_STEPS, MOE_STEPS),
                                               (gat_t, it, 1), (gs_t, it, 1), (cmb_t, 4 * it, 4)):
                            pe.wait_ge(s, before)
                            pe.sem_inc(s, per)

        @block.scalar
        def _(act):
            A_ = act.activation
            spl = [0]

            def hi_piece(p):
                u = unit_of_split(p // 2)
                if p % 2 == 0:
                    act.wait_ge(raw_landed[slot(u)], landed[u])
                if p >= SPL:
                    act.wait_ge(piece_used, p - SPL + 1)
                A_(hi[:, p % SPL, :], raw[:, slot(u), (p % 2) * PIECE:(p % 2 + 1) * PIECE], ACT.Copy
                   ).then_inc(hi_ready, 1)

            def hi_to(n):
                while spl[0] < min(n, P_MOE):
                    hi_piece(spl[0])
                    spl[0] += 1
                if n > P_MOE:
                    for i in range(spl[0] - P_MOE, n - P_MOE):
                        hi_moe(i, 0)
                        spl[0] += 1

            def hi_moe(i, it):
                if i % 2 == 0:
                    u = U_MOE + i // 2
                    act.wait_ge(raw_landed[slot(u)], landed_moe(i // 2, it))
                p = P_MOE + i
                act.wait_ge(piece_used, it * MOE_PIECES + p - SPL + 1)
                u = slot(U_MOE + i // 2)
                A_(hi[:, p % SPL, :], raw[:, u, (i % 2) * PIECE:(i % 2 + 1) * PIECE], ACT.Copy).then_inc(hi_ready, 1)

            steps = [0]

            def own(ins):
                ins.then_inc(astep, 1)
                steps[0] += 1
                act.wait_ge(astep, steps[0])

            act.wait_ge(vec_cols, 3)
            act.wait_ge(zeroed, 1)
            A_(sc[:, :, 0], cols[:, V_C:V_C + KC], ACT.Silu).then_inc(sc_ready, 1)
            A_(sc[:, :, 1], cols[:, V_CC:V_CC + KC], ACT.Silu).then_inc(sc_ready, 1)

            def ada_copy(a):
                act.wait_ge(ada_used, a + 1)
                if a > 0:
                    act.wait_ge(ada_col, a)
                A_(part, bank[6][:, :], ACT.Copy).then_inc(ada_part, 1)

            def norm_a(n):
                if n < 4:
                    act.wait_ge(*((ld_x, 16) if n < 2 else (ld_ctx, 16)))
                else:
                    act.wait_ge(po_done, n - 3)
                if n >= 2:
                    act.wait_ge(xt_done, n - 1)
                if n == 0:
                    act.wait_ge(eps_ready, 1)
                A_(xn_of(n), xblk[NORMS[n][2]], ACT.Square, accum_out=ss[:, n:n + 1]).then_inc(n_ss, 1)
                act.wait_ge(n_ss, n + 1)
                A_(rms[:, n:n + 1], ss[:, n:n + 1], ACT.Sqrt, scale=1.0 / D_MODEL, bias=epsc[:, 0:1]).then_inc(n_rms, 1)

            def norm_b(n):
                m, s, b = NORMS[n]
                act.wait_ge(xt_done, n + 1)
                act.wait_ge(mod_ready, 1 if m == 0 else 8)
                if n >= 2:
                    act.wait_ge(xsplit_done, n - 1)
                a_, b_ = mod_cols(m, s)
                for k in range(KC):
                    i = A_(t32_of(n)[:, k * P:(k + 1) * P], bank[2 * (n % 2) + k // 4][:, (k % 4) * P:(k % 4 + 1) * P],
                           ACT.Identity, scale=a_[:, k:k + 1], bias=b_[:, k:k + 1])
                i.then_inc(xmod_done, 1)

            def post_a(n):
                A_(pjunk if n < 8 else mpjunk, post_src(n), ACT.Square, accum_out=ss[:, 14 + n:15 + n]).then_inc(po_ss, 1)
                act.wait_ge(po_ss, n + 1)
                A_(rms[:, 14 + n:15 + n], ss[:, 14 + n:15 + n], ACT.Sqrt, scale=1.0 / D_MODEL, bias=epsc[:, 0:1]
                   ).then_inc(po_rms, 1)

            ada_copy(0)
            norm_a(0)
            norm_a(1)
            ada_copy(1)
            norm_a(2)
            norm_a(3)
            for a in range(2, ADA_FIRST):
                ada_copy(a)
            for n in range(4):
                norm_b(n)
            hi_to(SPL)

            def lin_out(s0, lin0, dst):
                for u in range(U_MIXIN if s0 == S_MIXIN else U_MIXOUT):
                    hi_to(2 * (s0 + u) + 1 + SPL)
                    hi_to(2 * (s0 + u) + 2 + SPL)
                    act.wait_ge(piece_used, 2 * (s0 + u) + 2)
                    for b in range(NBLK):
                        A_(dst[:, b, u * UCOL:(u + 1) * UCOL], bank[(u % 2) * 4 + b][:, 0:UCOL], ACT.Copy
                           ).then_inc(lin_evac, 1)

            def lin_in():
                for u in range(U_MIXIN):
                    hi_to(min(2 * u + 2 + SPL, 2 * S_MIXOUT))
                    act.wait_ge(piece_used, 2 * u + 2)
                    for b in range(NBLK):
                        A_(px[:, b, u * UCOL:(u + 1) * UCOL], bank[(u % 2) * 4 + b][:, 0:UCOL], ACT.Copy
                           ).then_inc(lin_evac, 1)

            lin_in()

            def stage_1(k, i):
                if k == "dft":
                    act.wait_ge(dft_t1, i + 1)
                    if i >= 2:
                        act.wait_ge(dft_out, i - 1)
                    A_(t1s[i % 2], bank[i % 2][:, :], ACT.Copy).then_inc(dft_t1s, 1)
                    if i % 2 == 1:
                        b = i // 2
                        act.wait_ge(qk_ss, b + 1)
                        A_(qrms[:, b, :], qss[:, b, :], ACT.Sqrt, scale=1.0 / HEAD_DIM, bias=epsc[:, 0:1]
                           ).then_inc(qk_rms, 1)
                else:
                    nk = at_info(i)[3][1]
                    act.wait_ge(at_mx, i + 1)
                    if i >= 2:
                        act.wait_ge(at_t, i - 1)
                    A_(prob[i % 2][:, 0:nk * P], bank[i % 2][:, 0:nk * P], ACT.Exp, bias=nmx[:, i:i + 1], scale=AT_SCALE,
                       accum_out=rsum[:, i:i + 1]).then_inc(at_exp, 1)

            def stage_2(k, i):
                if k == "dft":
                    s, g = divmod(i, 4)
                    act.wait_ge(dft_out, i + 1)
                    A_(xh[:, g, s * SEQ:(s + 1) * SEQ], bank[2 + i % 2][:, 0:SEQ], ACT.Copy).then_inc(dft_hi, 1)
                else:
                    nk = at_info(i)[3][1]
                    act.wait_ge(at_t, i + 1)
                    if i >= 2:
                        act.wait_ge(at_pv, i - 1)
                    A_(pts[i % 2][:, 0:nk * P], bank[2 + i % 2][:, 0:nk * P], ACT.Copy).then_inc(at_pt, 1)

            def stage_3(k, i):
                if k == "att" and i % 8 == 7:
                    b = i // 8
                    act.wait_ge(at_pv, i + 1)
                    A_(xh[:, 4:8, b * P:(b + 1) * P], v3(bank[4 + b % 2][:, :], 4), ACT.Copy).then_inc(at_oh, 1)

            for j in range(N_PAIRS + 1):
                if j == 4:
                    for b in range(NBLK):
                        act.wait_ge(qk_t, b + 1)
                        A_(qT[:, b, :, :], qk_banks(b)[0][:, :].rearrange("p (c n) -> p c n", c=4), ACT.Copy).then_inc(qk_tc, 1)
                        A_(kT[:, :, b * P:(b + 1) * P], v3(qk_banks(b)[1][:, 0:2 * P], 2), ACT.Copy).then_inc(qk_tc, 1)
                for k, i in pair_of(j - 1):
                    stage_2(k, i)
                for k, i in pair_of(j):
                    stage_1(k, i)
                if j < N_PAIRS:
                    ada_copy(ADA_FIRST + j)
                for k, i in pair_of(j - 1):
                    stage_3(k, i)
            hi_to(2 * S_MIXOUT + SPL)
            lin_out(S_MIXOUT, LIN_MIXOUT, y)

            def grow_out(r):
                act.wait_ge(grow_t, r + 1)
                for k in range(2):
                    i = A_(grow_tile(r)[:, k * 512:(k + 1) * 512], grow_bank(r, k)[:, :], ACT.Copy)
                i.then_inc(grow_ready, 1)

            act.wait_ge(lin_evac, LIN_SSMOUT)
            post_a(0)
            grow_out(0)
            post_a(1)
            norm_a(4)
            norm_a(5)
            grow_out(1)
            post_a(2)
            norm_b(4)
            norm_b(5)
            post_a(3)
            norm_a(6)
            norm_a(7)

            def swiglu(s0, it, nblk, n, pos, c0, t0, sgt, look, at_step=None):
                pd, cd, td = it * MOE_PIECES, it * MOE_STEPS, it * MOE_STEPS
                for j in range(n + 2):
                    if j < n:
                        for kind in ("g", "u"):
                            for h in range(2):
                                look(2 * pos[(kind, j)] + h)
                        act.wait_ge(piece_used, pd + 2 * (s0 + pos[("u", j)]) + 2)
                        for b in range(nblk):
                            c = c0 + j * nblk + b
                            if c >= 2:
                                act.wait_ge(h_done, cd + c - 1)
                            A_(sgt[c % 2], bank[4 + c % 2][:, 0:UCOL], ACT.Silu).then_inc(sil_done, 1)
                    if 1 <= j <= n:
                        tj = t0 + j - 1
                        act.wait_ge(ht_t, td + tj + 1)
                        if j >= 3:
                            act.wait_ge(piece_used, pd + 2 * (s0 + pos[("d", j - 3)]) + 2)
                        A_(hth[:, tj % 2, 0:2 * nblk * P], bank[6 + tj % 2][:, 0:2 * nblk * P], ACT.Copy
                           ).then_inc(ht_hi, 1)
                    if at_step:
                        at_step(j)
                    if j >= 2:
                        for h in range(2):
                            look(2 * pos[("d", j - 2)] + h)

            def mlp_side(ps, j):
                if j == 0 and ps == 0:
                    grow_out(2)
                    grow_out(3)
                if j == 0 and ps == 1:
                    act.wait_ge(y_evac, 4)
                    post_a(4)
                    post_a(5)
                    norm_a(8)
                    norm_a(9)
                if j == 1:
                    norm_b(6 + 2 * ps)
                    norm_b(7 + 2 * ps)

            for ps in range(2):
                s0 = S_FFN + ps * FFN_N
                swiglu(s0, 0, 2, FFN_STEPS, pos_ffn, ps * 2 * FFN_STEPS, ps * FFN_STEPS, sg,
                       lambda i, s0=s0: hi_to(2 * s0 + i + 1 + SPL), lambda j, ps=ps: mlp_side(ps, j))
                act.wait_ge(piece_used, 2 * (s0 + FFN_N))
                for half in range(2):
                    A_(y[:, 2 * ps, half * 512:(half + 1) * 512], bank[half][:, :], ACT.Copy).then_inc(y_evac, 1)
            act.wait_ge(y_evac, 8)
            post_a(6)
            post_a(7)
            norm_a(10)
            norm_a(11)
            norm_b(10)
            norm_b(11)

            act.wait_ge(piece_used, 2 * S_DT + 2)
            for i in range(2):
                A_(dtr[:, i * 2 * P:(i + 1) * 2 * P], bank[4 + i][0:64, 0:2 * P], ACT.Copy).then_inc(dt_rows, 1)
            for h in range(2):
                hi_to(2 * S_DT + h + 1 + SPL)
            act.wait_ge(ld_ssm, 48)
            A_(arow, arow, ACT.Exp).then_inc(dt_e, 1)
            act.wait_ge(dt_v, 2)
            A_(st2, st2, ACT.Exp, scale=-1.0).then_inc(dt_e, 1)

            def conv_in(g, i):
                n, ui = 6 * g + i, i // 2
                act.wait_ge(piece_used, 2 * (S_GRP + g * GROUP_UNITS + ui) + 2)
                if n == 0:
                    act.wait_ge(zeroed, 3)
                if n >= 2:
                    act.wait_ge(cv_acc, n - 1)
                ns = 1 if i == 1 else 2
                A_(cpad[n % 2][:, 0:ns, 2:2 + SEQ], v3(bank[i % 2][:, 0:ns * SEQ], ns), ACT.Copy).then_inc(pr_copy, 1)

            def conv_out(g, i):
                n = 6 * g + i
                act.wait_ge(cv_acc, n + 1)
                if i == 0 and g > 0:
                    act.wait_ge(cb_t, g)
                src = cacc[n % 2] if i != 1 else cacc[n % 2][:, 0:SEQ]
                if i >= 2:
                    src = v3(src, 2)
                dst = bT if i == 0 else cT[g % 2] if i == 1 else xs[:, g % 2::2 - g % 2, i - 2, :]
                ch = (16 + g, 20 + g, 4 * g, 4 * g + 1, 4 * g + 2, 4 * g + 3)[i]
                A_(dst, src, ACT.Silu, bias=cols[:, V_CONVB + ch:V_CONVB + ch + 1]).then_inc(cv_out, 1)

            def tok(g, i):
                act.wait_ge(tr_t, 5 * g + i + 1)
                dst = btok[g % 2][:, :, :] if i == 0 else xtok[g % 2][:, :, (i - 1) * P:i * P]
                A_(dst, v3(bank[5][:, :], NBLK), ACT.Copy).then_inc(tr_copy, 1)

            def zs(g, ui, func):
                act.wait_ge(piece_used, 2 * (S_GRP + g * GROUP_UNITS + ui) + 2)
                for c in range(2):
                    A_(gy[:, 4 * g + 2 * (ui - 3) + c, :], bank[c][:, 0:SEQ], func).then_inc(pr_copy, 1)

            def norm_rms(g0, g1):
                for g in range(g0, g1):
                    act.wait_ge(gn_copy, g + 1)
                    A_(ssg[g], ssg[g], ACT.Sqrt, scale=1.0 / 512, bias=epsc[:, 0:1]).then_inc(gn_rms, 1)

            def norm_hi(g):
                act.wait_ge(gf_v, 4 * (g + 1))
                A_(xh16[:, 4 * g:4 * g + 4, :], gy[:, 4 * g:4 * g + 4, :], ACT.Copy).then_inc(gf_hi, 1)

            def project(g, k):
                if g == N_GROUPS:
                    if 6 <= k <= 7:
                        hi_to(2 * S_SSMOUT + k - 5 + SPL)
                    if k == 0:
                        norm_rms(0, 2)
                    if k in (2, 3):
                        norm_hi(k - 2)
                    if k == 4:
                        norm_rms(2, 3)
                    if k == 6:
                        norm_hi(2)
                    return
                hi_to(split_by(g, k))
                if k == 0:
                    conv_in(g, 0)
                    conv_in(g, 1)
                if k == 2:
                    conv_in(g, 2)
                    conv_in(g, 3)
                if k == 3:
                    conv_out(g, 0)
                    conv_out(g, 1)
                if k == 4:
                    tok(g, 0)
                    conv_in(g, 4)
                if k == 5:
                    conv_in(g, 5)
                    conv_out(g, 2)
                    conv_out(g, 3)
                if k == 6:
                    zs(g, 3, ACT.Copy)
                    tok(g, 1)
                if k == 7:
                    conv_out(g, 4)
                    conv_out(g, 5)
                    z01 = gy[:, 4 * g:4 * g + 2, :]
                    act.wait_ge(pr_copy, 10 * g + 8)
                    A_(z01, z01, ACT.Silu).then_inc(zs_done, 1)
                    zs(g, 4, ACT.Silu)
                    tok(g, 2)
                if k == 8:
                    tok(g, 3)
                if k == 9:
                    tok(g, 4)

            def ce_(g, q):
                n = g * NQ + q
                act.wait_ge(bc_t, n + 1)
                if n >= 2:
                    act.wait_ge(yy_t, n - 1)
                A_(ce[q % 2], bank[2 + q % 2][:, :], ACT.Exp).then_inc(ce_exp, 1)

            def m_(g, q):
                act.wait_ge(sg_ready, g * NQ + q + 1)
                A_(mt[q % 2], mt[q % 2], ACT.Exp).then_inc(mt_exp, 1)

            def scan(g, k):
                if k == 0:
                    ce_(g, 0)
                    project(g + 1, k)
                    ce_(g, 1)
                elif k <= NQ:
                    q = k - 1
                    m_(g, q)
                    project(g + 1, k)
                    if q + 2 < NQ:
                        ce_(g, q + 2)
                else:
                    project(g + 1, k)

            def late(g, k):
                x = xs[:, g % 2, :, :]
                if k == 0:
                    act.wait_ge(gy_done, g + 1)
                    A_(x, gy[:, 4 * g:4 * g + 4, :], ACT.Square).then_inc(gq_done, 1)
                if k == 2:
                    act.wait_ge(gn_t, g + 1)
                    A_(ssg[g], bank[5][:, 0:SEQ], ACT.Copy).then_inc(gn_copy, 1)

            for k in range(SLOTS):
                project(0, k)
                if k == 8:
                    act.wait_ge(dt_v, 4)
                    A_(cdec[:, :, :], v3(bank[7][:, 0:256], 4), ACT.Exp).then_inc(dt_e, 1)
                    A_(eE[:, :, :], v3(st1, 4), ACT.Exp).then_inc(dt_e, 1)
            for g in range(N_GROUPS):
                for k in range(SLOTS):
                    if g > 0:
                        late(g - 1, k)
                    scan(g, k)
            late(N_GROUPS - 1, 0)
            hi_to(2 * S_SSMOUT + 4 + SPL)
            late(N_GROUPS - 1, 2)
            norm_rms(3, 4)
            hi_to(2 * S_SSMOUT + 6 + SPL)
            norm_hi(3)
            hi_to(2 * S_SSMOUT + 8 + SPL)
            for q in range(U_MIXOUT):
                p = 2 * (S_SSMOUT + U_MIXOUT + q)
                hi_to(p + 1 + SPL)
                hi_to(p + 2 + SPL)
                act.wait_ge(piece_used, p + 2)
                A_(yout[:, :, q * UCOL:(q + 1) * UCOL], v3(bank[q][:, :], 2), ACT.Copy).then_inc(lin_evac, 1)
                if q == 0:
                    for r in (4, 5):
                        grow_out(r)
            act.wait_ge(lin_evac, LIN_SSMOUT + U_MIXOUT)
            post_a(8)
            post_a(9)
            norm_a(12)
            norm_a(13)
            norm_b(12)
            norm_b(13)
            act.wait_ge(lg_rows, 1)
            A_(lgT[0:8, :], bank[4][0:8, 0:2 * P], ACT.Copy).then_inc(lg_copy, 1)
            act.wait_ge(rt_v, 2)
            A_(ge, gd, ACT.Exp).then_inc(rt_e, 1)

            def gather_mod(it):
                act.wait_ge(gat_t, it + 1)
                a_, b_ = mod_cols(3, 0)
                for k in range(KC):
                    i = A_(mt32[:, k * P:(k + 1) * P], bank[2 + k // 4][:, (k % 4) * P:(k % 4 + 1) * P],
                           ACT.Identity, scale=a_[:, k:k + 1], bias=b_[:, k:k + 1])
                i.then_inc(gat_mod, 1)

            def expert(it, after):
                def look(i):
                    if i + SPL < MOE_PIECES or after:
                        hi_moe(i + SPL, it)

                def at_step(j):
                    if j == 3:
                        act.wait_ge(gs_t, it + 1)
                        A_(gT[:, :, :], v3(bank[2][:, 0:2 * P], 2), ACT.Copy).then_inc(gT_ready, 1)
                    if j == J_GATHER and after:
                        gather_mod(it + 1)

                swiglu(S_MOE, it, 1, MOE_STEPS, pos_moe, C_MOE, T_MOE, msg, look, at_step)
                act.wait_ge(piece_used, P_MOE + (it + 1) * MOE_PIECES)
                A_(yexp[:, 0:512], bank[0][:, :], ACT.Copy).then_inc(y_evac, 1)

            act.wait_ge(xsplit_done, 14)
            gather_mod(0)
            expert(0, True)
            with act.Fori(1, N_EXPERTS - 1) as e:
                expert(e, True)
            expert(N_EXPERTS - 1, False)
            most = act.value_load(cnt[0:1, 8:9], min_val=0, max_val=2 * P)
            with act.If(most > CAP):
                with act.Fori(0, N_EXPERTS) as e:
                    n = act.value_load(cnt[0:1, bass.ds(e, 1)], min_val=0, max_val=2 * P)
                    with act.If(n > CAP):
                        for i in range(SPL):
                            hi_moe(i, e + N_EXPERTS)
                        gather_mod(e + N_EXPERTS)
                        expert(e + N_EXPERTS, False)
                    with act.Else():
                        it = e + N_EXPERTS
                        for s, before, per in ((hi_ready, P_MOE + it * MOE_PIECES, MOE_PIECES),
                                               (sil_done, C_MOE + it * MOE_STEPS, MOE_STEPS),
                                               (ht_hi, T_MOE + it * MOE_STEPS, MOE_STEPS),
                                               (gat_mod, it, 1), (gT_ready, it, 1), (y_evac, Y_MOE + 2 * it, 1)):
                            act.wait_ge(s, before)
                            act.sem_inc(s, per)
            act.wait_ge(cmb_add, 4 * 2 * N_EXPERTS + 1)
            post_a(10)
            post_a(11)

        @block.vector
        def _(dve):
            TT, TS, STT = dve.tensor_tensor, dve.tensor_scalar, dve.scalar_tensor_tensor
            spl = [0]

            def lo_sub(p, u, h):
                TT(lo[:, p % SPL, :], raw[:, u, h * PIECE:(h + 1) * PIECE], hi[:, p % SPL, :].bitcast(F32), ALU.subtract
                   ).then_inc(lo_ready, 1)

            def lo_to(n):
                while spl[0] < n:
                    p = spl[0]
                    if p < P_MOE:
                        dve.wait_ge(hi_ready, p + 1)
                        lo_sub(p, slot(unit_of_split(p // 2)), p % 2)
                    else:
                        lo_moe(p - P_MOE, 0)
                    spl[0] += 1

            def lo_moe(i, it):
                dve.wait_ge(hi_ready, it * MOE_PIECES + P_MOE + i + 1)
                lo_sub(P_MOE + i, slot(U_MOE + i // 2), i % 2)

            steps = [0]

            def own(ins):
                ins.then_inc(vstep, 1)
                steps[0] += 1
                dve.wait_ge(vstep, steps[0])

            for i, (n, c) in enumerate(((96, V_NORM), (120, V_ADAB), (120, V_CONVW))):
                dve.wait_ge(vec_t, i + 1)
                dve.tensor_copy(cols[:, c:c + n], bank[5 + i][:, 0:n]).then_inc(vec_cols, 1)

            def ada_take(a):
                l, c = divmod(a, N_ADA // 2)
                dve.wait_ge(ada_col, a + 1)
                TT(ada[:, l, 4 * c:4 * c + 4, :], v3(bank[7][:, 0:8], 4),
                   cols[:, V_ADAB + l * 48 + 4 * c:V_ADAB + l * 48 + 4 * c + 4].unsqueeze(2).to_broadcast((P, 4, 2)),
                   ALU.add).then_inc(ada_done, 1)

            def norm_w(l, i):
                a = V_NORM + (l * 4 + i) * KC
                return cols[:, a:a + KC].unsqueeze(2).to_broadcast((P, KC, 2))

            def scale_cols(m):
                l, w = divmod(m, 2)
                STT(moda[:, m, :, :], ada[:, l, 24 * w + KC:24 * w + 2 * KC, :], 1.0, norm_w(l, 2 * w),
                    ALU.add, ALU.mult).then_inc(mod_ready, 1)

            def gate_cols(m):
                l, w = divmod(m, 2)
                TT(gatec[:, m, :, :], ada[:, l, 24 * w + 2 * KC:24 * w + 3 * KC, :], norm_w(l, 2 * w + 1), ALU.mult
                   ).then_inc(mod_ready, 1)

            def norm_a(n):
                dve.wait_ge(n_rms, n + 1)
                dve.reciprocal(rstd[:, n:n + 1], rms[:, n:n + 1]).then_inc(n_rstd, 1)
                dve.wait_ge(n_rstd, n + 1)
                TS(xn_of(n), xblk[NORMS[n][2]], rstd[:, n:n + 1], None, ALU.mult).then_inc(xn_ready, 1)

            def norm_b(n):
                b = NORMS[n][2]
                dve.wait_ge(xmod_done, n + 1)
                dve.tensor_copy(xh[:, :, b * P:(b + 1) * P], v3(t32_of(n), KC)).then_inc(xsplit_hi, 1)
                dve.wait_ge(xsplit_hi, n + 1)
                TT(xl[:, :, b * P:(b + 1) * P], v3(t32_of(n), KC), xh[:, :, b * P:(b + 1) * P].bitcast(F32), ALU.subtract
                   ).then_inc(xsplit_done, 1)

            def post(n):
                m, s, b = POSTS[n]
                t = ptmp if n < 8 else mptmp
                dve.wait_ge(po_rms, n + 1)
                dve.reciprocal(rstd[:, 14 + n:15 + n], rms[:, 14 + n:15 + n]).then_inc(po_rstd, 1)
                dve.wait_ge(po_rstd, n + 1)
                dve.wait_ge(grow_ready, grow_of(n) + 1)
                STT(t, post_src(n), rstd[:, 14 + n:15 + n], grow_tile(grow_of(n)), ALU.mult, ALU.mult
                    ).then_inc(po_t, 1)
                dve.wait_ge(po_t, n + 1)
                TT(xblk[b], xblk[b], t, ALU.add).then_inc(po_done, 1)

            ada_take(0)
            norm_a(0)
            norm_a(1)
            ada_take(1)
            norm_a(2)
            norm_a(3)
            for a in range(2, ADA_FIRST):
                ada_take(a)
            dve.wait_ge(ada_done, ADA_FIRST)
            scale_cols(0)
            for n in range(4):
                norm_b(n)
            lo_to(SPL)
            for u in range(U_MIXIN):
                lo_to(min(2 * u + 2 + SPL, 2 * S_MIXOUT))

            dve.wait_ge(lin_evac, LIN_MIXOUT)
            dve.wait_ge(ld_qkw, 32)
            dve.wait_ge(ld_first, 16)

            def heads(b, n0=0, n1=10):
                a = F_WIDTH
                return px[:, b, a + n0 * 64:a + n1 * 64].rearrange("p (h n) -> p h n", n=64)

            def qk_1(b):
                own(TT(qsq, px[:, b, F_WIDTH:F_WIDTH + 640], px[:, b, F_WIDTH:F_WIDTH + 640], ALU.mult))
                dve.tensor_reduce(qss[:, b, :], qsq.rearrange("p (h n) -> p h n", n=64), AX.X, ALU.add
                                  ).then_inc(qk_ss, 1)

            def qk_2(b):
                dve.wait_ge(qk_rms, b + 1)
                own(dve.reciprocal(qrs[:, b, :], qrms[:, b, :]))
                own(TT(heads(b), heads(b), qrs[:, b, :].unsqueeze(2).to_broadcast((P, 10, 64)), ALU.mult))
                TT(heads(b, 0, 8), heads(b, 0, 8), qkw[:, 0:1, :].to_broadcast((P, 8, 64)), ALU.mult)
                own(TT(heads(b, 8, 10), heads(b, 8, 10), qkw[:, 1:2, :].to_broadcast((P, 2, 64)), ALU.mult))

            def qk_3(b):
                if b in LAT:
                    x = px[:, b, F_WIDTH:F_WIDTH + 640].rearrange("p (h n two) -> p h n two", n=32, two=2)
                    x1, x2 = x[:, :, :, 0], x[:, :, :, 1]
                    c, s = (rope[:, i, b, :].unsqueeze(1).to_broadcast((P, 10, 32)) for i in range(2))
                    r = [rtmp[:, i * 320:(i + 1) * 320].rearrange("p (h n) -> p h n", n=32) for i in range(4)]
                    TT(r[0], x1, c, ALU.mult)
                    TT(r[1], x2, s, ALU.mult)
                    TT(r[2], x1, s, ALU.mult)
                    own(TT(r[3], x2, c, ALU.mult))
                    TT(x1, r[0], r[1], ALU.subtract)
                    own(TT(x2, r[2], r[3], ALU.add))

            def qk_4(b):
                a = F_WIDTH + Q_WIDTH
                dve.tensor_copy(kdup[:, b, :].rearrange("p (v two n) -> p v two n", v=2, two=2),
                                px[:, b, a:a + 2 * 64].rearrange("p (v n) -> p v n", v=2).unsqueeze(2)
                                .to_broadcast((P, 2, 2, 64))).then_inc(qk_ready, 1)

            def stage_1(k, i):
                if k == "dft":
                    if i % 2 == 0:
                        qk_1(i // 2)
                    else:
                        qk_2(i // 2)
                        qk_3(i // 2)
                else:
                    nk = at_info(i)[3][1]
                    dve.wait_ge(at_s, i + 1)
                    dve.tensor_reduce(mx[:, i:i + 1], bank[i % 2][:, 0:nk * P], AX.X, ALU.max).then_inc(at_m, 1)
                    dve.wait_ge(at_m, i + 1)
                    TS(nmx[:, i:i + 1], mx[:, i:i + 1], -AT_SCALE, None, ALU.mult).then_inc(at_mx, 1)

            def stage_2(k, i):
                if k == "dft":
                    s, g = divmod(i, 4)
                    dve.wait_ge(dft_hi, i + 1)
                    TT(xl[:, g, s * SEQ:(s + 1) * SEQ], bank[2 + i % 2][:, 0:SEQ],
                       xh[:, g, s * SEQ:(s + 1) * SEQ].bitcast(F32), ALU.subtract).then_inc(dft_lo, 1)
                else:
                    dve.wait_ge(at_exp, i + 1)
                    nk = at_info(i)[3][1]
                    dve.reciprocal(rinv[:, i:i + 1], rsum[:, i:i + 1]).then_inc(at_r, 1)
                    dve.wait_ge(at_r, i + 1)
                    TS(prob[i % 2][:, 0:nk * P], prob[i % 2][:, 0:nk * P], rinv[:, i:i + 1], None, ALU.mult
                       ).then_inc(at_nrm, 1)

            def stage_3(k, i):
                if k == "att" and i % 8 == 7:
                    b = i // 8
                    dve.wait_ge(at_oh, b + 1)
                    TT(xl[:, 4:8, b * P:(b + 1) * P], v3(bank[4 + b % 2][:, :], 4),
                       xh[:, 4:8, b * P:(b + 1) * P].bitcast(F32), ALU.subtract).then_inc(at_ol, 1)

            for j in range(N_PAIRS + 1):
                if j == 4:
                    for b in range(NBLK):
                        qk_4(b)
                for k, i in pair_of(j - 1):
                    stage_2(k, i)
                for k, i in pair_of(j):
                    stage_1(k, i)
                if j >= 1:
                    ada_take(ADA_FIRST + j - 1)
                for k, i in pair_of(j - 1):
                    stage_3(k, i)
            lo_to(2 * S_MIXOUT + SPL)
            dve.wait_ge(ada_done, N_ADA)
            for m in range(1, 4):
                scale_cols(m)
            for m in range(4):
                gate_cols(m)
            for u in range(U_MIXOUT):
                lo_to(2 * (S_MIXOUT + u) + 2 + SPL)

            post(0)
            post(1)
            norm_a(4)
            norm_a(5)
            post(2)
            norm_b(4)
            norm_b(5)
            post(3)
            norm_a(6)
            norm_a(7)

            def swiglu(s0, it, nblk, n, pos, c0, t0, sgt, ht, look, at_step=None):
                cd, td = it * MOE_STEPS, it * MOE_STEPS
                for j in range(n + 2):
                    if j < n:
                        for kind in ("g", "u"):
                            for h in range(2):
                                look(2 * pos[(kind, j)] + h)
                        for b in range(nblk):
                            c = c0 + j * nblk + b
                            dve.wait_ge(sil_done, cd + c + 1)
                            free = t0 + j - (2 // nblk) + 1
                            if free >= 1:
                                dve.wait_ge(ht_t, td + free)
                            TT(ht[c % 2], sgt[c % 2], bank[4 + c % 2][:, UCOL:2 * UCOL], ALU.mult).then_inc(h_done, 1)
                    if 1 <= j <= n:
                        tj = t0 + j - 1
                        dve.wait_ge(ht_hi, td + tj + 1)
                        w = 2 * nblk * P
                        TT(htl[:, tj % 2, 0:w], bank[6 + tj % 2][:, 0:w], hth[:, tj % 2, 0:w].bitcast(F32), ALU.subtract
                           ).then_inc(ht_lo, 1)
                    if at_step:
                        at_step(j)
                    if j >= 2:
                        for h in range(2):
                            look(2 * pos[("d", j - 2)] + h)

            def mlp_side(ps, j):
                if j == 0 and ps == 1:
                    post(4)
                    post(5)
                    norm_a(8)
                    norm_a(9)
                if j == 1:
                    norm_b(6 + 2 * ps)
                    norm_b(7 + 2 * ps)

            for ps in range(2):
                s0 = S_FFN + ps * FFN_N
                swiglu(s0, 0, 2, FFN_STEPS, pos_ffn, ps * 2 * FFN_STEPS, ps * FFN_STEPS, sg, hb,
                       lambda i, s0=s0: lo_to(2 * s0 + i + 1 + SPL), lambda j, ps=ps: mlp_side(ps, j))
                dve.wait_ge(piece_used, 2 * (s0 + FFN_N))
                for half in range(2):
                    dve.tensor_copy(y[:, 2 * ps + 1, half * 512:(half + 1) * 512], bank[2 + half][:, :]).then_inc(y_evac, 1)
            post(6)
            post(7)
            norm_a(10)
            norm_a(11)
            norm_b(10)
            norm_b(11)

            for h in range(2):
                lo_to(2 * S_DT + h + 1 + SPL)
            dve.wait_ge(ld_ssm, 48)
            dve.wait_ge(dt_cols, 1)
            TT(v3(st1, NBLK), v3(bank[6][:, 0:256], NBLK), dbias.unsqueeze(1).to_broadcast((P, NBLK, 64)), ALU.add
               ).then_inc(dt_v, 1)
            dve.wait_ge(dt_v, 1)
            STT(st2, st1, -1.0, st1, ALU.mult, ALU.max).then_inc(dt_v, 1)
            dve.tensor_copy(dcol[0:64, :], drow[0:64, 0:32:2])
            own(dve.tensor_copy(dcol[64:128, :], drow[64:128, 1:32:2]))
            dve.wait_ge(dt_e, 2)
            own(TS(st3, st2, 2.0, None, ALU.add))
            own(dve.reciprocal(st3, st3))
            own(TT(st2, st2, st3, ALU.mult))
            own(TT(st3, st2, st2, ALU.mult))
            p_ = acum[:, :, :].rearrange("p b n -> p (b n)")
            own(TS(p_, st3, 1.0 / 17, None, ALU.mult))
            for k in range(7, 0, -1):
                own(STT(p_, p_, 1.0 / (2 * k + 1), st3, ALU.add, ALU.mult))
            own(STT(p_, p_, 1.0, st2, ALU.add, ALU.mult))
            own(TS(st1, st1, 0.0, None, ALU.max))
            d_ = dt_[:, :, :].rearrange("p b n -> p (b n)")
            own(STT(d_, p_, 2.0, st1, ALU.mult, ALU.add))
            STT(dta[:, :, :], dt_[:, :, :], -1.0, arow.unsqueeze(1).to_broadcast((P, NBLK, 64)), ALU.mult, ALU.mult
                ).then_inc(dt_a, 1)

            def conv(g, i):
                n = 6 * g + i
                ch = (16 + g, 20 + g, 4 * g, 4 * g + 1, 4 * g + 2, 4 * g + 3)[i]
                ns = 1 if i == 1 else 2
                dve.wait_ge(pr_copy, 10 * g + i + 1)
                if n >= 2:
                    dve.wait_ge(cv_out, n - 1)
                o = v3(cacc[n % 2][:, 0:ns * SEQ], ns)

                def tap(t):
                    a = V_CONVW + t * 24 + ch
                    return cpad[n % 2][:, 0:ns, t:t + SEQ], cols[:, a:a + 1]

                x, w = tap(0)
                TS(o, x, w, None, ALU.mult).then_inc(cv_v, 1)
                for t in range(1, D_CONV):
                    dve.wait_ge(cv_v, 4 * n + t)
                    x, w = tap(t)
                    STT(o, x, w, o, ALU.mult, ALU.add).then_inc(cv_v if t < D_CONV - 1 else cv_acc, 1)

            def norm_ab(g):
                dve.wait_ge(gn_rms, g + 1)
                dve.reciprocal(ssg[g], ssg[g]).then_inc(gn_rstd, 1)
                dve.wait_ge(gn_rstd, g + 1)
                for k in range(4 * g, 4 * g + 4):
                    STT(gy[:, k, :], gy[:, k, :], cols[:, V_SNORM + k:V_SNORM + k + 1], ssg[g], ALU.mult, ALU.mult
                        ).then_inc(gf_v, 1)

            def norm_lo(g):
                dve.wait_ge(gf_hi, g + 1)
                TT(xl16[:, 4 * g:4 * g + 4, :], gy[:, 4 * g:4 * g + 4, :], xh16[:, 4 * g:4 * g + 4, :].bitcast(F32),
                   ALU.subtract).then_inc(gf_done, 1)

            def project(g, k):
                if g == N_GROUPS:
                    if 6 <= k <= 7:
                        lo_to(2 * S_SSMOUT + k - 5 + SPL)
                    if k in (1, 2):
                        norm_ab(k - 1)
                    if k in (3, 4):
                        norm_lo(k - 3)
                    if k == 5:
                        norm_ab(2)
                    if k == 7:
                        norm_lo(2)
                    return
                lo_to(split_by(g, k))
                if 1 <= k <= 6:
                    conv(g, k - 1)
                if k == 9:
                    dve.wait_ge(cb_t, g + 1)
                    for d in range(2):
                        i = TT(cbm[g % 2][:, d, :, :], v3(bank[4][:, 0:2 * P], 2),
                               tri[d].unsqueeze(1).to_broadcast((P, 2, P)), ALU.mult)
                    i.then_inc(cb_m, 1)

            def seg(g, q):
                d, b, hq = ssd_idx[q]
                n = g * NQ + q
                dve.wait_ge(ce_exp, n + 1)
                if n >= 2:
                    dve.wait_ge(yy_t, n - 1)
                for i in range(4):
                    a = d * N_SSM_HEADS + g * HPG + hq * 4 + i
                    m = TS(mt[q % 2][:, i * P:(i + 1) * P], bank[2 + q % 2][:, i * P:(i + 1) * P],
                           acum[:, b, a:a + 1], 0.0, ALU.subtract, ALU.min)
                m.then_inc(sg_ready, 1)

            def mul(g, q):
                d, b, _ = ssd_idx[q]
                dve.wait_ge(mt_exp, g * NQ + q + 1)
                TT(v3(mt[q % 2], 4), v3(mt[q % 2], 4), cbm[g % 2][:, d, b:b + 1, :].to_broadcast((P, 4, P)), ALU.mult
                   ).then_inc(mt_ready, 1)

            def state(g, k):
                d, kk, b = ssd_states[k]
                n = g * NST + k
                dve.wait_ge(st_t, n + 1)
                if kk == 0:
                    dve.tensor_copy(hst[d], bank[4][:, :]).then_inc(st_done, 1)
                    return
                if kk == 2:
                    dve.wait_ge(yy_t, g * NQ + (2 if d == 0 else 6))
                dve.wait_ge(st_done, n)
                a = d * N_SSM_HEADS + g * HPG
                hv = hst[d].rearrange("p (h q) -> p h q", h=HPG)
                own(TT(hv, hv, cdec[:, b, a:a + HPG].unsqueeze(2).to_broadcast((P, HPG, 64)), ALU.mult))
                TT(hst[d], hst[d], bank[4][:, :], ALU.add).then_inc(st_done, 1)

            def gated(g):
                dve.wait_ge(yy_t, (g + 1) * NQ)
                dve.wait_ge(cv_out, 6 * (g + 1))
                for c in range(4):
                    x = xs[:, g % 2, c, :]
                    STT(x, x, dcol[:, 4 * g + c:4 * g + c + 1], bank[6 + c // 2][:, (c % 2) * SEQ:(c % 2 + 1) * SEQ],
                        ALU.mult, ALU.add).then_inc(gy_v, 1)
                dve.wait_ge(gy_v, 4 * (g + 1))
                dve.wait_ge(pr_copy, 10 * (g + 1))
                dve.wait_ge(zs_done, g + 1)
                z = gy[:, 4 * g:4 * g + 4, :]
                TT(z, z, xs[:, g % 2, :, :], ALU.mult).then_inc(gy_done, 1)

            def scan(g, k):
                if k == 0:
                    seg(g, 0)
                    project(g + 1, k)
                    state(g, 0)
                    state(g, 1)
                    seg(g, 1)
                elif k <= NQ:
                    q = k - 1
                    mul(g, q)
                    project(g + 1, k)
                    if q == 1:
                        state(g, 2)
                    if q + 2 < NQ:
                        seg(g, q + 2)
                    for i in {2: (3, 4), 5: (5,)}.get(q, ()):
                        state(g, i)
                else:
                    project(g + 1, k)
                    gated(g)

            for k in range(SLOTS):
                project(0, k)
                if k == 7:
                    dve.wait_ge(dt_t, 1)
                    dve.tensor_copy(p_, bank[6][:, 0:256]).then_inc(dt_v, 1)
                    dve.wait_ge(dt_v, 3)
                    TT(st1, bank[7][:, 0:256], p_, ALU.subtract).then_inc(dt_v, 1)
                if k == 8:
                    dve.wait_ge(dt_e, 4)
                    TT(eE[:, :, :], eE[:, :, :], dt_[:, :, :], ALU.mult).then_inc(dt_x, 1)
            for g in range(N_GROUPS):
                for k in range(SLOTS):
                    scan(g, k)
            lo_to(2 * S_SSMOUT + 4 + SPL)
            norm_ab(3)
            lo_to(2 * S_SSMOUT + 6 + SPL)
            norm_lo(3)
            for i in range(6, 16):
                lo_to(2 * S_SSMOUT + i + 1 + SPL)
            dve.wait_ge(ld_rw, 16)
            dve.tensor_copy(rwh, rw).then_inc(rw_hi, 1)
            dve.wait_ge(rw_hi, 1)
            TT(rwl, rw, rwh.bitcast(F32), ALU.subtract).then_inc(rw_lo, 1)
            post(8)
            post(9)
            norm_a(12)
            norm_a(13)
            norm_b(12)
            norm_b(13)

            dve.wait_ge(lg_t, 1)
            own(dve.tensor_copy(lg[:, :, :], v3(bank[5][:, 32:48], 2)))
            for b in range(2):
                own(dve.max(top[:, b, :], lg[:, b, :]))
                own(dve.max_index(idx8[:, b, :], top[:, b, :], lg[:, b, :]))
            own(dve.tensor_copy(idxf[:, :, :], idx8[:, :, :]))
            for b in range(2):
                TS(sel1[:, b, :], iota8, idxf[:, b, 0:1], None, ALU.is_equal)
                own(TS(sel2[:, b, :], iota8, idxf[:, b, 1:2], None, ALU.is_equal))
            TT(mask[:, :, :], sel1[:, :, :], sel2[:, :, :], ALU.add).then_inc(rt_v, 1)
            TT(gd, top[:, :, 1], top[:, :, 0], ALU.subtract).then_inc(rt_v, 1)
            dve.wait_ge(rt_e, 1)
            own(TS(gs, ge, 1.0, None, ALU.add))
            own(dve.reciprocal(g1, gs))
            own(TT(g2, ge, g1, ALU.mult))
            for b in range(2):
                own(TS(sel1[:, b, :], sel1[:, b, :], g1[:, b:b + 1], None, ALU.mult))
                own(STT(comb[:, b, :], sel2[:, b, :], g2[:, b:b + 1], sel1[:, b, :], ALU.mult, ALU.add))
            dve.wait_ge(rt_t, 1)
            own(STT(posm[:, :, :], mask[:, :, :], -1000.0, v3(bank[5][:, 0:16], 2), ALU.mult, ALU.add))
            own(TS(posm[:, :, :], posm[:, :, :], 1000.0, None, ALU.add))
            own(TS(posm2[:, :, :], posm[:, :, :], -float(CAP), None, ALU.add))
            own(dve.tensor_reduce(most_f, bank[5][:, 16:24], AX.X, ALU.max))
            dve.tensor_copy(cnt[:, 8:9], most_f)
            dve.tensor_copy(cnt[:, 0:8], bank[5][:, 16:24]).then_inc(rt_done, 1)

            def slots(e, it, pm):
                for b in range(2):
                    i = TS(slot1[:, b, :], iota, pm[:, b, bass.ds(e, 1)], None, ALU.is_equal)
                i.then_inc(slot_ready, 1)

            def gather_split(it):
                dve.wait_ge(gat_mod, it + 1)
                dve.tensor_copy(xh[:, :, 0:P], v3(mt32, KC)).then_inc(gat_hi, 1)
                dve.wait_ge(gat_hi, it + 1)
                TT(xl[:, :, 0:P], v3(mt32, KC), xh[:, :, 0:P].bitcast(F32), ALU.subtract).then_inc(gat_lo, 1)

            def add(it, b):
                for half in range(2):
                    i = 2 * b + half
                    dve.wait_ge(cmb_t, 4 * it + i + 1)
                    dve.wait_ge(cmb_add, 4 * it + i + 1)
                    o = yout[:, b, half * 512:(half + 1) * 512]
                    TT(o, o, bank[2 + half][:, :], ALU.add).then_inc(cmb_add, 1)

            def expert(e, it, before, after):
                def look(i):
                    if i + SPL < MOE_PIECES or after:
                        lo_moe(i + SPL, it)

                def at_step(j):
                    if j in (1, 2) and before:
                        add(it - 1, j - 1)
                    if j == 1:
                        dve.wait_ge(slot_ready, it + 1)
                        for b in range(2):
                            i = TS(slotg[:, b, :], slot1[:, b, :], comb[:, b, bass.ds(e, 1)], None, ALU.mult)
                        i.then_inc(gs_ready, 1)
                    if j == MOE_STEPS // 2 and after:
                        slots(e + 1, it + 1, posm)
                    if j == MOE_STEPS and after:
                        dve.wait_ge(piece_used, P_MOE + it * MOE_PIECES + 2 * pos_moe[("u", MOE_STEPS - 1)] + 2)
                        gather_split(it + 1)

                swiglu(S_MOE, it, 1, MOE_STEPS, pos_moe, C_MOE, T_MOE, msg, mhb, look, at_step)
                dve.wait_ge(piece_used, P_MOE + (it + 1) * MOE_PIECES)
                dve.tensor_copy(yexp[:, 512:1024], bank[1][:, :]).then_inc(y_evac, 1)

            slots(0, 0, posm)
            gather_split(0)
            expert(0, 0, False, True)
            with dve.Fori(1, N_EXPERTS - 1) as e:
                expert(e, e, True, True)
            expert(N_EXPERTS - 1, N_EXPERTS - 1, True, False)
            for b in range(2):
                add(N_EXPERTS - 1, b)
            most = dve.value_load(cnt[0:1, 8:9], min_val=0, max_val=2 * P)
            with dve.If(most > CAP):
                with dve.Fori(0, N_EXPERTS) as e:
                    n = dve.value_load(cnt[0:1, bass.ds(e, 1)], min_val=0, max_val=2 * P)
                    with dve.If(n > CAP):
                        slots(e, e + N_EXPERTS, posm2)
                        for i in range(SPL):
                            lo_moe(i, e + N_EXPERTS)
                        gather_split(e + N_EXPERTS)
                        expert(e, e + N_EXPERTS, False, False)
                        for b in range(2):
                            add(e + N_EXPERTS, b)
                    with dve.Else():
                        it = e + N_EXPERTS
                        for s, before, per in ((lo_ready, P_MOE + it * MOE_PIECES, MOE_PIECES),
                                               (h_done, C_MOE + it * MOE_STEPS, MOE_STEPS),
                                               (ht_lo, T_MOE + it * MOE_STEPS, MOE_STEPS),
                                               (slot_ready, it, 1), (gs_ready, it, 1), (gat_hi, it, 1), (gat_lo, it, 1),
                                               (y_evac, Y_MOE + 2 * it, 1), (cmb_add, 4 * it + 1, 4)):
                            dve.wait_ge(s, before)
                            dve.sem_inc(s, per)
            with dve.Else():
                dve.wait_ge(cmb_add, 4 * N_EXPERTS + 1)
                dve.sem_inc(cmb_add, 4 * N_EXPERTS)
            post(10)
            post(11)


_INS = ["x", "c", "ctx", "c_ctx", "ada_w", "ada_b", "norm_w", "mix_in_w", "q_norm_w", "k_norm_w", "mix_out_w",
        "ffn_gu_w", "ffn_down_w", "ssm_in_w", "ssm_conv_w", "ssm_conv_b", "ssm_dt_bias", "ssm_a_log", "ssm_d",
        "ssm_norm_w", "ssm_out_w", "router_w", "moe_gu_w", "moe_down_w"]


def kernel(**inputs):
    import numpy as _np
    import concourse.bacc as _bacc
    from concourse import mybir as _mybir
    from concourse.bass_utils import run_bass_kernel_spmd as _run

    nc = _bacc.Bacc("TRN2", target_bir_lowering=False, num_devices=1)
    const, first = shape_constants()
    arrays, aps = {}, {}
    for name in _INS + ["const", "first"]:
        a = _np.ascontiguousarray({"const": const, "first": first}[name] if name in ("const", "first") else inputs[name])
        arrays[f"in_{name}_dram"] = a
        aps[name] = nc.dram_tensor(f"in_{name}_dram", a.shape, _mybir.dt.from_np(a.dtype), kind="ExternalInput").ap()
    out = nc.dram_tensor("out_0_dram", (1, SEQ, D_MODEL), F32, kind="ExternalOutput").ap()
    build(nc, aps, out)
    r = _run(nc, [arrays], core_ids=[0])
    return r.results[0]["out_0_dram"]
```
